# Optimizing a Trainium2 kernel written in Bass

```python
import jax, jax.numpy as jnp
from jax import lax
import numpy as np

D_MODEL = 1024
BATCH = 1
SEQ = 2048
DEPTH = 1
DEC_BATCH = 1
DEC_SEQ = 32
PAST_LEN = 1024

CHUNK = 64
PLE_DIM = 256
EPS = 1e-6
N_BRANCH = 3
A_HEAD_DIM = 64
A_HEADS = D_MODEL // 128
A_KV_HEADS = 2
A_WIDTH = A_HEADS * A_HEAD_DIM
A_KV_WIDTH = A_KV_HEADS * A_HEAD_DIM
IDX_HEADS = 4
IDX_DIM = 64
IDX_W_SCALE = (IDX_HEADS * IDX_DIM) ** -0.5
TOPK_MAX = 256
Q_BLOCK = 128
B_WIDTH = D_MODEL // 2
B_GROUPS = 4
B_CHUNK = 128
C_WIDTH = D_MODEL // 2
C_CONV = 31
SPLIT_WIDTHS = (A_WIDTH, A_KV_WIDTH, A_KV_WIDTH, IDX_HEADS * IDX_DIM, IDX_DIM, IDX_HEADS, A_WIDTH,
                2 * B_WIDTH, B_WIDTH, 2 * C_WIDTH, C_WIDTH, N_BRANCH * D_MODEL)
IN_COLS = sum(SPLIT_WIDTHS)

kernel_name = "hybrid_dsa_gmlp_conformer_stream_step"

def rms_norm(x, g):
    xf = x.astype(jnp.float32)
    y = xf * lax.rsqrt(jnp.mean(jnp.square(xf), axis=-1, keepdims=True) + EPS)
    return (y * g.astype(jnp.float32)).astype(x.dtype)

def layer_norm(x, g, b):
    xf = x.astype(jnp.float32)
    xc = xf - jnp.mean(xf, axis=-1, keepdims=True)
    var = jnp.mean(jnp.square(xc), axis=-1, keepdims=True)
    return (xc * lax.rsqrt(var + EPS) * g.astype(jnp.float32) + b.astype(jnp.float32)).astype(x.dtype)

def split_columns(proj):
    cuts, acc = [], 0
    for w in SPLIT_WIDTHS[:-1]:
        acc += w
        cuts.append(acc)
    return jnp.split(proj, cuts, axis=-1)

def alibi_slopes():
    return jnp.asarray(2.0 ** (-8.0 * np.arange(1, A_HEADS + 1) / A_HEADS), dtype=jnp.float32)

def dsa_attend(q, iq, iw, k, v, ik, q_pos, topk):
    bsz, t = q.shape[:2]
    k_pos = jnp.arange(k.shape[1], dtype=jnp.int32)
    visible = (k_pos[None, :] // CHUNK) <= (q_pos[:, None] // CHUNK)
    rel = jax.nn.relu(jnp.einsum('bthd,bsd->bths', iq, ik).astype(jnp.float32))
    score = jnp.einsum('bths,bth->bts', rel, iw.astype(jnp.float32))
    score = jnp.where(visible[None], score, -jnp.inf)
    _, sel = lax.top_k(score, topk)
    valid = (sel // CHUNK) <= (q_pos[None, :, None] // CHUNK)
    kg = jax.vmap(lambda kk, ss: kk[ss])(k, sel)
    vg = jax.vmap(lambda vv, ss: vv[ss])(v, sel)
    qg = q.reshape(bsz, t, A_KV_HEADS, A_HEADS // A_KV_HEADS, A_HEAD_DIM)
    logits = jnp.einsum('btgrd,btkgd->btgrk', qg, kg).astype(jnp.float32) * (A_HEAD_DIM ** -0.5)
    dist = jnp.abs(q_pos[None, :, None] - sel).astype(jnp.float32)
    slopes = alibi_slopes().reshape(A_KV_HEADS, A_HEADS // A_KV_HEADS)
    logits = logits - slopes[None, None, :, :, None] * dist[:, :, None, None, :]
    logits = jnp.where(valid[:, :, None, None, :], logits, -jnp.inf)
    prob = jax.nn.softmax(logits, axis=-1).astype(v.dtype)
    out = jnp.einsum('btgrk,btkgd->btgrd', prob, vg)
    return out.reshape(bsz, t, A_WIDTH)

def dsa_prompt(q, iq, iw, k, v, ik):
    bsz, s = q.shape[:2]
    nb = s // Q_BLOCK
    topk = min(TOPK_MAX, s // 4)

    def blocks(a):
        return jnp.moveaxis(a.reshape((bsz, nb, Q_BLOCK) + a.shape[2:]), 1, 0)

    pos = jnp.arange(s, dtype=jnp.int32).reshape(nb, Q_BLOCK)
    out = lax.map(lambda xs: dsa_attend(xs[0], xs[1], xs[2], k, v, ik, xs[3], topk),
                  (blocks(q), blocks(iq), blocks(iw), pos))
    return jnp.moveaxis(out, 0, 1).reshape(bsz, s, A_WIDTH)

def gmlp_unit(uv, ln_g, ln_b, ws, bs):
    u, v = jnp.split(jax.nn.gelu(uv, approximate=False), 2, axis=-1)
    v = layer_norm(v, ln_g, ln_b)
    bsz, t = v.shape[:2]
    n = min(t, B_CHUNK)
    i = jnp.arange(B_CHUNK)
    mask = (i[None, :] // CHUNK) <= (i[:, None] // CHUNK)
    w = (ws * mask[None].astype(ws.dtype))[:, :n, :n]
    vc = v.reshape(bsz, t // n, n, B_GROUPS, B_WIDTH // B_GROUPS)
    mixed = jnp.einsum('gij,bnjgc->bnigc', w, vc) + bs[:, :n].T[None, None, :, :, None]
    return u * mixed.reshape(bsz, t, B_WIDTH), v

def conv_module(glu_in, left, w, b, ln_g, ln_b):
    a, g = jnp.split(glu_in, 2, axis=-1)
    c = a * jax.nn.sigmoid(g)
    ext = jnp.concatenate([left.astype(c.dtype), c], axis=1)
    y = lax.conv_general_dilated(ext, w[:, None, :], window_strides=(1,), padding='VALID',
                                 dimension_numbers=('NWC', 'WIO', 'NWC'),
                                 feature_group_count=ext.shape[-1]) + b
    y = jax.nn.silu(layer_norm(y, ln_g, ln_b))
    return y, ext[:, -(C_CONV - 1):]

def layer_forward(x, p, past, lw):
    (norm_g, w_in, g_ln_g, g_ln_b, g_ws, g_bs, c_w, c_b, c_ln_g, c_ln_b,
     w_a, w_b, w_c, w_out, ple_g, w_pg, w_ple) = lw
    bsz, t = x.shape[:2]
    (aq, ak, av, iq, ik, iw, za, uv, zb, glu, zc, gates) = split_columns(rms_norm(x, norm_g) @ w_in)
    q = aq.reshape(bsz, t, A_HEADS, A_HEAD_DIM)
    k = ak.reshape(bsz, t, A_KV_HEADS, A_HEAD_DIM)
    v = av.reshape(bsz, t, A_KV_HEADS, A_HEAD_DIM)
    iq = iq.reshape(bsz, t, IDX_HEADS, IDX_DIM)
    iw = iw * IDX_W_SCALE
    if past is None:
        o_a = dsa_prompt(q, iq, iw, k, v, ik)
        left = jnp.zeros((bsz, C_CONV - 1, C_WIDTH), x.dtype)
    else:
        ck, cv, cik, left = past
        past_len = ck.shape[1]
        q_pos = past_len + jnp.arange(t, dtype=jnp.int32)
        o_a = dsa_attend(q, iq, iw,
                         jnp.concatenate([ck.astype(k.dtype), k], axis=1),
                         jnp.concatenate([cv.astype(v.dtype), v], axis=1),
                         jnp.concatenate([cik.astype(ik.dtype), ik], axis=1),
                         q_pos, min(TOPK_MAX, (past_len + t) // 4))
    o_b, v_rows = gmlp_unit(uv, g_ln_g, g_ln_b, g_ws, g_bs)
    o_c, conv_tail = conv_module(glu, left, c_w, c_b, c_ln_g, c_ln_b)
    ga, gb, gc = jnp.split(jax.nn.sigmoid(gates), N_BRANCH, axis=-1)
    merged = (ga * ((o_a * jax.nn.silu(za)) @ w_a)
              + gb * ((o_b * jax.nn.silu(zb)) @ w_b)
              + gc * ((o_c * jax.nn.silu(zc)) @ w_c))
    x = x + merged @ w_out
    x = x + jax.nn.sigmoid(rms_norm(x, ple_g) @ w_pg) * (p @ w_ple)
    return x, k, v, ik, conv_tail, v_rows

def setup_inputs(seed: int = 0) -> dict:
    key = jax.random.key(seed)
    ks = jax.random.split(key, 32)
    f32 = jnp.float32

    def nrm(k, shape, scale):
        return jax.random.normal(k, shape, f32) * scale

    return {
        'x_prompt': nrm(ks[0], (BATCH, SEQ, D_MODEL), 1.0),
        'x_sample': nrm(ks[1], (DEC_BATCH, DEC_SEQ, D_MODEL), 1.0),
        'cache_k': nrm(ks[2], (DEPTH, DEC_BATCH, PAST_LEN, A_KV_HEADS, A_HEAD_DIM), 1.0),
        'cache_v': nrm(ks[3], (DEPTH, DEC_BATCH, PAST_LEN, A_KV_HEADS, A_HEAD_DIM), 1.0),
        'cache_idx_k': nrm(ks[4], (DEPTH, DEC_BATCH, PAST_LEN, IDX_DIM), 1.0),
        'state_conv': nrm(ks[5], (DEPTH, DEC_BATCH, C_CONV - 1, C_WIDTH), 0.5),
        'p_prompt': nrm(ks[6], (DEPTH, BATCH, SEQ, PLE_DIM), 1.0),
        'p_sample': nrm(ks[7], (DEPTH, DEC_BATCH, DEC_SEQ, PLE_DIM), 1.0),
        'norm_g': 1.0 + nrm(ks[8], (DEPTH, D_MODEL), 0.05),
        'w_in': nrm(ks[9], (DEPTH, D_MODEL, IN_COLS), D_MODEL ** -0.5),
        'gmlp_ln_g': 1.0 + nrm(ks[10], (DEPTH, B_WIDTH), 0.05),
        'gmlp_ln_b': nrm(ks[11], (DEPTH, B_WIDTH), 0.02),
        'gmlp_ws': nrm(ks[12], (DEPTH, B_GROUPS, B_CHUNK, B_CHUNK), B_CHUNK ** -0.5),
        'gmlp_bs': 1.0 + nrm(ks[13], (DEPTH, B_GROUPS, B_CHUNK), 0.05),
        'conv_w': nrm(ks[14], (DEPTH, C_CONV, C_WIDTH), C_CONV ** -0.5),
        'conv_b': nrm(ks[15], (DEPTH, C_WIDTH), 0.02),
        'conv_ln_g': 1.0 + nrm(ks[16], (DEPTH, C_WIDTH), 0.05),
        'conv_ln_b': nrm(ks[17], (DEPTH, C_WIDTH), 0.02),
        'w_branch_a': nrm(ks[18], (DEPTH, A_WIDTH, D_MODEL), A_WIDTH ** -0.5),
        'w_branch_b': nrm(ks[19], (DEPTH, B_WIDTH, D_MODEL), B_WIDTH ** -0.5),
        'w_branch_c': nrm(ks[20], (DEPTH, C_WIDTH, D_MODEL), C_WIDTH ** -0.5),
        'w_out': nrm(ks[21], (DEPTH, D_MODEL, D_MODEL), D_MODEL ** -0.5),
        'ple_norm_g': 1.0 + nrm(ks[22], (DEPTH, D_MODEL), 0.05),
        'w_ple_gate': nrm(ks[23], (DEPTH, D_MODEL, D_MODEL), D_MODEL ** -0.5),
        'w_ple': nrm(ks[24], (DEPTH, PLE_DIM, D_MODEL), PLE_DIM ** -0.5),
        'final_norm_g': 1.0 + nrm(ks[25], (D_MODEL,), 0.05),
    }

def reference(x_prompt, x_sample, cache_k, cache_v, cache_idx_k, state_conv, p_prompt, p_sample,
              norm_g, w_in, gmlp_ln_g, gmlp_ln_b, gmlp_ws, gmlp_bs, conv_w, conv_b, conv_ln_g, conv_ln_b,
              w_branch_a, w_branch_b, w_branch_c, w_out, ple_norm_g, w_ple_gate, w_ple, final_norm_g):
    xp, xs = x_prompt, x_sample
    kp, vp, ikp, cvp = [], [], [], []
    ks_, vs_, iks, cvs, gvs = [], [], [], [], []
    for l in range(DEPTH):
        lw = (norm_g[l], w_in[l], gmlp_ln_g[l], gmlp_ln_b[l], gmlp_ws[l], gmlp_bs[l],
              conv_w[l], conv_b[l], conv_ln_g[l], conv_ln_b[l],
              w_branch_a[l], w_branch_b[l], w_branch_c[l], w_out[l],
              ple_norm_g[l], w_ple_gate[l], w_ple[l])
        xp, k1, v1, ik1, c1, _ = layer_forward(xp, p_prompt[l], None, lw)
        kp.append(k1); vp.append(v1); ikp.append(ik1); cvp.append(c1)
        past = (cache_k[l], cache_v[l], cache_idx_k[l], state_conv[l])
        xs, k2, v2, ik2, c2, g2 = layer_forward(xs, p_sample[l], past, lw)
        ks_.append(k2); vs_.append(v2); iks.append(ik2); cvs.append(c2); gvs.append(g2)
    y_prompt = rms_norm(xp, final_norm_g)
    y_sample = rms_norm(xs, final_norm_g)
    return (y_prompt, y_sample,
            jnp.stack(kp), jnp.stack(vp), jnp.stack(ikp), jnp.stack(cvp),
            jnp.stack(ks_), jnp.stack(vs_), jnp.stack(iks), jnp.stack(cvs), jnp.stack(gvs))


_drawn_inputs = setup_inputs


def setup_inputs(seed=0):
    import zlib

    import numpy as np

    out = dict(_drawn_inputs(seed))
    spreads = {}
    factors = {'gmlp_ln_b': 2.758,
     'gmlp_bs': 6.35,
     'conv_b': 8.0,
     'conv_ln_g': 5.398,
     'conv_ln_b': 26.67,
     'ple_norm_g': 23.915,
     'cache_k': 3.47}
    for name, (base, spread) in spreads.items():
        noise = np.random.default_rng([zlib.crc32(name.encode()), seed]).standard_normal(out[name].shape)
        drawn = base * np.exp(spread * noise) if base else spread * noise
        out[name] = __import__('jax').numpy.asarray(drawn.astype(out[name].dtype))
    for name, factor in factors.items():
        out[name] = (out[name] * factor).astype(out[name].dtype)
    return out
```

```python
from contextlib import ExitStack, contextmanager

import numpy as np

import concourse.bass as bass
import concourse.mybir as mybir
from concourse.alu_op_type import AluOpType as ALU

F32 = mybir.dt.float32
F32R = mybir.dt.float32r
BF16 = mybir.dt.bfloat16
I32 = mybir.dt.int32
I16 = mybir.dt.int16
U16 = mybir.dt.uint16
U8 = mybir.dt.uint8
ACT = mybir.ActivationFunctionType
AX = mybir.AxisListType

P = 128
D = 1024
KD = D // P
SEQ, DEC, PAST = 2048, 32, 1024
TILES = SEQ // P + 1
DT = TILES - 1
TOK = TILES * P
EPS = 1e-6
HD = 64
HEADS, KVH, IH = 8, 2, 4
AW = HEADS * HD
BW = CW = 512
CONV = 31
CHUNK = 64
TOPK = 256
IN_COLS = 7748
IDX_W_SCALE = (IH * HD) ** -0.5
C_Q, C_K, C_V, C_IQ, C_IK, C_IW, C_ZA, C_U, C_GV, C_ZB, C_GA, C_GG, C_ZC, C_G = (
    0, 512, 640, 768, 1024, 1088, 1092, 1604, 2116, 2628, 3140, 3652, 4164, 4676)
SPANS = [(0, 512), (512, 512), (1024, 512), (1536, 512), (2048, 128)]


class Shared:
    pass


class Programs:

    def __init__(self, sync=None, gpsimd=None, scalar=None, vector=None, tensor=None, ready=None):
        self.sync, self.gpsimd, self.scalar, self.vector, self.tensor = sync, gpsimd, scalar, vector, tensor
        self.ready = ready


class Steps:

    def __init__(self, eng, sem):
        self.eng, self.sem, self.base, self.n = eng, sem, 0, 0

    def did(self, ins):
        ins.then_inc(self.sem, 1)
        self.n += 1

    def wait(self):
        self.eng.wait_ge(self.sem, self.base + self.n)

    def did_wait(self, ins):
        self.did(ins)
        self.wait()

    @contextmanager
    def turns(self, count, per):
        start = self.base + self.n
        with self.eng.Fori(0, count) as i:
            self.base, self.n = i * per + start, 0
            yield i
            assert self.n == per, (self.n, per)
        self.base, self.n = start + count * per, 0


RSQRT_STEPS = 11


def rsqrt(steps, y, v, t):
    vec = steps.eng
    yi, ti = y.bitcast(I32), t.bitcast(I32)
    steps.did_wait(vec.tensor_scalar(ti, v.bitcast(I32), 1, None, ALU.logical_shift_right))
    steps.did_wait(vec.tensor_scalar(yi, ti, -1.0, 1597463007.0, ALU.mult, ALU.add))
    for _ in range(3):
        steps.did_wait(vec.scalar_tensor_tensor(out=t, in0=y, scalar=v, in1=y, op0=ALU.mult, op1=ALU.mult))
        steps.did_wait(vec.tensor_scalar(t, t, -0.5, 1.5, ALU.mult, ALU.add))
        steps.did_wait(vec.tensor_tensor(y, y, t, ALU.mult))


class Sbuf:

    def __init__(self, nc, at):
        self.nc, self.at = nc, at

    def __call__(self, name, shape, dt=F32):
        size = {F32: 4, F32R: 4, I32: 4, BF16: 2, I16: 2, U16: 2, U8: 1}[dt]
        n = int(np.prod(shape[1:])) * size
        n = (n + 31) // 32 * 32
        t = self.nc.alloc_sbuf_tensor_at(name, shape, dt, offset=self.at)
        self.at += n
        assert self.at <= self.nc.sbuf_usable_end, (name, self.at)
        return t


def f32(ap):
    return ap.bitcast(F32)


def at(t, n=P):
    return slice(t * n, (t + 1) * n) if isinstance(t, int) else bass.ds(t * n, n)



def stage_norm(c):
    nc, sb = c.nc, Sbuf(c.nc, c.after_hT)
    x_in = [sb(f"n_x{p}", [P, D]) for p in range(2)]
    xn = [sb(f"n_xn{p}", [P, D]) for p in range(2)]
    junk = [sb(f"n_junk{p}", [P, D]) for p in range(2)]
    g_rows = sb("n_g", [P, D])
    ssq = [sb(f"n_ssq{p}", [P, 1]) for p in range(2)]
    var = sb("n_var", [P, 1])
    rstd = sb("n_rstd", [P, 1])
    tmp = sb("n_tmp", [P, 1])
    S = c.sem
    own_steps = S("n_steps")
    g_full = S("n_g_full")
    x_full = [S(f"n_x_full{p}") for p in range(2)]
    squared = [S(f"n_squared{p}") for p in range(2)]
    normed = [S(f"n_normed{p}") for p in range(2)]
    turned = [S(f"n_turned{p}") for p in range(2)]
    hi_done = [S(f"n_hi{p}") for p in range(2)]
    lo_done = [S(f"n_lo{p}") for p in range(2)]
    half = DT // 2
    pT = [c.psum[:, 2 * p:2 * p + 2, :].rearrange("q b (k t) -> q (b k) t", k=4) for p in range(2)]

    def cols(i, p):
        return bass.ds((i * 2 + p) * P, P) if not isinstance(i, int) else slice((2 * i + p) * P, (2 * i + p + 1) * P)

    def sync(sp):
        sp.dma_start(g_rows[:], c.I["norm_g"].partition_broadcast(P)).then_inc(g_full, 16)

        def load(i, p, last=False):
            sp.wait_ge(squared[p], i)
            sp.wait_ge(normed[p], i)
            if last:
                sp.dma_start(x_in[p][0:DEC, :], c.I["x_sample"]).then_inc(x_full[p], 16)
            else:
                sp.dma_start(x_in[p][:], c.I["x_prompt"][cols(i, p), :]).then_inc(x_full[p], 16)

        with sp.Fori(0, half) as i:
            load(i, 0)
            load(i, 1)
        load(half, 0, last=True)

    def scalar(act):
        def square(i, p):
            act.wait_ge(x_full[p], i * 16 + 16)
            act.wait_ge(normed[p], i)
            act.wait_ge(squared[p], i)
            act.activation(junk[p][:], x_in[p][:], ACT.Square, accum_out=ssq[p][:]).then_inc(squared[p], 1)

        def high(i, p):
            act.wait_ge(turned[p], i + 1)
            act.copy(c.hT_hi[:, :, cols(i, p)], pT[p]).then_inc(hi_done[p], 1)

        square(0, 0)
        with act.Fori(0, half) as i:
            square(i, 1)
            high(i, 0)
            square(i + 1, 0)
            high(i, 1)
        high(half, 0)

    def vector(vec):
        steps = Steps(vec, own_steps)

        def norm(i, p):
            vec.wait_ge(squared[p], i + 1)
            vec.wait_ge(turned[p], i)
            steps.did_wait(vec.tensor_scalar(var[:], ssq[p][:], 1.0 / D, EPS, ALU.mult, ALU.add))
            rsqrt(steps, rstd[:], var[:], tmp[:])
            vec.scalar_tensor_tensor(out=xn[p][:], in0=x_in[p][:], scalar=rstd[:], in1=g_rows[:],
                                     op0=ALU.mult, op1=ALU.mult).then_inc(normed[p], 1)

        def low(i, p):
            vec.wait_ge(turned[p], i + 1)
            vec.wait_ge(hi_done[p], i + 1)
            vec.tensor_tensor(c.hT_lo[:, :, cols(i, p)], pT[p], f32(c.hT_hi[:, :, cols(i, p)]),
                              ALU.subtract).then_inc(lo_done[p], 1)

        per = 1 + RSQRT_STEPS
        vec.wait_ge(g_full, 16)
        norm(0, 0)
        with steps.turns(half, 2 * per) as i:
            norm(i, 1)
            low(i, 0)
            norm(i + 1, 0)
            low(i, 1)
        low(half, 0)

    def tensor(pe):
        def turn(i, p):
            pe.wait_ge(normed[p], i + 1)
            pe.wait_ge(hi_done[p], i)
            pe.wait_ge(lo_done[p], i)
            for k in range(KD):
                last = pe.transpose(pT[p][:, k, :], xn[p][:, k * P:(k + 1) * P], c.ident[:])
            last.then_inc(turned[p], 1)

        pe.wait_ge(c.ident_ready, 1)
        with pe.Fori(0, half) as i:
            turn(i, 0)
            turn(i, 1)
        turn(half, 0)

    c.hT_done = (hi_done[0], half + 1), (hi_done[1], half), (lo_done[0], half + 1), (lo_done[1], half)
    return Programs(sync=sync, scalar=scalar, vector=vector, tensor=tensor)


S_IKW, S_Q, S_K, S_V, S_IQ, S_GA, S_U, S_GV, S_ZA, S_ZB, S_ZC, S_GG, S_G = (
    0, 1, 5, 6, 7, 9, 13, 17, 21, 25, 29, 33, 37)
RUNS = [(C_IK, 1, S_IKW, "copy"), (C_Q, 8, S_Q, "copy"), (C_GA, 4, S_GA, "copy"), (C_U, 8, S_U, "gelu"),
        (C_ZA, 4, S_ZA, "silu"), (C_ZB, 4, S_ZB, "silu"), (C_ZC, 4, S_ZC, "silu"),
        (C_GG, 4, S_GG, "sigmoid"), (C_G, 24, S_G, "sigmoid")]
SLOTS = sum(r[1] for r in RUNS)
FUNC = {"copy": ACT.Copy, "gelu": ACT.Gelu, "silu": ACT.Silu, "sigmoid": ACT.Sigmoid}


FIRST_JOBS = RUNS[0][1] + RUNS[1][1]


def project(c, first):
    nc = c.nc
    if first:
        sb = Sbuf(nc, c.after_hT)
        c.w_raw = [sb(f"j_w{p}", [P, KD, P]) for p in range(2)]
        c.w_hi = [sb(f"j_whi{p}", [P, KD, P], F32R) for p in range(2)]
        c.w_lo = [sb(f"j_wlo{p}", [P, KD, P], F32R) for p in range(2)]
        c.out = sb("j_out", [P, TOK])
        c.after_project = sb.at
        S = c.sem
        c.w_hi_done = [S(f"j_hi{p}") for p in range(2)]
        c.w_lo_done = [S(f"j_lo{p}") for p in range(2)]
        c.bank_full = S("j_bank_full")
        c.bank_read = S("j_bank_read")
        c.stored = [S(f"j_stored{b}") for b in range(5)]
    w_raw, w_hi, w_lo, out = c.w_raw, c.w_hi, c.w_lo, c.out
    w_full, hi_done, lo_done, bank_full, bank_read, stored = (
        c.w_full, c.w_hi_done, c.w_lo_done, c.bank_full, c.bank_read, c.stored)
    w_in = c.I["w_in"].rearrange("(k q) n -> q k n", q=P)

    def jobs(eng, body):
        j = 0
        for n_run, (col, n, slot, func) in enumerate(RUNS):
            if (n_run < 2) == first:
                if n == 1:
                    body(j, j // 2, j % 2, col, slot, func)
                else:
                    with eng.Fori(0, n // 2) as i:
                        for o in range(2):
                            body(i * 2 + (j + o), i + (j + o) // 2, (j + o) % 2,
                                 i * (2 * P) + (col + o * P), i * 2 + (slot + o), func)
            j += n

    def gpsimd(pool):
        for s, n in c.hT_done if first else c.scores_stored:
            pool.wait_ge(s, n)

        zeros = c.zero[:].unsqueeze(1).to_broadcast([P, KD, P])

        def weights(j, m, p, col, slot, func):
            pool.wait_ge(lo_done[p], m)
            col = bass.ds(col, P) if not isinstance(col, int) else slice(col, col + P)
            pool.dma_start(w_raw[p][:], w_in[:, :, col]).then_inc(w_full[p], 16)
            pool.wait_ge(w_full[p], m * 16 + 16)
            if not isinstance(j, int):
                pool.wait_ge(bank_full, j * 5 - 5)
            pool.tensor_tensor(w_hi[p][:], w_raw[p][:], zeros, ALU.add).then_inc(hi_done[p], 1)
            pool.wait_ge(hi_done[p], m + 1)
            pool.tensor_tensor(w_lo[p][:], w_raw[p][:], f32(w_hi[p][:]), ALU.subtract).then_inc(lo_done[p], 1)
        jobs(pool, weights)

    def tensor(pe):
        for s, n in c.hT_done:
            pe.wait_ge(s, n)
        if not first:
            for s, n in c.scores_stored:
                pe.wait_ge(s, n)

        def job(j, m, p, col, slot, func):
            pe.wait_ge(lo_done[p], m + 1)
            for b, (t0, n) in enumerate(SPANS):
                if not isinstance(j, int):
                    pe.wait_ge(bank_read, j * 5 + (b - 4))
                bank = c.psum[:, b, 0:n]
                for k in range(KD):
                    for q, (w, h) in enumerate(((w_hi, c.hT_hi), (w_hi, c.hT_lo), (w_lo, c.hT_hi))):
                        last = pe.matmul(bank, w[p][:, k, :], h[:, k, t0:t0 + n],
                                         start=(k == 0 and q == 0), stop=(k == KD - 1 and q == 2))
                last.then_inc(bank_full, 1)
        jobs(pe, job)

    def scalar(act):
        def evacuate(j, m, p, col, slot, func):
            for b, (t0, n) in enumerate(SPANS):
                act.wait_ge(bank_full, j * 5 + (b + 1))
                act.wait_ge(stored[b], j * 16)
                act.activation(out[:, t0:t0 + n], c.psum[:, b, 0:n], FUNC[func]).then_inc(bank_read, 1)
                act.wait_ge(bank_read, j * 5 + (b + 1))
                act.dma_start(c.T_dram[at(slot, 1), :, t0:t0 + n].rearrange("a q t -> q (a t)"),
                              out[:, t0:t0 + n]).then_inc(stored[b], 16)
        jobs(act, evacuate)

    done = [(s, 16 * (FIRST_JOBS if first else SLOTS)) for s in stored]
    if first:
        c.first_stored = done
    else:
        c.T_stored = done
    return Programs(scalar=scalar, tensor=tensor, gpsimd=gpsimd)


def stage_project_first(c):
    return project(c, True)


def stage_project_rest(c):
    return project(c, False)


CLASSES = [(4 * j, 512 * (j + 1)) for j in range(4)] + [(DT, PAST + DEC)]


def pieces(keys):
    return [(a, min(512, keys - a)) for a in range(0, keys, 512)]


def query_tiles(loop, body):
    for j, (t0, keys) in enumerate(CLASSES):
        if t0 == DT:
            body(j, DT, DT // 2, 0)
            continue
        with loop(j) as i:
            for p in range(2):
                body(j, i * 2 + (t0 + p), i + t0 // 2, p)


def doubled(eng, dst, src, sem):
    eng.dma_start(dst[0:HD], src).then_inc(sem, 16)
    eng.dma_start(dst[HD:P], src).then_inc(sem, 16)


def stage_natural(c):
    nc, sb = c.nc, Sbuf(c.nc, c.after_hT)
    kvT = [sb(f"t_kvT{p}", [P, 3, P]) for p in range(2)]
    nat = [sb(f"t_nat{p}", [P, 3, P]) for p in range(2)]
    iw = sb("t_iw", [P, TILES, IH])
    S = c.sem
    own_steps = S("t_steps")
    full = [S(f"t_full{p}") for p in range(2)]
    turned = [S(f"t_turned{p}") for p in range(2)]
    copied = [S(f"t_copied{p}") for p in range(2)]
    iw_read = [S(f"t_iw_read{p}") for p in range(2)]
    stored = c.natural_stored
    half = DT // 2

    def tiles(eng, body):
        with eng.Fori(0, half) as i:
            body(i * 2, i, 0)
            body(i * 2 + 1, i, 1)
        body(DT, half, 0)

    def sync(sp):
        for s, n in c.first_stored:
            sp.wait_ge(s, n)

        def load(t, m, p):
            sp.wait_ge(turned[p], m)
            sp.dma_start(kvT[p][:, 0:2, :], c.T_dram[S_K:S_K + 2, :, at(t)].rearrange("s q t -> q s t")).then_inc(full[p], 16)
            sp.dma_start(kvT[p][:, 2, :], c.T_dram[S_IKW, :, at(t)]).then_inc(full[p], 16)
        tiles(sp, load)

    def tensor(pe):
        pe.wait_ge(c.bank_read, 5 * FIRST_JOBS)

        def turn(t, m, p):
            pe.wait_ge(full[p], m * 32 + 32)
            pe.wait_ge(copied[p], m)
            for s in range(3):
                last = pe.transpose(c.psum[:, p, s * P:(s + 1) * P], kvT[p][:, s, :], c.ident[:])
            last.then_inc(turned[p], 1)
        tiles(pe, turn)

    def vector(vec):
        steps = Steps(vec, own_steps)

        def copy(t, m, p):
            vec.wait_ge(turned[p], m + 1)
            vec.wait_ge(stored[p], m * 48)
            vec.wait_ge(iw_read[p], m)
            vec.tensor_copy(nat[p][:], c.psum[:, p, 0:3 * P].rearrange("q (s n) -> q s n", s=3)).then_inc(copied[p], 1)
            vec.wait_ge(copied[p], m + 1)
            vec.tensor_copy(iw[:, bass.ds(t, 1) if not isinstance(t, int) else slice(t, t + 1), :],
                            nat[p][:, 2:3, HD:HD + IH]).then_inc(iw_read[p], 1)
        tiles(vec, copy)
        for p in range(2):
            vec.wait_ge(iw_read[p], half + 1 - p)
        steps.did_wait(vec.tensor_scalar(c.sg[:], iw[:], 0.0, 2.0, ALU.is_ge, ALU.mult))
        steps.did_wait(vec.tensor_scalar(c.sg[:], c.sg[:], -1.0, None, ALU.add))
        steps.did_wait(vec.tensor_scalar(iw[:], iw[:], IDX_W_SCALE, 0.0, ALU.mult, ALU.add))
        vec.tensor_tensor(c.aw[:], iw[:], c.sg[:], ALU.mult).then_inc(c.weights_ready, 1)

    def gpsimd(pool):
        def store(t, m, p):
            pool.wait_ge(copied[p], m + 1)
            for s, n, name in ((0, P, "k"), (1, P, "v"), (2, HD, "ik")):
                if isinstance(t, int):
                    dst, rows = c.O[name + "_sample"], DEC
                else:
                    dst, rows = c.O[name + "_prompt"].rearrange("(t h) d -> t (h d)", t=SEQ)[at(t), :], P
                if isinstance(t, int):
                    dst = dst.rearrange("(t h) d -> t (h d)", t=DEC)
                pool.dma_start(dst, nat[p][0:rows, s, 0:n]).then_inc(stored[p], 16)
        tiles(pool, store)
        for p in range(2):
            pool.wait_ge(stored[p], 48 * (half + 1 - p))

    c.natural_freed = (stored[0], 48 * (half + 1)), (stored[1], 48 * half), (c.weights_ready, 1)
    return Programs(sync=sync, vector=vector, tensor=tensor, gpsimd=gpsimd)


def stage_scores(c):
    nc, sb = c.nc, Sbuf(c.nc, c.after_hT)
    NS = PAST + DEC
    ik_hi = sb("i_ikhi", [P, SEQ], F32R)
    ik_lo = sb("i_iklo", [P, SEQ], F32R)
    iks_hi = sb("i_ikshi", [P, NS], F32R)
    iks_lo = sb("i_ikslo", [P, NS], F32R)
    acc = [sb(f"i_acc{p}", [P, SEQ]) for p in range(2)]
    iq2 = [sb(f"i_iq{p}", [P, IH, P]) for p in range(2)]
    iqs = [sb(f"i_iqs{p}", [P, IH, P], F32R) for p in range(2)]
    R = [sb(f"i_r{r}", [P, 512]) for r in range(4)]
    aw = [sb(f"i_aw{p}", [P, IH]) for p in range(2)]
    S = c.sem
    own_steps = S("i_steps")
    raw_full = S("i_raw_full")
    raws_full = S("i_raws_full")
    cache_full = S("i_cache_full")
    cache_turned = S("i_cache_turned")
    ik_ready = S("i_ik_ready")
    iq_full = [S(f"i_iq_full{p}") for p in range(2)]
    iqs_ready = [S(f"i_iqs_ready{p}") for p in range(2)]
    product = S("i_product")
    bank_read = [S(f"i_bank_read{b}") for b in range(8)]
    r_used = [S(f"i_r_used{r}") for r in range(4)]
    acc_ready = [S(f"i_acc_ready{p}") for p in range(2)]
    stored = c.acc_stored
    cache = acc[1][:, 0:SEQ // 2].rearrange("q (t u d) -> q t u d", t=8, u=2)
    cacheT = c.psum[:, 0:2, :].rearrange("q b n -> q (b n)")
    new_ik = acc[1][:, SEQ // 2:SEQ // 2 + DEC]

    per_tile = [IH * len(pieces(keys)) for _, keys in CLASSES]
    before = [4 * sum(per_tile[:j]) for j in range(len(CLASSES))]

    def units(j, m, p):
        t0, keys = CLASSES[j]
        i = m - t0 // 2 if not isinstance(m, int) else 0
        for n, (h, (a, w)) in enumerate((h, s) for h in range(IH) for s in pieces(keys)):
            u = p * per_tile[j] + n
            start = before[j] + u
            turn = 2 * per_tile[j]
            back = start - len(pieces(keys))
            yield (h, a, w, u % 8, i * (turn // 8) + start // 8, u % 4, i * (turn // 4) + start // 4,
                   i * turn + start, back % 4, i * (turn // 4) + back // 4 + 1)

    def fori(eng):
        return lambda j: eng.Fori(0, 2)

    def sync(sp):
        for s, n in c.natural_freed:
            sp.wait_ge(s, n)
        doubled(sp, acc[0], c.T_dram[S_IKW, 0:HD, 0:SEQ], raw_full)
        doubled(sp, new_ik, c.T_dram[S_IKW, 0:HD, SEQ:SEQ + DEC], raws_full)
        for u in range(2):
            sp.dma_start(cache[:, :, u, :], c.I["cache_idx_k"].rearrange("(t q) d -> q t d", q=P)).then_inc(cache_full, 16)

        def load(j, t, m, p):
            sp.wait_ge(iqs_ready[p], m)
            rows = c.T_dram[S_IQ:S_IQ + 2].rearrange("s q t -> (s q) t").rearrange("(h d) t -> d h t", d=HD)
            doubled(sp, iq2[p], rows[:, :, at(t)], iq_full[p])
        query_tiles(fori(sp), load)

    def tensor(pe):
        pe.wait_ge(cache_full, 32)
        for s, n in c.natural_freed:
            pe.wait_ge(s, n)
        for t in range(8):
            last = pe.transpose(cacheT[:, t * P:(t + 1) * P], cache[:, t].rearrange("q u d -> q (u d)"), c.ident[:])
        last.then_inc(cache_turned, 1)
        pe.wait_ge(ik_ready, 1)

        def score(j, t, m, p):
            hi, lo = (iks_hi, iks_lo) if t is DT else (ik_hi, ik_lo)
            pe.wait_ge(iqs_ready[p], m + 1)
            for h, a, w, b, nb, *_ in units(j, m, p):
                pe.wait_ge(bank_read[b], nb)
                pe.matmul(c.psum[:, b, 0:w], iqs[p][:, h, :], hi[:, a:a + w], start=True, stop=False)
                pe.matmul(c.psum[:, b, 0:w], iqs[p][:, h, :], lo[:, a:a + w], start=False, stop=True).then_inc(product, 1)
        query_tiles(fori(pe), score)

    def scalar(act):
        act.wait_ge(c.weights_ready, 1)

        def relu(j, t, m, p):
            for h, a, w, b, _, r, nr, n, *_ in units(j, m, p):
                act.wait_ge(product, n + 1)
                act.wait_ge(r_used[r], nr)
                act.activation(R[r][:, 0:w], c.psum[:, b, 0:w], ACT.Relu,
                               scale=aw[p][:, h:h + 1]).then_inc(bank_read[b], 1)
        query_tiles(fori(act), relu)

    def vector(vec):
        steps = Steps(vec, own_steps)
        vec.wait_ge(raw_full, 32)
        steps.did_wait(vec.tensor_copy(ik_hi[:], acc[0][:]))
        steps.did_wait(vec.tensor_tensor(ik_lo[:], acc[0][:], f32(ik_hi[:]), ALU.subtract))
        vec.wait_ge(raws_full, 32)
        vec.wait_ge(cache_turned, 1)
        for dst, src in ((slice(0, PAST), cacheT), (slice(PAST, NS), new_ik)):
            steps.did_wait(vec.tensor_copy(iks_hi[:, dst], src))
            steps.did_wait(vec.tensor_tensor(iks_lo[:, dst], src, f32(iks_hi[:, dst]), ALU.subtract))
        vec.sem_inc(ik_ready, 1)

        def split(t, m, p):
            vec.wait_ge(iq_full[p], m * 32 + 32)
            steps.did(vec.tensor_scalar(aw[p][:], c.aw[:, at(t, 1), :], 1.0, None, ALU.mult))
            steps.did_wait(vec.tensor_copy(iqs[p][:], iq2[p][:]))
            vec.tensor_tensor(iqs[p][HD:P], iq2[p][HD:P], f32(iqs[p][HD:P]), ALU.subtract).then_inc(iqs_ready[p], 1)

        def add(j, t, m, p):
            if t is not DT:
                split(t + 1, m + p, 1 - p)
            vec.wait_ge(stored[p], m * 16)
            for h, a, w, b, nb, r, nr, n, r_before, n_before in units(j, m, p):
                vec.wait_ge(bank_read[b], nb + 1)
                sg = c.sg[:, at(t, 1), h]
                if h == 0:
                    ins = vec.tensor_scalar(acc[p][:, a:a + w], R[r][:, 0:w], sg, 0.0, ALU.mult, ALU.add)
                else:
                    vec.wait_ge(r_used[r_before], n_before)
                    ins = vec.scalar_tensor_tensor(out=acc[p][:, a:a + w], in0=R[r][:, 0:w], scalar=sg,
                                                   in1=acc[p][:, a:a + w], op0=ALU.mult, op1=ALU.add)
                ins.then_inc(r_used[r], 1)
            vec.wait_ge(r_used[r], nr + 1)
            vec.sem_inc(acc_ready[p], 1)
        split(0, 0, 0)
        query_tiles(lambda j: steps.turns(2, 4), add)

    def gpsimd(pool):
        def store(j, t, m, p):
            pool.wait_ge(acc_ready[p], m + 1)
            keys = CLASSES[j][1]
            dst = c.SC_dram[at(t, 1), :, 0:keys].rearrange("a q n -> q (a n)")
            pool.dma_start(dst, acc[p][:, 0:keys]).then_inc(stored[p], 16)
        query_tiles(fori(pool), store)

    c.scores_stored = (stored[0], 16 * (DT // 2 + 1)), (stored[1], 16 * (DT // 2))
    return Programs(sync=sync, scalar=scalar, vector=vector, tensor=tensor, gpsimd=gpsimd)


def stage_constants(c):
    nc, sb = c.nc, Sbuf(c.nc, c.after_hT)
    sb.at += 4 * 14 * 1024
    pos = sb("c_pos", [P, TILES], I32)
    chunk = sb("c_chunk", [P, TILES], I32)
    made, step = c.sem("c_made"), c.sem("c_step")

    def gpsimd(pool):
        pool.iota(pos[:, 0:DT], pattern=[[P, DT]], base=0, channel_multiplier=1).then_inc(made, 1)
        pool.iota(pos[:, DT:TILES], pattern=[[0, 1]], base=PAST, channel_multiplier=1).then_inc(made, 1)

    def vector(vec):
        steps = Steps(vec, step)
        vec.wait_ge(made, 2)
        steps.did_wait(vec.tensor_copy(c.qpos[:], pos[:]))
        steps.did_wait(vec.tensor_scalar(chunk[:], pos[:], 6, None, ALU.arith_shift_right))
        steps.did_wait(vec.tensor_scalar(c.lim[:], chunk[:], 1.0, float(CHUNK), ALU.add, ALU.mult))

    return Programs(gpsimd=gpsimd, vector=vector)


MASKED = 1e30
SELECT_STEPS = 2 * 49 + 23


def stage_select(c):
    nc, sb = c.nc, Sbuf(c.nc, c.after_project)
    key = [sb(f"s_key{p}", [P, SEQ], I32) for p in range(2)]
    mask = sb("s_mask", [P, SEQ], I32)
    junk = sb("s_junk", [P, SEQ], BF16)
    order = sb("s_order", [P, SEQ], I16)
    iota = sb("s_iota", [P, SEQ], I16)
    cnt, g, cand, th, need, u, th1 = (sb(f"s_{n}", [P, 1]) for n in ("cnt", "g", "cand", "th", "need", "u", "th1"))
    H = mask[:, 0:SEQ // 2].bitcast(U16)
    eq = mask[:, SEQ // 2:].bitcast(BF16)
    S = c.sem
    own_steps = S("s_steps")
    full = [S(f"s_full{p}") for p in range(2)]
    done = [S(f"s_done{p}") for p in range(2)]
    stored = [S(f"s_stored{p}") for p in range(2)]
    iota_made = S("s_iota_made")

    def sync(sp):
        for s, n in c.scores_stored:
            sp.wait_ge(s, n)

        def rows(dram, t):
            keys = CLASSES[t // 4][1]
            return dram[t, :, 0:keys], key[t % 2][:, 0:keys]

        for t in range(TILES + 1):
            p = t % 2
            if t < TILES:
                dram, sbuf = rows(c.SC_dram, t)
                sp.wait_ge(stored[p], t // 2 * 16)
                sp.dma_start(sbuf, dram.bitcast(I32)).then_inc(full[p], 16)
            if t > 0:
                dram, sbuf = rows(c.ND_dram, t - 1)
                sp.wait_ge(done[1 - p], (t - 1) // 2 + 1)
                sp.dma_start(dram, f32(sbuf)).then_inc(stored[1 - p], 16)
        for p in range(2):
            sp.wait_ge(stored[p], 16 * (DT // 2 + 1 - p))

    def gpsimd(pool):
        for s, n in c.scores_stored:
            pool.wait_ge(s, n)
        pool.iota(iota[:], pattern=[[1, SEQ]], base=0, channel_multiplier=0).then_inc(iota_made, 1)

    def vector(vec):
        steps = Steps(vec, own_steps)
        do = steps.did_wait

        def search(src, first, k):
            do(vec.tensor_scalar(cand[:], c.zero[:], float(first + 2 ** 15), None, ALU.add))
            for b in reversed(range(16)):
                do(vec.tensor_scalar(junk[:, 0:src.shape[1]], src, cand[:], 0.0, ALU.is_ge, ALU.add, accum_out=cnt[:]))
                do(vec.tensor_scalar(g[:], cnt[:], k, float(2 ** b), ALU.is_ge, ALU.mult))
                do(vec.scalar_tensor_tensor(out=cand[:], in0=g[:], scalar=-(2.0 ** (b - 1)) if b else -1.0,
                                            in1=cand[:], op0=ALU.add, op1=ALU.add))

        def select(j, t, m, p):
            n = CLASSES[j][1]
            lo = max(0, n - 512)
            tail = slice(lo, n)
            K, M, Hn, e, o = key[p][:, 0:n], mask[:, 0:n], H[:, 0:n], eq[:, 0:n], order[:, 0:n]
            high = key[p][:].bitcast(I16)[:, 1:2 * n:2]
            low = key[p][:].bitcast(U16)[:, 0:2 * n:2]
            lim, qpos = c.lim[:, at(t, 1)], c.qpos[:, at(t, 1)]
            vec.wait_ge(full[p], m * 16 + 16)
            do(vec.tensor_scalar(M, K, 31, 0x7FFFFFFF, ALU.arith_shift_right, ALU.bitwise_and))
            do(vec.tensor_tensor(K, M, K, ALU.bitwise_xor))
            do(vec.tensor_scalar(junk[:, 0:n - lo], iota[:, tail], lim, None, ALU.is_lt))
            if lo:
                do(vec.tensor_scalar(Hn[:, 0:lo], high[:, 0:lo], 32768.0, None, ALU.add))
            else:
                steps.did(vec.tensor_scalar(g[:], c.zero[:], 0.0, None, ALU.add))
            do(vec.scalar_tensor_tensor(out=Hn[:, tail], in0=high[:, tail], scalar=32768.0, in1=junk[:, 0:n - lo],
                                        op0=ALU.add, op1=ALU.mult))
            search(Hn, 0, float(TOPK))
            do(vec.tensor_scalar(th[:], cand[:], 0.0, None, ALU.add))
            do(vec.tensor_scalar(th1[:], cand[:], 1.0, None, ALU.add))
            do(vec.tensor_scalar(junk[:, 0:n], Hn, th1[:], 0.0, ALU.is_ge, ALU.add, accum_out=cnt[:]))
            do(vec.tensor_scalar(need[:], cnt[:], -1.0, float(TOPK), ALU.mult, ALU.add))
            do(vec.tensor_scalar(e, Hn, th[:], None, ALU.is_equal))
            do(vec.scalar_tensor_tensor(out=f32(K), in0=low, scalar=1.0, in1=e, op0=ALU.add, op1=ALU.mult))
            search(f32(K), 1, need[:])
            do(vec.tensor_scalar(u[:], cand[:], 1.0, None, ALU.add))
            do(vec.tensor_scalar(junk[:, 0:n], f32(K), u[:], 0.0, ALU.is_ge, ALU.add, accum_out=cnt[:]))
            do(vec.tensor_tensor(need[:], need[:], cnt[:], ALU.subtract))
            do(vec.tensor_scalar(e, f32(K), cand[:], None, ALU.is_equal))
            do(vec.tensor_tensor_scan(o, e, e, 0.0, ALU.add, ALU.max))
            do(vec.scalar_tensor_tensor(out=e, in0=o, scalar=need[:], in1=e, op0=ALU.is_le, op1=ALU.mult))
            do(vec.scalar_tensor_tensor(out=e, in0=f32(K), scalar=u[:], in1=e, op0=ALU.is_ge, op1=ALU.add))
            do(vec.scalar_tensor_tensor(out=e, in0=Hn, scalar=th1[:], in1=e, op0=ALU.is_ge, op1=ALU.add))
            do(vec.scalar_tensor_tensor(out=e[:, tail], in0=iota[:, tail], scalar=lim, in1=e[:, tail],
                                        op0=ALU.is_lt, op1=ALU.mult))
            do(vec.tensor_scalar(f32(K), e, -1.0, MASKED, ALU.add, ALU.mult))
            do(vec.scalar_tensor_tensor(out=f32(K), in0=iota[:, 0:n], scalar=qpos, in1=f32(K),
                                        op0=ALU.subtract, op1=ALU.min))
            do(vec.tensor_scalar(o[:, tail], iota[:, tail], -1.0, qpos, ALU.mult, ALU.add))
            vec.tensor_tensor(f32(K[:, tail]), o[:, tail], f32(K[:, tail]), ALU.min).then_inc(done[p], 1)

        vec.wait_ge(iota_made, 1)
        query_tiles(lambda j: steps.turns(2, 2 * SELECT_STEPS), select)

    c.selected = (stored[0], 16 * (DT // 2 + 1)), (stored[1], 16 * (DT // 2))
    return Programs(sync=sync, vector=vector, gpsimd=gpsimd)


def token_tiles(eng, body, turns=None):
    with (turns or eng.Fori(0, DT // 2)) as i:
        body(i * 2, i, 0)
        body(i * 2 + 1, i, 1)
    body(DT, DT // 2, 0)


GMLP_STEPS = 7 + RSQRT_STEPS + 4


def stage_gmlp(c):
    nc, sb = c.nc, Sbuf(c.nc, c.first)
    w_raw = sb("g_wraw", [P, 4, P])
    wT = sb("g_wT", [P, 4, P])
    bias = sb("g_bias", [P, 4, P])
    ln_g = sb("g_lng", [P, BW])
    ln_b = sb("g_lnb", [P, BW])
    vT, uT, zT, vn, ob = ([sb(f"g_{n}{p}", [P, 4, P]) for p in range(2)] for n in ("vT", "uT", "zT", "vn", "ob"))
    stats = sb("g_stats", [P, 6])
    mv = sb("g_mv", [P, 2])
    mean = sb("g_mean", [P, 1])
    var, rstd, tmp = sb("g_var", [P, 1]), sb("g_rstd", [P, 1]), sb("g_tmp", [P, 1])
    S = c.sem
    own_steps = S("g_steps")
    const_full = S("g_const_full")
    w_turned = S("g_w_turned")
    w_ready = S("g_w_ready")
    v_full = [S(f"g_v_full{p}") for p in range(2)]
    uz_full = [S(f"g_uz_full{p}") for p in range(2)]
    turned = [S(f"g_turned{p}") for p in range(2)]
    normed = [S(f"g_normed{p}") for p in range(2)]
    mixed = [S(f"g_mixed{p}") for p in range(2)]
    gated = [S(f"g_gated{p}") for p in range(2)]
    stored = [S(f"g_stored{p}") for p in range(2)]
    v_stored = S("g_v_stored")
    slot = lambda s, t: c.T_dram[s:s + 4, :, at(t)].rearrange("s q t -> q s t")

    def sync(sp):
        for s, n in c.T_stored + list(c.selected):
            sp.wait_ge(s, n)
        sp.dma_start(w_raw[:], c.I["gmlp_ws"].rearrange("(g i) j -> i g j", g=4)).then_inc(const_full, 16)
        sp.dma_start(bias[:].rearrange("q g i -> q (g i)"),
                     c.I["gmlp_bs"].rearrange("g i -> (g i)").partition_broadcast(P)).then_inc(const_full, 16)
        sp.dma_start(ln_g[:], c.I["gmlp_ln_g"].partition_broadcast(P)).then_inc(const_full, 16)
        sp.dma_start(ln_b[:], c.I["gmlp_ln_b"].partition_broadcast(P)).then_inc(const_full, 16)

        def load(t, m, p):
            sp.wait_ge(turned[p], m)
            sp.dma_start(vT[p][:], slot(S_GV, t)).then_inc(v_full[p], 16)
            sp.wait_ge(gated[p], m)
            sp.dma_start(uT[p][:], slot(S_U, t)).then_inc(uz_full[p], 16)
            sp.dma_start(zT[p][:], slot(S_ZB, t)).then_inc(uz_full[p], 16)
        token_tiles(sp, load)

    def tensor(pe):
        pe.wait_ge(const_full, 64)
        for g in range(4):
            last = pe.transpose(c.psum[:, 4, g * P:(g + 1) * P], w_raw[:, g, :], c.ident[:])
        last.then_inc(w_turned, 1)
        pe.wait_ge(w_ready, 2)

        def turn(t, m, p):
            pe.wait_ge(v_full[p], m * 16 + 16)
            pe.wait_ge(normed[p], m)
            for s in range(4):
                last = pe.transpose(c.psum[:, p, s * P:(s + 1) * P], vT[p][:, s, :], c.ident[:])
            last.then_inc(turned[p], 1)

        def mix(t, m, p):
            rows = DEC if isinstance(t, int) else P
            pe.wait_ge(normed[p], m + 1)
            pe.wait_ge(gated[p], m)
            for g in range(4):
                last = pe.matmul(c.psum[:, 2 + p, g * P:(g + 1) * P], vn[p][0:rows, g, :], wT[0:rows, g, :],
                                 start=True, stop=True)
            last.then_inc(mixed[p], 1)

        turn(0, 0, 0)
        with pe.Fori(0, DT // 2) as i:
            turn(i * 2 + 1, i, 1)
            mix(i * 2, i, 0)
            turn(i * 2 + 2, i + 1, 0)
            mix(i * 2 + 1, i, 1)
        mix(DT, DT // 2, 0)

    def vector(vec):
        steps = Steps(vec, own_steps)
        do = steps.did_wait
        vec.wait_ge(w_turned, 1)
        vec.tensor_copy(wT[:], c.psum[:, 4, :].rearrange("q (g i) -> q g i", g=4)).then_inc(w_ready, 1)
        vec.wait_ge(w_ready, 1)
        vec.memset(wT[CHUNK:P, :, 0:CHUNK], 0.0).then_inc(w_ready, 1)

        def norm(t, m, p):
            vec.wait_ge(turned[p], m + 1)
            vec.wait_ge(mixed[p], m)
            v = c.psum[:, p, :]
            do(vec.bn_stats(stats[:], v))
            do(vec.tensor_tensor(mv[:], stats[:, 1:3], stats[:, 4:6], ALU.add))
            do(vec.tensor_tensor(tmp[:], stats[:, 1:2], stats[:, 4:5], ALU.subtract))
            do(vec.tensor_scalar(mean[:], mv[:, 0:1], 0.5, None, ALU.mult))
            do(vec.scalar_tensor_tensor(out=tmp[:], in0=tmp[:], scalar=0.25, in1=tmp[:], op0=ALU.mult, op1=ALU.mult))
            do(vec.scalar_tensor_tensor(out=var[:], in0=mv[:, 1:2], scalar=1.0 / BW, in1=tmp[:], op0=ALU.mult, op1=ALU.add))
            do(vec.tensor_scalar(var[:], var[:], EPS, None, ALU.add))
            rsqrt(steps, rstd[:], var[:], tmp[:])
            flat = vn[p][:].rearrange("q g n -> q (g n)")
            do(vec.tensor_scalar(flat, v, mean[:], rstd[:], ALU.subtract, ALU.mult))
            do(vec.tensor_tensor(flat, flat, ln_g[:], ALU.mult))
            vec.tensor_tensor(flat, flat, ln_b[:], ALU.add).then_inc(normed[p], 1)

        def gate(t, m, p):
            vec.wait_ge(mixed[p], m + 1)
            vec.wait_ge(uz_full[p], m * 32 + 32)
            vec.wait_ge(stored[p], m * 16)
            mix = c.psum[:, 2 + p, :].rearrange("q (g i) -> q g i", g=4)
            do(vec.tensor_tensor(ob[p][:], mix, bias[:], ALU.add))
            do(vec.tensor_tensor(ob[p][:], ob[p][:], uT[p][:], ALU.mult))
            vec.tensor_tensor(ob[p][:], ob[p][:], zT[p][:], ALU.mult).then_inc(gated[p], 1)

        vec.wait_ge(const_full, 64)
        norm(0, 0, 0)
        with steps.turns(DT // 2, 2 * GMLP_STEPS) as i:
            norm(i * 2 + 1, i, 1)
            gate(i * 2, i, 0)
            norm(i * 2 + 2, i + 1, 0)
            gate(i * 2 + 1, i, 1)
        gate(DT, DT // 2, 0)

    def scalar(act):
        def store(t, m, p):
            act.wait_ge(gated[p], m + 1)
            act.dma_start(c.B_dram[1, :, :, at(t)].rearrange("s q t -> q s t"), ob[p][:]).then_inc(stored[p], 16)
        token_tiles(act, store)
        act.wait_ge(normed[0], DT // 2 + 1)
        act.dma_start(c.O["gmlp_sample"], vn[0][0:DEC].rearrange("q g n -> q (g n)")).then_inc(v_stored, 16)
        act.wait_ge(v_stored, 16)
        for p in range(2):
            act.wait_ge(stored[p], 16 * (DT // 2 + 1 - p))

    c.gmlp_done = (stored[0], 16 * (DT // 2 + 1)), (stored[1], 16 * (DT // 2)), (v_stored, 16)
    return Programs(sync=sync, scalar=scalar, vector=vector, tensor=tensor)


LEFT = CONV - 1
EXT = LEFT + SEQ + LEFT + DEC
CONVS = EXT - LEFT
DEC_AT = SEQ + LEFT
CONV_SPANS = [(a, min(512, CONVS - a)) for a in range(0, CONVS, 512)]


def stage_conv(c):
    nc, sb = c.nc, Sbuf(c.nc, c.first)
    par = sb("v_par", [P, CW])
    parT = sb("v_parT", [P, 4, CONV + 3])
    state = sb("v_state", [LEFT, CW])
    ones = sb("v_ones", [P, P])
    ext = [sb(f"v_ext{p}", [P, EXT]) for p in range(2)]
    gate = [sb(f"v_gate{p}", [P, TOK]) for p in range(2)]
    y = [sb(f"v_y{s}", [P, CONVS]) for s in range(4)]
    rstd = sb("v_rstd", [P, CONVS])
    tmp = sb("v_tmp", [P, CONVS])
    tails = sb("v_tails", [LEFT, 2, CW])
    S = c.sem
    own_steps = S("v_steps")
    par_full, par_turned, par_ready = S("v_par_full"), S("v_par_turned"), S("v_par_ready")
    a_full = [S(f"v_a_full{p}") for p in range(2)]
    ext_ready, tail_turned, tail_copied, conv_done = S("v_ext"), S("v_tail_turned"), S("v_tail_copied"), S("v_conv")
    tails_stored = S("v_tails_stored")
    summed, var_summed, centred, rooted, normed = S("v_summed"), S("v_var_summed"), S("v_centred"), S("v_rooted"), S("v_normed")
    acted, gated, stored = S("v_acted"), S("v_gated"), S("v_stored")
    z_full = [S(f"v_z_full{p}") for p in range(2)]
    squared = S("v_squared")

    def sync(sp):
        for s, n in c.gmlp_done:
            sp.wait_ge(s, n)
        for row, name, n in ((0, "conv_w", CONV), (CONV, "conv_b", 1), (CONV + 1, "conv_ln_g", 1), (CONV + 2, "conv_ln_b", 1)):
            sp.dma_start(par[row:row + n, :], c.I[name]).then_inc(par_full, 16)
        sp.dma_start(state[:], c.I["state_conv"]).then_inc(par_full, 16)
        for s in range(4):
            p = s % 2
            if s >= 2:
                sp.wait_ge(conv_done, s - 1)
                sp.wait_ge(tail_turned, s - 1)
            sp.dma_start(ext[p][:, LEFT:LEFT + SEQ], c.T_dram[S_GA + s, :, 0:SEQ]).then_inc(a_full[p], 16)
            sp.dma_start(ext[p][:, LEFT + SEQ + LEFT:EXT], c.T_dram[S_GA + s, :, SEQ:SEQ + DEC]).then_inc(a_full[p], 16)
            sp.dma_start(gate[p][:], c.T_dram[S_GG + s]).then_inc(a_full[p], 16)
        for s in range(4):
            sp.wait_ge(ext_ready, 4)
            if s >= 2:
                sp.wait_ge(gated, s - 1)
            sp.dma_start(gate[s % 2][:], c.T_dram[S_ZC + s]).then_inc(z_full[s % 2], 16)
        for s in range(4):
            sp.wait_ge(gated, s + 1)
            sp.dma_start(c.B_dram[2, s, :, 0:SEQ], y[s][:, 0:SEQ]).then_inc(stored, 16)
            sp.dma_start(c.B_dram[2, s, :, SEQ:SEQ + DEC], y[s][:, DEC_AT:CONVS]).then_inc(stored, 16)
        sp.wait_ge(tail_copied, 4)
        sp.dma_start(c.O["conv_prompt"], tails[:, 0, :]).then_inc(tails_stored, 16)
        sp.dma_start(c.O["conv_sample"], tails[:, 1, :]).then_inc(tails_stored, 16)
        sp.wait_ge(tails_stored, 32)
        sp.wait_ge(stored, 128)

    def tensor(pe):
        pe.wait_ge(par_full, 80)
        for s in range(4):
            pe.transpose(c.psum[:, 0, s * 64:s * 64 + CONV + 3], par[0:CONV + 3, s * P:(s + 1) * P], c.ident[0:CONV + 3, 0:CONV + 3])
            last = pe.transpose(c.psum[:, 1, s * 64:s * 64 + LEFT], state[:, s * P:(s + 1) * P], c.ident[0:LEFT, 0:LEFT])
        last.then_inc(par_turned, 1)
        for s in range(4):
            pe.wait_ge(ext_ready, s + 1)
            if s >= 1:
                pe.wait_ge(tail_copied, s)
            pe.transpose(c.psum[0:LEFT, 2, 0:P], ext[s % 2][:, SEQ:SEQ + LEFT], c.ident[:])
            pe.transpose(c.psum[0:LEFT, 2, P:2 * P], ext[s % 2][:, EXT - LEFT:EXT], c.ident[:]).then_inc(tail_turned, 1)
        pe.wait_ge(conv_done, 4)
        for b, (a, w) in enumerate(CONV_SPANS):
            for s in range(4):
                last = pe.matmul(c.psum[:, 3 + b, 0:w], ones[:], y[s][:, a:a + w], start=(s == 0), stop=(s == 3))
        last.then_inc(summed, 1)
        pe.wait_ge(centred, 4)
        for s in range(4):
            pe.wait_ge(squared, s + 1)
            for b, (a, w) in enumerate(CONV_SPANS):
                last = pe.matmul(c.psum[:, 3 + b, 0:w], ones[:], tmp[:, a:a + w], start=(s == 0), stop=(s == 3))
            last.then_inc(var_summed, 1)

    def vector(vec):
        steps = Steps(vec, own_steps)
        do = steps.did_wait
        for s, n in c.gmlp_done:
            vec.wait_ge(s, n)
        do(vec.memset(ones[:], 1.0 / CW))
        do(vec.memset(ext[0][:, 0:LEFT], 0.0))
        do(vec.memset(ext[1][:, 0:LEFT], 0.0))
        vec.wait_ge(par_turned, 1)
        do(vec.tensor_copy(parT[:], c.psum[:, 0, 0:256].rearrange("q (s n) -> q s n", s=4)[:, :, 0:CONV + 3]))
        for s in range(4):
            p = s % 2
            tap = lambda k: parT[:, s, k:k + 1]
            vec.wait_ge(a_full[p], (s // 2 + 1) * 48)
            do(vec.tensor_tensor(ext[p][:, LEFT:LEFT + SEQ], ext[p][:, LEFT:LEFT + SEQ], gate[p][:, 0:SEQ], ALU.mult))
            do(vec.tensor_tensor(ext[p][:, EXT - DEC:EXT], ext[p][:, EXT - DEC:EXT], gate[p][:, SEQ:SEQ + DEC], ALU.mult))
            do(vec.tensor_copy(ext[p][:, LEFT + SEQ:DEC_AT + LEFT], c.psum[:, 1, s * 64:s * 64 + LEFT]))
            vec.sem_inc(ext_ready, 1)
            do(vec.tensor_scalar(y[s][:], ext[p][:, 0:CONVS], tap(0), tap(CONV), ALU.mult, ALU.add))
            for k in range(1, CONV):
                do(vec.scalar_tensor_tensor(out=y[s][:], in0=ext[p][:, k:k + CONVS], scalar=tap(k), in1=y[s][:],
                                            op0=ALU.mult, op1=ALU.add))
            vec.sem_inc(conv_done, 1)
            vec.wait_ge(tail_turned, s + 1)
            vec.tensor_copy(tails[:, :, s * P:(s + 1) * P], c.psum[0:LEFT, 2, 0:2 * P].rearrange("q (u n) -> q u n", u=2)
                            ).then_inc(tail_copied, 1)
        mean = c.psum[:, 3:8, :].rearrange("q b n -> q (b n)")[:, 0:CONVS]
        vec.wait_ge(summed, 1)
        for s in range(4):
            vec.tensor_tensor(y[s][:], y[s][:], mean, ALU.subtract).then_inc(centred, 1)
        vec.wait_ge(centred, 4)
        for s in range(4):
            if s:
                vec.wait_ge(var_summed, s)
            vec.tensor_tensor(tmp[:], y[s][:], y[s][:], ALU.mult).then_inc(squared, 1)
        vec.wait_ge(var_summed, 4)
        do(vec.tensor_scalar(tmp[:], mean, EPS, None, ALU.add))
        vec.sem_inc(rooted, 1)
        vec.wait_ge(acted, 1)
        do(vec.reciprocal(rstd[:], rstd[:]))
        do(vec.tensor_tensor(tmp[:], tmp[:], rstd[:], ALU.mult))
        do(vec.tensor_tensor(tmp[:], tmp[:], rstd[:], ALU.mult))
        do(vec.tensor_scalar(tmp[:], tmp[:], -0.5, 1.5, ALU.mult, ALU.add))
        do(vec.tensor_tensor(rstd[:], rstd[:], tmp[:], ALU.mult))
        for s in range(4):
            vec.tensor_tensor(y[s][:], y[s][:], rstd[:], ALU.mult).then_inc(normed, 1)
        for s in range(4):
            vec.wait_ge(acted, s + 2)
            vec.wait_ge(z_full[s % 2], (s // 2 + 1) * 16)
            z = gate[s % 2]
            do(vec.tensor_tensor(y[s][:, 0:SEQ], y[s][:, 0:SEQ], z[:, 0:SEQ], ALU.mult))
            vec.tensor_tensor(y[s][:, DEC_AT:CONVS], y[s][:, DEC_AT:CONVS], z[:, SEQ:SEQ + DEC], ALU.mult).then_inc(gated, 1)

    def scalar(act):
        act.wait_ge(rooted, 1)
        act.activation(rstd[:], tmp[:], ACT.Sqrt).then_inc(acted, 1)
        for s in range(4):
            act.wait_ge(normed, s + 1)
            act.activation(y[s][:], y[s][:], ACT.Silu, scale=parT[:, s, CONV + 1:CONV + 2],
                           bias=parT[:, s, CONV + 2:CONV + 3]).then_inc(acted, 1)

    c.conv_done = (stored, 128), (tails_stored, 32)
    return Programs(sync=sync, scalar=scalar, vector=vector, tensor=tensor)


LOWEST = -3.0e38


def stage_attend(c):
    nc, sb = c.nc, Sbuf(c.nc, c.first)
    NS, NV = PAST + DEC, PAST // P + 1
    k_hi, k_lo, ks_hi, ks_lo = ([sb(f"a_{n}{g}", [P, w], F32R) for g in range(KVH)]
                                for n, w in (("khi", SEQ), ("klo", SEQ), ("kshi", NS), ("kslo", NS)))
    v_p = sb("a_vp", [P, DT, KVH, P], F32R)
    v_s = sb("a_vs", [P, NV, KVH, P], F32R)
    nd = [sb(f"a_nd{p}", [P, SEQ]) for p in range(2)]
    L = [sb(f"a_l{h}", [P, SEQ]) for h in range(HEADS)]
    q2 = [sb(f"a_q2{p}", [P, HEADS, P]) for p in range(2)]
    qs = [sb(f"a_qs{p}", [P, HEADS, P], F32R) for p in range(2)]
    scale = sb("a_scale", [P, HEADS])
    pT_hi = [sb(f"a_pthi{u}", [P, 512], F32R) for u in range(2)]
    pT_lo = [sb(f"a_ptlo{u}", [P, 512], F32R) for u in range(2)]
    za = [sb(f"a_za{p}", [HD, HEADS, P]) for p in range(2)]
    oa = [sb(f"a_oa{p}", [HD, HEADS, P]) for p in range(2)]
    o_low = sb("a_olow", [HD, 512])
    peaks = sb("a_peaks", [P, HEADS, 4])
    peak = sb("a_peak", [P, HEADS])
    nbias = sb("a_nbias", [P, HEADS])
    sums = sb("a_sums", [P, HEADS])
    rs = sb("a_rs", [P, HEADS])
    S = c.sem
    own_steps = S("a_steps")
    k_full, v_full, cache_full, vs_full, cache_turned = (S("a_" + n) for n in ("k_full", "v_full", "cache_full", "vs_full", "cache_turned"))
    operands = S("a_operands")
    scale_set = S("a_scale_set")
    nd_full, q_full, za_full, q_scaled, q_hi, q_ready, o_done, stored = (
        [S(f"a_{n}{p}") for p in range(2)] for n in ("nd_full", "q_full", "za_full", "q_scaled", "q_hi", "q_ready", "o_done", "stored"))
    qk_full = S("a_qk_full")
    qk_read = [S(f"a_qk_read{b}") for b in range(4)]
    mark = S("a_mark")
    head_ready, exp_done, rs_ready, pt_full, pt_hi, bc_full, o_copied = (
        S("a_" + n) for n in ("head_ready", "exp_done", "rs_ready", "pt_full", "pt_hi", "bc_full", "o_copied"))
    pt_lo = [S(f"a_pt_lo{u}") for u in range(2)]
    pv_used = [S(f"a_pv_used{u}") for u in range(2)]
    PT, PO, PB = (4, 5), 6, 7
    kraw = [L[g] for g in range(KVH)]
    vraw = L[2][:].rearrange("q (t n) -> q t n", t=DT)
    vsraw = L[3][:, 0:NV * P].rearrange("q (t n) -> q t n", t=NV)
    cache = L[4][:].rearrange("q (t g u d) -> q t g u d", t=PAST // P, g=KVH, u=2)
    new_k = [L[5 + g][:, 0:DEC] for g in range(KVH)]

    per_tile = [HEADS * len(pieces(keys)) for _, keys in CLASSES]
    before = [4 * sum(per_tile[:j]) for j in range(len(CLASSES))]
    ktiles = [-(-keys // P) for _, keys in CLASSES]
    kt_before = [4 * 2 * sum(ktiles[:j]) for j in range(len(CLASSES))]

    def turn_of(j, m):
        return m - CLASSES[j][0] // 2 if not isinstance(m, int) else 0

    def score_units(j, m, p, g):
        i = turn_of(j, m)
        spans = pieces(CLASSES[j][1])
        for n, (r, (s, (a, w))) in enumerate((r, s) for r in range(4) for s in enumerate(spans)):
            u = before[j] + p * per_tile[j] + g * 4 * len(spans) + n
            yield 4 * g + r, s, a, w, u % 4, i * (per_tile[j] // 2) + u // 4, i * (2 * per_tile[j]) + u

    def key_units(j, m, p, g):
        i = turn_of(j, m)
        for kt in range(ktiles[j]):
            u = kt_before[j] + (2 * p + g) * ktiles[j] + kt
            yield kt, min(P, CLASSES[j][1] - kt * P), u % 2, i * (2 * ktiles[j]) + u // 2, i * (4 * ktiles[j]) + u

    def group_order(score, weigh, loop):
        for j, (t0, _) in enumerate(CLASSES):
            if t0 == DT:
                groups = [(j, DT, DT // 2, 0, g) for g in range(2)]
                score(*groups[0])
                score(*groups[1])
                weigh(*groups[0])
                weigh(*groups[1])
                continue
            with loop(j) as i:
                groups = [(j, i * 2 + (t0 + p), i + t0 // 2, p, g) for p in range(2) for g in range(2)]
                score(*groups[0])
                for n in range(4):
                    if n < 3:
                        score(*groups[n + 1])
                    weigh(*groups[n])

    def output_free(eng, m, p, g):
        if g:
            eng.wait_ge(o_done[p], m * 2 + 1)
        else:
            eng.wait_ge(o_done[1 - p], (m + p) * 2)

    def by_head(slot):
        return c.T_dram[slot:slot + 4].rearrange("s q t -> (s q) t").rearrange("(h d) t -> d h t", d=HD)

    def sync(sp):
        for g in range(KVH):
            doubled(sp, kraw[g], c.T_dram[S_K, g * HD:(g + 1) * HD, 0:SEQ], k_full)
            doubled(sp, new_k[g], c.T_dram[S_K, g * HD:(g + 1) * HD, SEQ:SEQ + DEC], k_full)
            for u in range(2):
                sp.dma_start(cache[:, :, g, u, :],
                             c.I["cache_k"].rearrange("(t q g) d -> q t g d", q=P, g=KVH)[:, :, g, :]).then_inc(cache_full, 16)
        sp.dma_start(vraw, c.O["v_prompt"].rearrange("(t q g) d -> q t (g d)", q=P, g=KVH)).then_inc(v_full, 16)
        sp.dma_start(vsraw[:, 0:NV - 1, :], c.I["cache_v"].rearrange("(t q g) d -> q t (g d)", q=P, g=KVH)).then_inc(vs_full, 16)
        sp.dma_start(vsraw[0:DEC, NV - 1, :], c.O["v_sample"].rearrange("(q g) d -> q (g d)", g=KVH)).then_inc(vs_full, 16)

        def load(j, t, m, p):
            keys = CLASSES[j][1]
            sp.wait_ge(q_ready[p], m)
            doubled(sp, q2[p], by_head(S_Q)[:, :, at(t)], q_full[p])
            sp.wait_ge(o_done[p], m * 2)
            sp.dma_start(nd[p][:, 0:keys], c.ND_dram[at(t, 1), :, 0:keys].rearrange("a q n -> q (a n)")).then_inc(nd_full[p], 16)
            sp.dma_start(za[p][:], by_head(S_ZA)[:, :, at(t)]).then_inc(za_full[p], 16)
        query_tiles(lambda j: sp.Fori(0, 2), load)

    def gpsimd(pool):
        for h in range(HEADS):
            pool.memset(scale[:, h:h + 1], HD ** -0.5 * 2.0 ** (h + 1)).then_inc(scale_set, 1)
        pool.wait_ge(scale_set, HEADS)
        scales = scale[:].unsqueeze(2).to_broadcast([P, HEADS, P])
        zeros = c.zero[:].unsqueeze(1).to_broadcast([P, HEADS, P])

        def split(t, m, p):
            pool.wait_ge(q_ready[1 - p], m + p)
            pool.wait_ge(q_full[p], m * 32 + 32)
            pool.wait_ge(o_done[p], m * 2)
            pool.tensor_tensor(q2[p][:], q2[p][:], scales, ALU.mult).then_inc(q_scaled[p], 1)
            pool.wait_ge(q_scaled[p], m + 1)
            pool.tensor_tensor(qs[p][:], q2[p][:], zeros, ALU.add).then_inc(q_hi[p], 1)
            pool.wait_ge(q_hi[p], m + 1)
            pool.tensor_tensor(qs[p][HD:P], q2[p][HD:P], f32(qs[p][HD:P]), ALU.subtract).then_inc(q_ready[p], 1)

        def store(t, m, p):
            pool.wait_ge(o_done[p], m * 2 + 2)
            pool.dma_start(c.B_dram[0].rearrange("s q t -> (s q) t").rearrange("(h d) t -> d h t", d=HD)[:, :, at(t)],
                           oa[p][:]).then_inc(stored[p], 16)

        split(0, 0, 0)
        with pool.Fori(0, DT // 2) as i:
            split(i * 2 + 1, i, 1)
            store(i * 2, i, 0)
            split(i * 2 + 2, i + 1, 0)
            store(i * 2 + 1, i, 1)
        store(DT, DT // 2, 0)
        for p in range(2):
            pool.wait_ge(stored[p], 16 * (DT // 2 + 1 - p))

    cacheT = [c.psum[:, 2 * g:2 * g + 2, :].rearrange("q b n -> q (b n)") for g in range(KVH)]

    def tensor(pe):
        pe.wait_ge(cache_full, 64)
        for g in range(KVH):
            for t in range(PAST // P):
                last = pe.transpose(cacheT[g][:, t * P:(t + 1) * P], cache[:, t, g].rearrange("q u d -> q (u d)"), c.ident[:])
        last.then_inc(cache_turned, 1)
        pe.wait_ge(operands, 1)

        def score(j, t, m, p, g):
            hi, lo = (ks_hi[g], ks_lo[g]) if t is DT else (k_hi[g], k_lo[g])
            pe.wait_ge(q_ready[p], m + 1)
            for h, s, a, w, b, nb, n in score_units(j, m, p, g):
                pe.wait_ge(qk_read[b], nb)
                pe.matmul(c.psum[:, b, 0:w], qs[p][:, h, :], hi[:, a:a + w], start=True, stop=False)
                pe.matmul(c.psum[:, b, 0:w], qs[p][:, h, :], lo[:, a:a + w], start=False, stop=True).then_inc(qk_full, 1)

        def weigh(j, t, m, p, g):
            v = v_s if t is DT else v_p
            units = list(key_units(j, m, p, g))

            def turn(kt, w, u, nu, n):
                pe.wait_ge(pt_lo[u], nu)
                for r in range(4):
                    last = pe.transpose(c.psum[0:w, PT[u], r * P:(r + 1) * P], L[4 * g + r][:, kt * P:kt * P + w], c.ident[:])
                last.then_inc(pt_full, 1)

            pe.wait_ge(exp_done, t * 8 + (4 * g + 4))
            turn(*units[0])
            for x, (kt, w, u, nu, n) in enumerate(units):
                if x + 1 < len(units):
                    turn(*units[x + 1])
                pe.wait_ge(pt_lo[u], nu + 1)
                if x == 0:
                    output_free(pe, m, p, g)
                pe.matmul(c.psum[:, PO, :], v[0:w, kt, g, :], pT_hi[u][0:w, :], start=(x == 0), stop=False)
                pe.matmul(c.psum[:, PO, :], v[0:w, kt, g, :], pT_lo[u][0:w, :], start=False,
                          stop=(x == len(units) - 1)).then_inc(pv_used[u], 1)
            pe.wait_ge(rs_ready, t * 2 + (g + 1))
            for r in range(4):
                last = pe.matmul(c.psum[:, PB, r * P:(r + 1) * P], rs[:, 4 * g + r:4 * g + r + 1].to_broadcast([P, P]),
                                 c.ident[:], start=True, stop=True)
            last.then_inc(bc_full, 1)
        group_order(score, weigh, lambda j: pe.Fori(0, 2))

    def scalar(act):
        def score(j, t, m, p, g):
            keys = CLASSES[j][1]
            for r in range(4):
                h = 4 * g + r
                act.wait_ge(head_ready, t * 8 + (h + 1))
                act.activation(L[h][:, 0:keys], L[h][:, 0:keys], ACT.Exp, bias=nbias[:, h:h + 1],
                               accum_out=sums[:, h:h + 1]).then_inc(exp_done, 1)

        def weigh(j, t, m, p, g):
            for kt, w, u, nu, n in key_units(j, m, p, g):
                act.wait_ge(pt_full, n + 1)
                act.wait_ge(pv_used[u], nu)
                act.activation(pT_hi[u][0:w, :], c.psum[0:w, PT[u], :], ACT.Copy).then_inc(pt_hi, 1)
            act.wait_ge(pv_used[u], nu + 1)
            act.activation(o_low[:], c.psum[HD:P, PO, :], ACT.Copy).then_inc(o_copied, 1)
        group_order(score, weigh, lambda j: act.Fori(0, 2))

    def vector(vec):
        steps = Steps(vec, own_steps)
        do = steps.did_wait
        vec.wait_ge(k_full, 128)
        vec.wait_ge(cache_turned, 1)
        for g in range(KVH):
            for hi, lo, src in ((k_hi[g][:], k_lo[g][:], kraw[g][:]),
                                (ks_hi[g][:, 0:PAST], ks_lo[g][:, 0:PAST], cacheT[g]),
                                (ks_hi[g][:, PAST:], ks_lo[g][:, PAST:], new_k[g])):
                do(vec.tensor_copy(hi, src))
                do(vec.tensor_tensor(lo, src, f32(hi), ALU.subtract))
        for full, n, v, raw, rows, tiles in ((v_full, 16, v_p, vraw, P, slice(0, DT)),
                                             (vs_full, 32, v_s, vsraw, P, slice(0, NV - 1)),
                                             (vs_full, 32, v_s, vsraw, DEC, slice(NV - 1, NV))):
            vec.wait_ge(full, n)
            for g in range(KVH):
                src, dst = raw[0:rows, tiles, g * HD:(g + 1) * HD], v[0:rows, tiles, g, :]
                do(vec.tensor_copy(dst[:, :, 0:HD], src))
                do(vec.tensor_tensor(dst[:, :, HD:P], src, f32(dst[:, :, 0:HD]), ALU.subtract))
        vec.sem_inc(operands, 1)

        def score(j, t, m, p, g):
            spans = len(pieces(CLASSES[j][1]))
            if g == 0:
                vec.wait_ge(nd_full[p], m * 16 + 16)
            for h, s, a, w, b, nb, n in score_units(j, m, p, g):
                vec.wait_ge(qk_full, n + 1)
                vec.sem_inc(mark, 1)
                vec.tensor_tensor_reduce(out=L[h][:, a:a + w], in0=nd[p][:, a:a + w], in1=c.psum[:, b, 0:w],
                                         scale=2.0 ** -(h + 1), scalar=LOWEST, op0=ALU.add, op1=ALU.max,
                                         accum_out=peaks[:, h, s:s + 1]).then_inc(qk_read[b], 1)
                if s == spans - 1:
                    vec.wait_ge(qk_read[b], nb + 1)
                    top = peaks[:, h, 0:1]
                    if spans > 1:
                        top = peak[:, h:h + 1]
                        do(vec.tensor_reduce(top, peaks[:, h, 0:spans], AX.X, ALU.max))
                    vec.tensor_scalar(nbias[:, h:h + 1], top, -1.0, None, ALU.mult).then_inc(head_ready, 1)

        def weigh(j, t, m, p, g):
            vec.wait_ge(exp_done, t * 8 + (4 * g + 4))
            vec.reciprocal(rs[:, 4 * g:4 * g + 4], sums[:, 4 * g:4 * g + 4]).then_inc(rs_ready, 1)
            for kt, w, u, nu, n in key_units(j, m, p, g):
                vec.wait_ge(pt_hi, n + 1)
                vec.tensor_tensor(pT_lo[u][0:w, :], c.psum[0:w, PT[u], :], f32(pT_hi[u][0:w, :]), ALU.subtract
                                  ).then_inc(pt_lo[u], 1)
            o = oa[p][:, 4 * g:4 * g + 4, :].rearrange("d h t -> d (h t)")
            vec.wait_ge(o_copied, t * 2 + (g + 1))
            vec.wait_ge(bc_full, t * 2 + (g + 1))
            vec.wait_ge(stored[p], m * 16)
            vec.wait_ge(za_full[p], m * 16 + 16)
            do(vec.tensor_tensor(o, c.psum[0:HD, PO, :], o_low[:], ALU.add))
            do(vec.tensor_tensor(o, c.psum[0:HD, PB, :], o, ALU.mult))
            vec.tensor_tensor(o, o, za[p][:, 4 * g:4 * g + 4, :].rearrange("d h t -> d (h t)"), ALU.mult).then_inc(o_done[p], 1)

        def per_turn(j):
            return 2 * (8 * (len(pieces(CLASSES[j][1])) > 1) + 4)
        group_order(score, weigh, lambda j: steps.turns(2, per_turn(j)))

    c.attended = (stored[0], 16 * (DT // 2 + 1)), (stored[1], 16 * (DT // 2))
    return Programs(sync=sync, scalar=scalar, vector=vector, tensor=tensor, gpsimd=gpsimd)


def split_weights(c, prefix, plan, n_raw=2):
    raw, full, hi_done, lo_done = [], [], [], []
    for r in range(n_raw):
        raw.append(c.place(f"{prefix}raw{r}", [P, D]))
        full.append(c.sem(f"{prefix}w_full{r}"))
        hi_done.append(c.sem(f"{prefix}w_hi{r}"))
        lo_done.append(c.sem(f"{prefix}w_lo{r}"))

    def sync(sp):
        for n, (src, hi, lo) in enumerate(plan):
            r = n % n_raw
            sp.wait_ge(hi_done[r], n // n_raw)
            sp.wait_ge(lo_done[r], n // n_raw)
            sp.dma_start(raw[r][:], src).then_inc(full[r], 16)

    def scalar(act):
        for n, (src, hi, lo) in enumerate(plan):
            r = n % n_raw
            act.wait_ge(full[r], 16 * (n // n_raw + 1))
            act.copy(hi, raw[r][:]).then_inc(hi_done[r], 1)

    def vector(vec):
        for n, (src, hi, lo) in enumerate(plan):
            r = n % n_raw
            vec.wait_ge(hi_done[r], n // n_raw + 1)
            vec.tensor_tensor(lo, raw[r][:], f32(hi), ALU.subtract).then_inc(lo_done[r], 1)

    def ready(eng):
        for r in range(n_raw):
            eng.wait_ge(lo_done[r], len(range(r, len(plan), n_raw)))
    return Programs(sync=sync, scalar=scalar, vector=vector, ready=ready)


def stage_merge(c):
    nc, sb = c.nc, Sbuf(c.nc, c.first)
    c.place = sb
    names = ("w_branch_a", "w_branch_b", "w_branch_c")
    w_hi = sb("m_whi", [P, 3, 4, D], F32R)
    w_lo = sb("m_wlo", [P, 3, 4, D], F32R)
    weights = split_weights(c, "m_", [(c.I[names[b]][k * P:(k + 1) * P, :], w_hi[:, b, k, :], w_lo[:, b, k, :])
                                      for b in range(3) for k in range(4)])
    o_raw = [sb(f"m_oraw{x}", [P, 4, 512]) for x in range(2)]
    o_hi = [sb(f"m_ohi{x}", [P, 4, 512], F32R) for x in range(2)]
    o_lo = [sb(f"m_olo{x}", [P, 4, 512], F32R) for x in range(2)]
    gate = [sb(f"m_gate{x}", [P, 2, 512]) for x in range(4)]
    merged = sb("m_merged", [P, 8, 512])
    tmp = [sb(f"m_tmp{x}", [P, 512]) for x in range(2)]
    S = c.sem
    o_full = [S(f"m_o_full{x}") for x in range(2)]
    o_hi_done = [S(f"m_o_hi{x}") for x in range(2)]
    o_lo_done = [S(f"m_o_lo{x}") for x in range(2)]
    g_full = [S(f"m_g_full{x}") for x in range(4)]
    product, gated, added, stored = S("m_product"), S("m_gated"), S("m_added"), S("m_stored")

    def spans(eng, body):
        with eng.Fori(0, 2) as i:
            for y in range(2):
                for b in range(3):
                    body(i, y, b, bass.ds(i * 1024 + y * 512, 512), 512)
        for b in range(3):
            body(2, 0, b, slice(SEQ, SEQ + DEC), DEC)

    def wait(eng, sem, i, y, n, per=24):
        n += per * y
        eng.wait_ge(sem, i * (2 * per) + (n if isinstance(i, int) else max(0, n)))

    def buffer(i, y, b):
        return (3 * y + b) % 2, i * 3 + (3 * y + b) // 2

    def sync(sp):
        for s, n in c.attended:
            sp.wait_ge(s, n)
        weights.sync(sp)

        def load(i, y, b, cols, w):
            u, nu = buffer(i, y, b)
            sp.wait_ge(o_lo_done[u], nu)
            sp.dma_start(o_raw[u][:, :, 0:w], c.B_dram[b, :, :, cols].rearrange("s q t -> q s t")).then_inc(o_full[u], 16)
            for n in range(4):
                wait(sp, gated, i, y, 8 * b - 8 + 2 * n + 2)
                slot = S_G + 8 * b + 2 * n
                sp.dma_start(gate[n][:, :, 0:w], c.T_dram[slot:slot + 2, :, cols].rearrange("s q t -> q s t")).then_inc(g_full[n], 16)
        spans(sp, load)

    def gpsimd(pool):
        def split(i, y, b, cols, w):
            u, nu = buffer(i, y, b)
            zeros = c.zero[:].unsqueeze(1).to_broadcast([P, 4, w])
            pool.wait_ge(o_full[u], nu * 16 + 16)
            wait(pool, product, i, y, 8 * b - 8)
            pool.tensor_tensor(o_hi[u][:, :, 0:w], o_raw[u][:, :, 0:w], zeros, ALU.add).then_inc(o_hi_done[u], 1)
            pool.wait_ge(o_hi_done[u], nu + 1)
            pool.tensor_tensor(o_lo[u][:, :, 0:w], o_raw[u][:, :, 0:w], f32(o_hi[u][:, :, 0:w]), ALU.subtract
                               ).then_inc(o_lo_done[u], 1)
        for s, n in c.attended:
            pool.wait_ge(s, n)
        spans(pool, split)

    def tensor(pe):
        weights.ready(pe)

        def products(i, y, b, cols, w):
            u, nu = buffer(i, y, b)
            pe.wait_ge(o_lo_done[u], nu + 1)
            for n in range(8):
                wait(pe, gated, i, y, 8 * b - 8 + n + 1)
                for k in range(4):
                    for q, (wt, o) in enumerate(((w_hi, o_hi), (w_hi, o_lo), (w_lo, o_hi))):
                        last = pe.matmul(c.psum[:, n, 0:w], wt[:, b, k, n * P:(n + 1) * P], o[u][:, k, 0:w],
                                         start=(k == 0 and q == 0), stop=(k == 3 and q == 2))
                last.then_inc(product, 1)
        spans(pe, products)

    def scalar(act):
        for s, n in c.attended:
            act.wait_ge(s, n)
        weights.scalar(act)

        def store(i, y, b, cols, w):
            if b == 2:
                act.wait_ge(added, i * 32 + (16 * y + 16))
                act.dma_start(c.M_dram[:, :, cols].rearrange("s q t -> q s t"), merged[:, :, 0:w]).then_inc(stored, 16)
        spans(act, store)
        act.wait_ge(stored, 80)

    def vector(vec):
        weights.vector(vec)

        def gating(i, y, b, cols, w):
            for n in range(8):
                wait(vec, product, i, y, 8 * b + n + 1)
                if n % 2 == 0:
                    vec.wait_ge(g_full[n // 2], i * 96 + (48 * y + 16 * b + 16))
                dst = merged[:, n, 0:w] if b == 0 else tmp[n % 2][:, 0:w]
                if b == 0:
                    vec.wait_ge(stored, i * 32 + 16 * y)
                else:
                    vec.wait_ge(added, i * 32 + (16 * y + 8 * (b - 1) + n))
                vec.tensor_tensor(dst, c.psum[:, n, 0:w], gate[n // 2][:, n % 2, 0:w], ALU.mult).then_inc(gated, 1)
                if b:
                    wait(vec, gated, i, y, 8 * b + n + 1)
                    vec.tensor_tensor(merged[:, n, 0:w], merged[:, n, 0:w], dst, ALU.add).then_inc(added, 1)
        spans(vec, gating)

    c.merged_stored = ((stored, 80),)
    return Programs(sync=sync, scalar=scalar, vector=vector, tensor=tensor, gpsimd=gpsimd)


FINISH_STEPS = 2 * (1 + RSQRT_STEPS) + 2


def stage_finish(c):
    nc, sb = c.nc, Sbuf(c.nc, c.first)
    c.place = sb
    KP = 2
    wo_hi, wo_lo, wg_hi, wg_lo = (sb(f"f_{n}", [P, KD, D], F32R) for n in ("wohi", "wolo", "wghi", "wglo"))
    wp_hi, wp_lo = (sb(f"f_{n}", [P, KP, D], F32R) for n in ("wphi", "wplo"))
    weights = split_weights(c, "f_", [(c.I[name][k * P:(k + 1) * P, :], hi[:, k, :], lo[:, k, :])
                                      for name, hi, lo, ks in (("w_out", wo_hi, wo_lo, KD), ("w_ple_gate", wg_hi, wg_lo, KD),
                                                               ("w_ple", wp_hi, wp_lo, KP)) for k in range(ks)])
    ple_g = sb("f_pleg", [P, D])
    fin_g = sb("f_fing", [P, D])
    m_raw = sb("f_mraw", [P, KD, P])
    m_hi = sb("f_mhi", [P, KD, P], F32R)
    m_lo = sb("f_mlo", [P, KD, P], F32R)
    x = [sb(f"f_x{p}", [P, D]) for p in range(2)]
    pl = [sb(f"f_p{p}", [P, KP * P]) for p in range(2)]
    p_hi = sb("f_phi", [P, KP, P], F32R)
    p_lo = sb("f_plo", [P, KP, P], F32R)
    xn = sb("f_xn", [P, D])
    h_hi = sb("f_hhi", [P, KD, P], F32R)
    h_lo = sb("f_hlo", [P, KD, P], F32R)
    sig = sb("f_sig", [P, D])
    ssq = sb("f_ssq", [P, 2])
    var, rstd, tmp = sb("f_var", [P, 1]), sb("f_rstd", [P, 1]), sb("f_tmp", [P, 1])
    S = c.sem
    own_steps = S("f_steps")
    g_full = S("f_g_full")
    m_full, m_hi_done, m_lo_done = S("f_m_full"), S("f_m_hi"), S("f_m_lo")
    x_full = [S(f"f_x_full{p}") for p in range(2)]
    p_full = [S(f"f_p_full{p}") for p in range(2)]
    out_product, added, squared, normed, x_turned, h_hi_done, h_lo_done = (
        S("f_" + n) for n in ("out_product", "added", "squared", "normed", "x_turned", "h_hi", "h_lo"))
    p_turned, p_hi_done, p_lo_done, ple_product, gate_product, sig_done, summed, squared2, finished = (
        S("f_" + n) for n in ("p_turned", "p_hi", "p_lo", "ple_product", "gate_product", "sig_done", "summed", "squared2",
                              "finished"))
    stored = [S(f"f_stored{p}") for p in range(2)]
    pair = lambda b: c.psum[:, b:b + 2, :].rearrange("q b n -> q (b n)")
    b_out, b_turn, b_gate, b_ple = 0, 2, 4, 6

    def sync(sp):
        for s, n in c.merged_stored:
            sp.wait_ge(s, n)
        sp.dma_start(ple_g[:], c.I["ple_norm_g"].partition_broadcast(P)).then_inc(g_full, 16)
        sp.dma_start(fin_g[:], c.I["final_norm_g"].partition_broadcast(P)).then_inc(g_full, 16)
        weights.sync(sp)

        def load(t, m, p):
            last = isinstance(t, int)
            n, rows, r = ("sample", slice(0, DEC), DEC) if last else ("prompt", at(t), P)
            cols = slice(SEQ, SEQ + DEC) if last else at(t)
            sp.wait_ge(m_lo_done, t)
            sp.dma_start(m_raw[:, :, 0:r], c.M_dram[:, :, cols].rearrange("s q t -> q s t")).then_inc(m_full, 16)
            sp.wait_ge(stored[p], m * 16)
            sp.dma_start(x[p][0:r, :], c.I["x_" + n][rows, :]).then_inc(x_full[p], 16)
            sp.dma_start(pl[p][0:r, :], c.I["p_" + n][rows, :]).then_inc(p_full[p], 16)
        token_tiles(sp, load)

    def tensor(pe):
        weights.ready(pe)

        def three(bank, lhs_hi, lhs_lo, w_hi, w_lo, ks):
            for half in range(2):
                cols = slice(half * 512, half * 512 + 512)
                for k in range(ks):
                    for q, (a, w) in enumerate(((lhs_hi, w_hi), (lhs_lo, w_hi), (lhs_hi, w_lo))):
                        last = pe.matmul(pair(bank)[:, cols], a[:, k, :], w[:, k, cols],
                                         start=(k == 0 and q == 0), stop=(k == ks - 1 and q == 2))
            return last

        def out(t, m, p):
            pe.wait_ge(m_lo_done, t + 1)
            pe.wait_ge(added, t)
            three(b_out, m_hi, m_lo, wo_hi, wo_lo, KD).then_inc(out_product, 1)

        def gate(t, m, p):
            pe.wait_ge(p_full[p], m * 16 + 16)
            pe.wait_ge(summed, t)
            for k in range(KP):
                last = pe.transpose(pair(b_ple)[:, k * P:(k + 1) * P], pl[p][:, k * P:(k + 1) * P], c.ident[:])
            last.then_inc(p_turned, 1)
            pe.wait_ge(normed, t + 1)
            pe.wait_ge(h_lo_done, t)
            for k in range(KD):
                last = pe.transpose(pair(b_turn)[:, k * P:(k + 1) * P], xn[:, k * P:(k + 1) * P], c.ident[:])
            last.then_inc(x_turned, 1)
            pe.wait_ge(p_lo_done, t + 1)
            three(b_ple, p_hi, p_lo, wp_hi, wp_lo, KP).then_inc(ple_product, 1)
            pe.wait_ge(h_lo_done, t + 1)
            pe.wait_ge(sig_done, t)
            three(b_gate, h_hi, h_lo, wg_hi, wg_lo, KD).then_inc(gate_product, 1)

        out(0, 0, 0)
        with pe.Fori(0, DT // 2) as i:
            out(i * 2 + 1, i, 1)
            gate(i * 2, i, 0)
            out(i * 2 + 2, i + 1, 0)
            gate(i * 2 + 1, i, 1)
        gate(DT, DT // 2, 0)

    def gpsimd(pool):
        zeros = c.zero[:].unsqueeze(1).to_broadcast([P, KD, P])

        def split(t, m, p):
            pool.wait_ge(m_full, t * 16 + 16)
            pool.wait_ge(out_product, t)
            pool.tensor_tensor(m_hi[:], m_raw[:], zeros, ALU.add).then_inc(m_hi_done, 1)
            pool.wait_ge(m_hi_done, t + 1)
            pool.tensor_tensor(m_lo[:], m_raw[:], f32(m_hi[:]), ALU.subtract).then_inc(m_lo_done, 1)
        for s, n in c.merged_stored:
            pool.wait_ge(s, n)
        token_tiles(pool, split)

    def scalar(act):
        for s, n in c.merged_stored:
            act.wait_ge(s, n)
        weights.scalar(act)

        def start(t, m, p):
            act.wait_ge(added, t + 1)
            act.wait_ge(sig_done, t)
            act.wait_ge(summed, t)
            act.activation(sig[:], x[p][:], ACT.Square, accum_out=ssq[:, 0:1]).then_inc(squared, 1)

        def rest(t, m, p):
            act.wait_ge(p_turned, t + 1)
            act.wait_ge(ple_product, t)
            act.copy(p_hi[:], pair(b_ple)[:, 0:KP * P].rearrange("q (k n) -> q k n", k=KP)).then_inc(p_hi_done, 1)
            act.wait_ge(x_turned, t + 1)
            act.wait_ge(gate_product, t)
            act.copy(h_hi[:], pair(b_turn).rearrange("q (k n) -> q k n", k=KD)).then_inc(h_hi_done, 1)
            act.wait_ge(gate_product, t + 1)
            act.activation(sig[:], pair(b_gate), ACT.Sigmoid).then_inc(sig_done, 1)
            act.wait_ge(summed, t + 1)
            act.wait_ge(x_turned, t + 1)
            act.activation(xn[:], x[p][:], ACT.Square, accum_out=ssq[:, 1:2]).then_inc(squared2, 1)
            act.wait_ge(finished, t + 1)
            last = isinstance(t, int)
            r = DEC if last else P
            act.dma_start(c.O["y_sample"] if last else c.O["y_prompt"][at(t), :], x[p][0:r, :]).then_inc(stored[p], 16)

        def both(t, m, p):
            start(t, m, p)
            rest(t, m, p)
        token_tiles(act, both)
        for p in range(2):
            act.wait_ge(stored[p], 16 * len(range(p, TILES, 2)))

    def vector(vec):
        weights.vector(vec)
        steps = Steps(vec, own_steps)
        do = steps.did_wait

        def root(col):
            do(vec.tensor_scalar(var[:], ssq[:, col:col + 1], 1.0 / D, EPS, ALU.mult, ALU.add))
            rsqrt(steps, rstd[:], var[:], tmp[:])

        def both(t, m, p):
            vec.wait_ge(out_product, t + 1)
            vec.wait_ge(x_full[p], m * 16 + 16)
            vec.tensor_tensor(x[p][:], x[p][:], pair(b_out), ALU.add).then_inc(added, 1)
            vec.wait_ge(squared, t + 1)
            root(0)
            vec.wait_ge(squared2, t)
            do(vec.scalar_tensor_tensor(out=xn[:], in0=x[p][:], scalar=rstd[:], in1=ple_g[:], op0=ALU.mult, op1=ALU.mult))
            vec.sem_inc(normed, 1)
            vec.wait_ge(p_hi_done, t + 1)
            vec.tensor_tensor(p_lo[:], pair(b_ple)[:, 0:KP * P].rearrange("q (k n) -> q k n", k=KP), f32(p_hi[:]),
                              ALU.subtract).then_inc(p_lo_done, 1)
            vec.wait_ge(h_hi_done, t + 1)
            vec.tensor_tensor(h_lo[:], pair(b_turn).rearrange("q (k n) -> q k n", k=KD), f32(h_hi[:]),
                              ALU.subtract).then_inc(h_lo_done, 1)
            vec.wait_ge(sig_done, t + 1)
            vec.wait_ge(ple_product, t + 1)
            do(vec.tensor_tensor(sig[:], pair(b_ple), sig[:], ALU.mult))
            vec.tensor_tensor(x[p][:], x[p][:], sig[:], ALU.add).then_inc(summed, 1)
            vec.wait_ge(squared2, t + 1)
            root(1)
            vec.scalar_tensor_tensor(out=x[p][:], in0=x[p][:], scalar=rstd[:], in1=fin_g[:], op0=ALU.mult,
                                     op1=ALU.mult).then_inc(finished, 1)
        vec.wait_ge(g_full, 32)
        token_tiles(vec, both, steps.turns(DT // 2, 2 * FINISH_STEPS))

    return Programs(sync=sync, scalar=scalar, vector=vector, tensor=tensor, gpsimd=gpsimd)


def stage_turnover(c):
    arrived, cleared = c.lasting_sem("arrived"), c.lasting_sem("cleared")
    numbers = c.release_semaphores()

    def report(eng):
        eng.drain().then_inc(arrived, 1)
        eng.wait_ge(cleared, 1)

    def gpsimd(pool):
        pool.drain().then_inc(arrived, 1)
        pool.wait_ge(arrived, 5)
        pool.sem_clear(numbers).then_inc(cleared, 1)
        pool.wait_ge(cleared, 1)

    return Programs(sync=report, scalar=report, vector=report, tensor=report, gpsimd=gpsimd)


OUTPUTS = [("y_prompt", (1, SEQ, D)), ("y_sample", (1, DEC, D)),
           ("k_prompt", (1, 1, SEQ, KVH, HD)), ("v_prompt", (1, 1, SEQ, KVH, HD)),
           ("ik_prompt", (1, 1, SEQ, HD)), ("conv_prompt", (1, 1, CONV - 1, CW)),
           ("k_sample", (1, 1, DEC, KVH, HD)), ("v_sample", (1, 1, DEC, KVH, HD)),
           ("ik_sample", (1, 1, DEC, HD)), ("conv_sample", (1, 1, CONV - 1, CW)),
           ("gmlp_sample", (1, 1, DEC, BW))]


def build(nc, I, O, stages=None):
    with ExitStack() as ctx:
        c = Shared()
        c.nc, c.I, c.O = nc, I, O
        c.lasting_sem = lambda name: ctx.enter_context(nc.semaphore(name))
        passing, held = ExitStack(), []

        def sem(name):
            held.append(passing.enter_context(nc.semaphore(name)))
            return held[-1]

        def release_semaphores():
            numbers = sorted(s.num for s in held)
            held.clear()
            passing.close()
            assert numbers == list(range(numbers[0], numbers[-1] + 1)), numbers
            return range(numbers[0], numbers[-1] + 1)

        c.sem, c.release_semaphores = sem, release_semaphores
        c.psum = ctx.enter_context(nc.psum_tensor("psum", [P, 8, 512], F32))
        sb = Sbuf(nc, (nc.sbuf_base + 31) // 32 * 32)
        c.ident = sb("ident", [P, P])
        c.zero = sb("zero", [P, 1])
        c.ident_ready = c.lasting_sem("ident_ready")
        c.aw = sb("aw", [P, TILES, IH])
        c.sg = sb("sg", [P, TILES, IH])
        c.weights_ready = c.lasting_sem("weights_ready")
        c.w_full = [c.lasting_sem(f"j_w_full{p}") for p in range(2)]
        c.natural_stored = [c.lasting_sem(f"t_stored{p}") for p in range(2)]
        c.acc_stored = [c.lasting_sem(f"i_stored{p}") for p in range(2)]
        c.qpos = sb("qpos", [P, TILES])
        c.lim = sb("lim", [P, TILES])
        c.first = sb.at
        c.hT_hi = sb("hT_hi", [P, KD, TOK], F32R)
        c.hT_lo = sb("hT_lo", [P, KD, TOK], F32R)
        c.after_hT = sb.at
        c.ND_dram = nc.dram_tensor("ND_dram", [TILES, P, SEQ], F32).ap()
        c.M_dram = nc.dram_tensor("M_dram", [KD, P, TOK], F32).ap()
        c.B_dram = nc.dram_tensor("B_dram", [3, 4, P, TOK], F32).ap()
        c.SC_dram = nc.dram_tensor("SC_dram", [TILES, P, SEQ], F32).ap()
        c.T_dram = nc.dram_tensor("T_dram", [SLOTS, P, TOK], F32).ap()
        identity_step = c.lasting_sem("identity_step")
        parts = [s(c) for s in (stages or STAGES)]
        block = ctx.enter_context(nc.Block())

        @block.sync
        def _(sp):
            for s in parts:
                if s.sync:
                    s.sync(sp)

        @block.gpsimd
        def _(pool):
            pool.memset(c.zero[:], 0.0).then_inc(identity_step, 1)
            pool.memset(c.ident[:], 0.0).then_inc(identity_step, 1)
            pool.wait_ge(identity_step, 2)
            pool.affine_select(out=c.ident[:], in_=c.ident[:], compare_op=ALU.not_equal, fill=1.0, base=0,
                               pattern=[[-1, P]], channel_multiplier=1).then_inc(c.ident_ready, 1)
            for s in parts:
                if s.gpsimd:
                    s.gpsimd(pool)

        @block.scalar
        def _(act):
            for s in parts:
                if s.scalar:
                    s.scalar(act)

        @block.vector
        def _(vec):
            for s in parts:
                if s.vector:
                    s.vector(vec)

        @block.tensor
        def _(pe):
            for s in parts:
                if s.tensor:
                    s.tensor(pe)
        passing.close()


STAGES = [stage_constants, stage_norm, stage_project_first, stage_natural, stage_scores, stage_select, stage_project_rest, stage_gmlp, stage_conv, stage_turnover, stage_attend, stage_merge, stage_finish]


def kernel(**inputs):
    import concourse.bacc as bacc
    from concourse.bass_utils import run_bass_kernel_spmd

    nc = bacc.Bacc("TRN2", target_bir_lowering=False, num_devices=1)
    arrays, I, O = {}, {}, {}
    for name, value in inputs.items():
        a = np.ascontiguousarray(value)
        arrays[f"in_{name}"] = a = a.reshape(-1, a.shape[-1])
        I[name] = nc.dram_tensor(f"in_{name}", a.shape, F32, kind="ExternalInput").ap()
    for name, shape in OUTPUTS:
        O[name] = nc.dram_tensor(f"out_{name}", (int(np.prod(shape[:-1])), shape[-1]), F32,
                                 kind="ExternalOutput").ap()
    build(nc, I, O)
    r = run_bass_kernel_spmd(nc, [arrays], core_ids=[0])
    return tuple(np.asarray(r.results[0][f"out_{name}"]).reshape(shape) for name, shape in OUTPUTS)
```

```python
from contextlib import ExitStack, contextmanager

import numpy as np

import concourse.bass as bass
import concourse.mybir as mybir
from concourse.alu_op_type import AluOpType as ALU

F32 = mybir.dt.float32
F32R = mybir.dt.float32r
BF16 = mybir.dt.bfloat16
I32 = mybir.dt.int32
I16 = mybir.dt.int16
U16 = mybir.dt.uint16
U8 = mybir.dt.uint8
ACT = mybir.ActivationFunctionType
AX = mybir.AxisListType

P = 128
D = 1024
KD = D // P
SEQ, DEC, PAST = 2048, 32, 1024
TILES = SEQ // P + 1
DT = TILES - 1
TOK = SEQ + DEC
SPAN = 416
EPS = 1e-6
HD = 64
HEADS, KVH, IH = 8, 2, 4
AW = HEADS * HD
BW = CW = 512
CONV = 31
CHUNK = 64
TOPK = 256
IN_COLS = 7748
IDX_W_SCALE = (IH * HD) ** -0.5
C_Q, C_K, C_V, C_IQ, C_IK, C_IW, C_ZA, C_U, C_GV, C_ZB, C_GA, C_GG, C_ZC, C_G = (
    0, 512, 640, 768, 1024, 1088, 1092, 1604, 2116, 2628, 3140, 3652, 4164, 4676)
SPANS = [(a, SPAN) for a in range(0, TOK, SPAN)]
assert TOK == len(SPANS) * SPAN


class Shared:
    pass


class Programs:

    def __init__(self, sync=None, gpsimd=None, scalar=None, vector=None, tensor=None, ready=None):
        self.sync, self.gpsimd, self.scalar, self.vector, self.tensor = sync, gpsimd, scalar, vector, tensor
        self.ready = ready


class Steps:

    def __init__(self, eng, sem):
        self.eng, self.sem, self.base, self.n = eng, sem, 0, 0

    def did(self, ins):
        ins.then_inc(self.sem, 1)
        self.n += 1

    def wait(self):
        self.eng.wait_ge(self.sem, self.base + self.n)

    def did_wait(self, ins):
        self.did(ins)
        self.wait()

    @contextmanager
    def turns(self, count, per):
        start = self.base + self.n
        with self.eng.Fori(0, count) as i:
            self.base, self.n = i * per + start, 0
            yield i
            assert self.n == per, (self.n, per)
        self.base, self.n = start + count * per, 0


RSQRT_STEPS = 11


def rsqrt(steps, y, v, t):
    vec = steps.eng
    yi, ti = y.bitcast(I32), t.bitcast(I32)
    steps.did_wait(vec.tensor_scalar(ti, v.bitcast(I32), 1, None, ALU.logical_shift_right))
    steps.did_wait(vec.tensor_scalar(yi, ti, -1.0, 1597463007.0, ALU.mult, ALU.add))
    for _ in range(3):
        steps.did_wait(vec.scalar_tensor_tensor(out=t, in0=y, scalar=v, in1=y, op0=ALU.mult, op1=ALU.mult))
        steps.did_wait(vec.tensor_scalar(t, t, -0.5, 1.5, ALU.mult, ALU.add))
        steps.did_wait(vec.tensor_tensor(y, y, t, ALU.mult))


class Sbuf:

    def __init__(self, nc, at):
        self.nc, self.at = nc, at

    def __call__(self, name, shape, dt=F32):
        size = {F32: 4, F32R: 4, I32: 4, BF16: 2, I16: 2, U16: 2, U8: 1}[dt]
        n = int(np.prod(shape[1:])) * size
        n = (n + 31) // 32 * 32
        t = self.nc.alloc_sbuf_tensor_at(name, shape, dt, offset=self.at)
        self.at += n
        assert self.at <= self.nc.sbuf_usable_end, (name, self.at)
        return t


def f32(ap):
    return ap.bitcast(F32)


def at(t, n=P):
    return slice(t * n, min((t + 1) * n, TOK)) if isinstance(t, int) else bass.ds(t * n, n)


def real(t):
    return DEC if isinstance(t, int) and t == DT else P



def stage_norm(c):
    nc, sb = c.nc, Sbuf(c.nc, c.after_hT)
    x_in = [sb(f"n_x{p}", [P, D]) for p in range(2)]
    xn = [sb(f"n_xn{p}", [P, D]) for p in range(2)]
    junk = [sb(f"n_junk{p}", [P, D]) for p in range(2)]
    g_rows = sb("n_g", [P, D])
    ssq = [sb(f"n_ssq{p}", [P, 1]) for p in range(2)]
    var = sb("n_var", [P, 1])
    rstd = sb("n_rstd", [P, 1])
    tmp = sb("n_tmp", [P, 1])
    S = c.sem
    own_steps = S("n_steps")
    g_full = S("n_g_full")
    x_full = [S(f"n_x_full{p}") for p in range(2)]
    squared = [S(f"n_squared{p}") for p in range(2)]
    normed = [S(f"n_normed{p}") for p in range(2)]
    turned = [S(f"n_turned{p}") for p in range(2)]
    hi_done = [S(f"n_hi{p}") for p in range(2)]
    lo_done = [S(f"n_lo{p}") for p in range(2)]
    half = DT // 2
    pT = [c.psum[:, 2 * p:2 * p + 2, :].rearrange("q b (k t) -> q (b k) t", k=4) for p in range(2)]

    def cols(i, p):
        return bass.ds((i * 2 + p) * P, P) if not isinstance(i, int) else at(2 * i + p)

    def width(i, p):
        return real(2 * i + p) if isinstance(i, int) else P

    def sync(sp):
        sp.dma_start(g_rows[:], c.I["norm_g"].partition_broadcast(P)).then_inc(g_full, 16)

        def load(i, p, last=False):
            sp.wait_ge(squared[p], i)
            sp.wait_ge(normed[p], i)
            if last:
                sp.dma_start(x_in[p][0:DEC, :], c.I["x_sample"]).then_inc(x_full[p], 16)
            else:
                sp.dma_start(x_in[p][:], c.I["x_prompt"][cols(i, p), :]).then_inc(x_full[p], 16)

        with sp.Fori(0, half) as i:
            load(i, 0)
            load(i, 1)
        load(half, 0, last=True)

    def scalar(act):
        def square(i, p):
            act.wait_ge(x_full[p], i * 16 + 16)
            act.wait_ge(normed[p], i)
            act.wait_ge(squared[p], i)
            act.activation(junk[p][:], x_in[p][:], ACT.Square, accum_out=ssq[p][:]).then_inc(squared[p], 1)

        def high(i, p):
            act.wait_ge(turned[p], i + 1)
            act.copy(c.hT_hi[:, :, cols(i, p)], pT[p][:, :, 0:width(i, p)]).then_inc(hi_done[p], 1)

        square(0, 0)
        with act.Fori(0, half) as i:
            square(i, 1)
            high(i, 0)
            square(i + 1, 0)
            high(i, 1)
        high(half, 0)

    def vector(vec):
        steps = Steps(vec, own_steps)

        def norm(i, p):
            vec.wait_ge(squared[p], i + 1)
            vec.wait_ge(turned[p], i)
            steps.did_wait(vec.tensor_scalar(var[:], ssq[p][:], 1.0 / D, EPS, ALU.mult, ALU.add))
            rsqrt(steps, rstd[:], var[:], tmp[:])
            vec.scalar_tensor_tensor(out=xn[p][:], in0=x_in[p][:], scalar=rstd[:], in1=g_rows[:],
                                     op0=ALU.mult, op1=ALU.mult).then_inc(normed[p], 1)

        def low(i, p):
            vec.wait_ge(turned[p], i + 1)
            vec.wait_ge(hi_done[p], i + 1)
            vec.tensor_tensor(c.hT_lo[:, :, cols(i, p)], pT[p][:, :, 0:width(i, p)], f32(c.hT_hi[:, :, cols(i, p)]),
                              ALU.subtract).then_inc(lo_done[p], 1)

        per = 1 + RSQRT_STEPS
        vec.wait_ge(g_full, 16)
        norm(0, 0)
        with steps.turns(half, 2 * per) as i:
            norm(i, 1)
            low(i, 0)
            norm(i + 1, 0)
            low(i, 1)
        low(half, 0)

    def tensor(pe):
        def turn(i, p):
            pe.wait_ge(normed[p], i + 1)
            pe.wait_ge(hi_done[p], i)
            pe.wait_ge(lo_done[p], i)
            for k in range(KD):
                last = pe.transpose(pT[p][:, k, :], xn[p][:, k * P:(k + 1) * P], c.ident[:])
            last.then_inc(turned[p], 1)

        pe.wait_ge(c.ident_ready, 1)
        with pe.Fori(0, half) as i:
            turn(i, 0)
            turn(i, 1)
        turn(half, 0)

    c.hT_done = (hi_done[0], half + 1), (hi_done[1], half), (lo_done[0], half + 1), (lo_done[1], half)
    return Programs(sync=sync, scalar=scalar, vector=vector, tensor=tensor)


S_IKW, S_Q, S_K, S_V, S_IQ, S_GA, S_U, S_GV, S_ZA, S_ZB, S_ZC, S_GG, S_G = (
    0, 1, 5, 6, 7, 9, 13, 17, 21, 25, 29, 33, 37)
FIRST_RUNS = [(C_IK, 1, S_IKW, "copy"), (C_Q, 8, S_Q, "copy")]
REST_RUNS = [(C_GA, 4, S_GA, "copy"), (C_GG, 4, S_GG, "sigmoid"), (C_ZC, 4, S_ZC, "silu"), (C_G, 24, S_G, "sigmoid"),
             (C_ZA, 4, S_ZA, "silu"), (C_U, 8, S_U, "gelu"), (C_ZB, 4, S_ZB, "silu")]
CONV_RUN = 3
JUMP_RUN = 4
SLOTS = sum(r[1] for r in FIRST_RUNS + REST_RUNS)
FUNC = {"copy": ACT.Copy, "gelu": ACT.Gelu, "silu": ACT.Silu, "sigmoid": ACT.Sigmoid}
OUTS = 3
FIRST_JOBS = sum(r[1] for r in FIRST_RUNS)
FIRST_OF_CONV = FIRST_JOBS + sum(r[1] for r in REST_RUNS[:CONV_RUN])
FIRST_OF_JUMP = FIRST_JOBS + sum(r[1] for r in REST_RUNS[:JUMP_RUN])


def project(c, first):
    nc = c.nc
    if first:
        sb = Sbuf(nc, c.after_hT)
        c.w_raw = sb("j_w", [P, KD, P])
        c.w_hi = [sb(f"j_whi{p}", [P, KD, P], F32R) for p in range(2)]
        c.w_lo = [sb(f"j_wlo{p}", [P, KD, P], F32R) for p in range(2)]
        c.out = [sb(f"j_out{r}", [P, SPAN]) for r in range(OUTS)]
        c.after_project = sb.at
        S = c.sem
        c.w_hi_done, c.w_lo_done, c.bank_full, c.bank_read = (
            S("j_" + n) for n in ("w_hi_done", "w_lo_done", "bank_full", "bank_read"))
        c.stored = [S(f"j_stored{r}") for r in range(OUTS)]
    w_raw, w_hi, w_lo, out = c.w_raw, c.w_hi, c.w_lo, c.out
    w_full, hi_done, lo_done, bank_full, bank_read, stored = (
        c.w_full, c.w_hi_done, c.w_lo_done, c.bank_full, c.bank_read, c.stored)
    uses = [len(range(r, len(SPANS), OUTS)) for r in range(OUTS)]
    w_in = c.I["w_in"].rearrange("(k q) n -> q k n", q=P)

    def pairs(eng, body, j, n, *starts, loop=True):
        def turn(i):
            for o in range(2):
                body(i * 2 + (j + o), (j + o) % 2, o, i, *(i * (2 * step) + (start + o * step) for start, step in starts))
        if loop:
            with eng.Fori(0, n // 2) as i:
                turn(i)
        else:
            turn(0)

    def jobs(eng, body):
        j = 0 if first else FIRST_JOBS
        for col, n, slot, func in FIRST_RUNS if first else REST_RUNS:
            if n == 1:
                body(j, j % 2, 0, None, slot, func)
            else:
                pairs(eng, lambda job, p, o, i, slot: body(job, p, o, i + (j - FIRST_OF_CONV) // 2 if j >= FIRST_OF_CONV else None,
                                                           slot, func), j, n, (slot, 1))
            j += n

    def load(pool, j, col):
        pool.wait_ge(lo_done, j)
        cols = bass.ds(col, P) if not isinstance(col, int) else slice(col, col + P)
        pool.dma_start(w_raw[:], w_in[:, :, cols]).then_inc(w_full, 16)

    def low(pool, j, p):
        pool.wait_ge(hi_done, j + 1)
        pool.tensor_tensor(w_lo[p][:], w_raw[:], f32(w_hi[p][:]), ALU.subtract).then_inc(lo_done, 1)

    def gpsimd_first(pool):
        for s, n in c.hT_done:
            pool.wait_ge(s, n)
        zeros = c.zero[:].unsqueeze(1).to_broadcast([P, KD, P])

        def weights(j, p, o, i, col):
            load(pool, j, col)
            pool.wait_ge(w_full, j * 16 + 16)
            if not isinstance(j, int):
                pool.wait_ge(bank_full, j * 5 - 5)
            pool.tensor_tensor(w_hi[p][:], w_raw[:], zeros, ALU.add).then_inc(hi_done, 1)
            low(pool, j, p)
        weights(0, 0, 0, 0, FIRST_RUNS[0][0])
        pairs(pool, weights, 1, FIRST_JOBS - 1, (FIRST_RUNS[1][0], P))

    def gpsimd_rest(pool):
        for s, n in c.scores_stored:
            pool.wait_ge(s, n)
        load(pool, FIRST_JOBS, C_GA)

        def weights(j, p, o, i, col, jump_to=None):
            pool.wait_ge(bank_full, j * 5 - 5)
            low(pool, j, p)
            load(pool, j + 1, col + P if jump_to is None else jump_to)

        def weights_and_unit(j, p, o, i, col, jump_to=None):
            weights(j, p, o, i, col, jump_to if o else None)
            c.add_taps(pool, (j - (FIRST_OF_CONV + o)) // 2 if isinstance(j, int) else i + unit0[0], o)

        unit0 = [0]
        n = FIRST_OF_CONV - FIRST_JOBS
        pairs(pool, weights, FIRST_JOBS, n, (C_GA, P))
        for start, end, col, jump_to in ((FIRST_OF_CONV, FIRST_OF_JUMP, C_G, C_ZA), (FIRST_OF_JUMP, SLOTS, C_ZA, C_Q)):
            unit0[0] = (start - FIRST_OF_CONV) // 2
            pairs(pool, weights_and_unit, start, end - start - 2, (col, P))
            pairs(pool, lambda *a: weights_and_unit(*a, jump_to=jump_to), end - 2, 2, (col + (end - start - 2) * P, P), loop=False)
        pool.wait_ge(hi_done, SLOTS + 1)

    def tensor(pe):
        for s, n in c.hT_done:
            pe.wait_ge(s, n)
        if not first:
            for s, n in c.scores_stored:
                pe.wait_ge(s, n)

        def job(j, p, *_):
            pe.wait_ge(lo_done, j + 1)
            for b, (t0, n) in enumerate(SPANS):
                if not isinstance(j, int):
                    pe.wait_ge(bank_read, j * 5 + (b - 4))
                bank = c.psum[:, b, 0:n]
                for k in range(KD):
                    for q, (w, h) in enumerate(((w_hi, c.hT_hi), (w_hi, c.hT_lo), (w_lo, c.hT_hi))):
                        last = pe.matmul(bank, w[p][:, k, :], h[:, k, t0:t0 + n],
                                         start=(k == 0 and q == 0), stop=(k == KD - 1 and q == 2))
                last.then_inc(bank_full, 1)
        jobs(pe, job)

    def scalar(act):
        def high(j, p):
            act.wait_ge(w_full, j * 16 + 16)
            act.wait_ge(bank_full, j * 5 - 5)
            act.copy(w_hi[p][:], w_raw[:]).then_inc(hi_done, 1)

        def evacuate(j, p, o, unit, slot, func):
            for b, (t0, n) in enumerate(SPANS):
                if b == 1 and not first:
                    high(j + 1, 1 - p)
                if unit is not None:
                    c.make_taps(act, unit, o, b)
                r = b % OUTS
                act.wait_ge(bank_full, j * 5 + (b + 1))
                act.wait_ge(stored[r], j * (16 * uses[r]) + 16 * (b // OUTS))
                act.activation(out[r][:], c.psum[:, b, 0:n], FUNC[func]).then_inc(bank_read, 1)
                act.wait_ge(bank_read, j * 5 + (b + 1))
                act.dma_start(c.T_dram[at(slot, 1), :, t0:t0 + n].rearrange("a q t -> q (a t)"), out[r][:]).then_inc(stored[r], 16)
        if not first:
            high(FIRST_JOBS, FIRST_JOBS % 2)
        jobs(act, evacuate)

    done = [(s, 16 * uses[r] * (FIRST_JOBS if first else SLOTS)) for r, s in enumerate(stored)]
    if first:
        c.first_stored = done
        c.conv_inputs_stored = [(s, 16 * uses[r] * (FIRST_JOBS + 8)) for r, s in enumerate(stored)]
    else:
        c.T_stored = done
    return Programs(scalar=scalar, tensor=tensor, gpsimd=gpsimd_first if first else gpsimd_rest)


def stage_project_first(c):
    return project(c, True)


def stage_project_rest(c):
    return project(c, False)


CLASSES = [(4 * j, 512 * (j + 1)) for j in range(4)] + [(DT, PAST + DEC)]


def pieces(keys):
    return [(a, min(512, keys - a)) for a in range(0, keys, 512)]


def query_tiles(loop, body):
    for j, (t0, keys) in enumerate(CLASSES):
        if t0 == DT:
            body(j, DT, DT // 2, 0)
            continue
        with loop(j) as i:
            for p in range(2):
                body(j, i * 2 + (t0 + p), i + t0 // 2, p)


def doubled(eng, dst, src, sem):
    eng.dma_start(dst[0:HD], src).then_inc(sem, 16)
    eng.dma_start(dst[HD:P], src).then_inc(sem, 16)


def stage_natural(c):
    nc, sb = c.nc, Sbuf(c.nc, c.after_hT)
    kvT = [sb(f"t_kvT{p}", [P, 3, P]) for p in range(2)]
    nat = [sb(f"t_nat{p}", [P, 3, P]) for p in range(2)]
    iw = sb("t_iw", [P, TILES, IH])
    S = c.sem
    own_steps = S("t_steps")
    full = [S(f"t_full{p}") for p in range(2)]
    turned = [S(f"t_turned{p}") for p in range(2)]
    copied = [S(f"t_copied{p}") for p in range(2)]
    iw_read = [S(f"t_iw_read{p}") for p in range(2)]
    stored = c.natural_stored
    half = DT // 2

    def tiles(eng, body):
        with eng.Fori(0, half) as i:
            body(i * 2, i, 0)
            body(i * 2 + 1, i, 1)
        body(DT, half, 0)

    def sync(sp):
        for s, n in c.first_stored:
            sp.wait_ge(s, n)

        def load(t, m, p):
            sp.wait_ge(turned[p], m)
            sp.dma_start(kvT[p][:, 0:2, 0:real(t)], c.T_dram[S_K:S_K + 2, :, at(t)].rearrange("s q t -> q s t")).then_inc(full[p], 16)
            sp.dma_start(kvT[p][:, 2, 0:real(t)], c.T_dram[S_IKW, :, at(t)]).then_inc(full[p], 16)
        tiles(sp, load)

    def tensor(pe):
        pe.wait_ge(c.bank_read, 5 * FIRST_JOBS)

        def turn(t, m, p):
            pe.wait_ge(full[p], m * 32 + 32)
            pe.wait_ge(copied[p], m)
            for s in range(3):
                last = pe.transpose(c.psum[:, p, s * P:(s + 1) * P], kvT[p][:, s, :], c.ident[:])
            last.then_inc(turned[p], 1)
        tiles(pe, turn)

    def vector(vec):
        steps = Steps(vec, own_steps)

        def copy(t, m, p):
            vec.wait_ge(turned[p], m + 1)
            vec.wait_ge(stored[p], m * 48)
            vec.wait_ge(iw_read[p], m)
            vec.tensor_copy(nat[p][:], c.psum[:, p, 0:3 * P].rearrange("q (s n) -> q s n", s=3)).then_inc(copied[p], 1)
            vec.wait_ge(copied[p], m + 1)
            vec.tensor_copy(iw[:, bass.ds(t, 1) if not isinstance(t, int) else slice(t, t + 1), :],
                            nat[p][:, 2:3, HD:HD + IH]).then_inc(iw_read[p], 1)
        tiles(vec, copy)
        for p in range(2):
            vec.wait_ge(iw_read[p], half + 1 - p)
        steps.did_wait(vec.tensor_scalar(c.sg[:], iw[:], 0.0, 2.0, ALU.is_ge, ALU.mult))
        steps.did_wait(vec.tensor_scalar(c.sg[:], c.sg[:], -1.0, None, ALU.add))
        steps.did_wait(vec.tensor_scalar(iw[:], iw[:], IDX_W_SCALE, 0.0, ALU.mult, ALU.add))
        vec.tensor_tensor(c.aw[:], iw[:], c.sg[:], ALU.mult).then_inc(c.weights_ready, 1)

    def gpsimd(pool):
        def store(t, m, p):
            pool.wait_ge(copied[p], m + 1)
            for s, n, name in ((0, P, "k"), (1, P, "v"), (2, HD, "ik")):
                if isinstance(t, int):
                    dst, rows = c.O[name + "_sample"], DEC
                else:
                    dst, rows = c.O[name + "_prompt"].rearrange("(t h) d -> t (h d)", t=SEQ)[at(t), :], P
                if isinstance(t, int):
                    dst = dst.rearrange("(t h) d -> t (h d)", t=DEC)
                pool.dma_start(dst, nat[p][0:rows, s, 0:n]).then_inc(stored[p], 16)
        tiles(pool, store)
        for p in range(2):
            pool.wait_ge(stored[p], 48 * (half + 1 - p))

    c.natural_freed = (stored[0], 48 * (half + 1)), (stored[1], 48 * half), (c.weights_ready, 1)
    return Programs(sync=sync, vector=vector, tensor=tensor, gpsimd=gpsimd)


def stage_scores(c):
    nc, sb = c.nc, Sbuf(c.nc, c.after_hT)
    NS = PAST + DEC
    ik_hi = sb("i_ikhi", [P, SEQ], F32R)
    ik_lo = sb("i_iklo", [P, SEQ], F32R)
    iks_hi = sb("i_ikshi", [P, NS], F32R)
    iks_lo = sb("i_ikslo", [P, NS], F32R)
    acc = [sb(f"i_acc{p}", [P, SEQ]) for p in range(2)]
    iq2 = [sb(f"i_iq{p}", [P, IH, P]) for p in range(2)]
    iqs = [sb(f"i_iqs{p}", [P, IH, P], F32R) for p in range(2)]
    R = [sb(f"i_r{r}", [P, 512]) for r in range(4)]
    aw = [sb(f"i_aw{p}", [P, IH]) for p in range(2)]
    S = c.sem
    own_steps = S("i_steps")
    raw_full = S("i_raw_full")
    raws_full = S("i_raws_full")
    cache_full = S("i_cache_full")
    cache_turned = S("i_cache_turned")
    ik_ready = S("i_ik_ready")
    iq_full = [S(f"i_iq_full{p}") for p in range(2)]
    iqs_ready = [S(f"i_iqs_ready{p}") for p in range(2)]
    product = S("i_product")
    bank_read = [S(f"i_bank_read{b}") for b in range(8)]
    r_used = [S(f"i_r_used{r}") for r in range(4)]
    acc_ready = [S(f"i_acc_ready{p}") for p in range(2)]
    stored = c.acc_stored
    cache = acc[1][:, 0:SEQ // 2].rearrange("q (t u d) -> q t u d", t=8, u=2)
    cacheT = c.psum[:, 0:2, :].rearrange("q b n -> q (b n)")
    new_ik = acc[1][:, SEQ // 2:SEQ // 2 + DEC]

    per_tile = [IH * len(pieces(keys)) for _, keys in CLASSES]
    before = [4 * sum(per_tile[:j]) for j in range(len(CLASSES))]

    def units(j, m, p):
        t0, keys = CLASSES[j]
        i = m - t0 // 2 if not isinstance(m, int) else 0
        for n, (h, (a, w)) in enumerate((h, s) for h in range(IH) for s in pieces(keys)):
            u = p * per_tile[j] + n
            start = before[j] + u
            turn = 2 * per_tile[j]
            back = start - len(pieces(keys))
            yield (h, a, w, u % 8, i * (turn // 8) + start // 8, u % 4, i * (turn // 4) + start // 4,
                   i * turn + start, back % 4, i * (turn // 4) + back // 4 + 1)

    def fori(eng):
        return lambda j: eng.Fori(0, 2)

    def sync(sp):
        for s, n in c.natural_freed:
            sp.wait_ge(s, n)
        doubled(sp, acc[0], c.T_dram[S_IKW, 0:HD, 0:SEQ], raw_full)
        doubled(sp, new_ik, c.T_dram[S_IKW, 0:HD, SEQ:SEQ + DEC], raws_full)
        for u in range(2):
            sp.dma_start(cache[:, :, u, :], c.I["cache_idx_k"].rearrange("(t q) d -> q t d", q=P)).then_inc(cache_full, 16)

        def load(j, t, m, p):
            sp.wait_ge(iqs_ready[p], m)
            rows = c.T_dram[S_IQ:S_IQ + 2].rearrange("s q t -> (s q) t").rearrange("(h d) t -> d h t", d=HD)
            doubled(sp, iq2[p][:, :, 0:real(t)], rows[:, :, at(t)], iq_full[p])
        query_tiles(fori(sp), load)

    def tensor(pe):
        pe.wait_ge(cache_full, 32)
        for s, n in c.natural_freed:
            pe.wait_ge(s, n)
        for t in range(8):
            last = pe.transpose(cacheT[:, t * P:(t + 1) * P], cache[:, t].rearrange("q u d -> q (u d)"), c.ident[:])
        last.then_inc(cache_turned, 1)
        pe.wait_ge(ik_ready, 1)

        def score(j, t, m, p):
            hi, lo = (iks_hi, iks_lo) if t is DT else (ik_hi, ik_lo)
            pe.wait_ge(iqs_ready[p], m + 1)
            for h, a, w, b, nb, *_ in units(j, m, p):
                pe.wait_ge(bank_read[b], nb)
                pe.matmul(c.psum[:, b, 0:w], iqs[p][:, h, :], hi[:, a:a + w], start=True, stop=False)
                pe.matmul(c.psum[:, b, 0:w], iqs[p][:, h, :], lo[:, a:a + w], start=False, stop=True).then_inc(product, 1)
        query_tiles(fori(pe), score)

    def scalar(act):
        act.wait_ge(c.weights_ready, 1)

        def relu(j, t, m, p):
            for h, a, w, b, _, r, nr, n, *_ in units(j, m, p):
                act.wait_ge(product, n + 1)
                act.wait_ge(r_used[r], nr)
                act.activation(R[r][:, 0:w], c.psum[:, b, 0:w], ACT.Relu,
                               scale=aw[p][:, h:h + 1]).then_inc(bank_read[b], 1)
        query_tiles(fori(act), relu)

    def vector(vec):
        steps = Steps(vec, own_steps)
        vec.wait_ge(raw_full, 32)
        steps.did_wait(vec.tensor_copy(ik_hi[:], acc[0][:]))
        steps.did_wait(vec.tensor_tensor(ik_lo[:], acc[0][:], f32(ik_hi[:]), ALU.subtract))
        vec.wait_ge(raws_full, 32)
        vec.wait_ge(cache_turned, 1)
        for dst, src in ((slice(0, PAST), cacheT), (slice(PAST, NS), new_ik)):
            steps.did_wait(vec.tensor_copy(iks_hi[:, dst], src))
            steps.did_wait(vec.tensor_tensor(iks_lo[:, dst], src, f32(iks_hi[:, dst]), ALU.subtract))
        vec.sem_inc(ik_ready, 1)

        def split(t, m, p):
            vec.wait_ge(iq_full[p], m * 32 + 32)
            steps.did(vec.tensor_scalar(aw[p][:], c.aw[:, at(t, 1), :], 1.0, None, ALU.mult))
            steps.did_wait(vec.tensor_copy(iqs[p][:], iq2[p][:]))
            vec.tensor_tensor(iqs[p][HD:P], iq2[p][HD:P], f32(iqs[p][HD:P]), ALU.subtract).then_inc(iqs_ready[p], 1)

        def add(j, t, m, p):
            if t is not DT:
                split(t + 1, m + p, 1 - p)
            vec.wait_ge(stored[p], m * 16)
            for h, a, w, b, nb, r, nr, n, r_before, n_before in units(j, m, p):
                vec.wait_ge(bank_read[b], nb + 1)
                sg = c.sg[:, at(t, 1), h]
                if h == 0:
                    ins = vec.tensor_scalar(acc[p][:, a:a + w], R[r][:, 0:w], sg, 0.0, ALU.mult, ALU.add)
                else:
                    vec.wait_ge(r_used[r_before], n_before)
                    ins = vec.scalar_tensor_tensor(out=acc[p][:, a:a + w], in0=R[r][:, 0:w], scalar=sg,
                                                   in1=acc[p][:, a:a + w], op0=ALU.mult, op1=ALU.add)
                ins.then_inc(r_used[r], 1)
            vec.wait_ge(r_used[r], nr + 1)
            vec.sem_inc(acc_ready[p], 1)
        split(0, 0, 0)
        query_tiles(lambda j: steps.turns(2, 4), add)

    def gpsimd(pool):
        def store(j, t, m, p):
            pool.wait_ge(acc_ready[p], m + 1)
            keys = CLASSES[j][1]
            dst = c.SC_dram[at(t, 1), :, 0:keys].rearrange("a q n -> q (a n)")
            pool.dma_start(dst, acc[p][:, 0:keys]).then_inc(stored[p], 16)
        query_tiles(fori(pool), store)

    c.scores_stored = (stored[0], 16 * (DT // 2 + 1)), (stored[1], 16 * (DT // 2))
    return Programs(sync=sync, scalar=scalar, vector=vector, tensor=tensor, gpsimd=gpsimd)


def stage_constants(c):
    nc, sb = c.nc, Sbuf(c.nc, c.after_hT)
    sb.at += 4 * 14 * 1024
    pos = sb("c_pos", [P, TILES], I32)
    chunk = sb("c_chunk", [P, TILES], I32)
    made, step = c.sem("c_made"), c.sem("c_step")

    def gpsimd(pool):
        pool.iota(pos[:, 0:DT], pattern=[[P, DT]], base=0, channel_multiplier=1).then_inc(made, 1)
        pool.iota(pos[:, DT:TILES], pattern=[[0, 1]], base=PAST, channel_multiplier=1).then_inc(made, 1)

    def vector(vec):
        steps = Steps(vec, step)
        vec.wait_ge(made, 2)
        steps.did_wait(vec.tensor_copy(c.qpos[:], pos[:]))
        steps.did_wait(vec.tensor_scalar(chunk[:], pos[:], 6, None, ALU.arith_shift_right))
        steps.did_wait(vec.tensor_scalar(c.lim[:], chunk[:], 1.0, float(CHUNK), ALU.add, ALU.mult))

    return Programs(gpsimd=gpsimd, vector=vector)


MASKED = 1e30
PACE = 1.0
SELECT_STEPS = 2 * 49 + 23


def stage_select(c):
    nc, sb = c.nc, Sbuf(c.nc, c.after_convolve)
    key = [sb(f"s_key{p}", [P, SEQ], I32) for p in range(2)]
    mask = sb("s_mask", [P, SEQ], I32)
    junk = sb("s_junk", [P, SEQ], BF16)
    order = sb("s_order", [P, SEQ], I16)
    iota = sb("s_iota", [P, SEQ], I16)
    cnt, g, cand, th, need, u, th1 = (sb(f"s_{n}", [P, 1]) for n in ("cnt", "g", "cand", "th", "need", "u", "th1"))
    H = mask[:, 0:SEQ // 2].bitcast(U16)
    eq = mask[:, SEQ // 2:].bitcast(BF16)
    S = c.sem
    own_steps = S("s_steps")
    full = [S(f"s_full{p}") for p in range(2)]
    done = [S(f"s_done{p}") for p in range(2)]
    stored = [S(f"s_stored{p}") for p in range(2)]
    iota_made = S("s_iota_made")

    def sync(sp):
        for s, n in c.scores_stored:
            sp.wait_ge(s, n)

        columns = [CLASSES[t // 4][1] + 200 for t in range(TILES)]

        def unit_due(u):
            return PACE * sum(columns) * (FIRST_OF_CONV - FIRST_JOBS + 2 * u) / (SLOTS - FIRST_JOBS)

        upcoming = [0]

        def units(until):
            while upcoming[0] <= UNITS and unit_due(upcoming[0]) < until:
                if upcoming[0]:
                    c.move_unit(sp, upcoming[0] - 1)
                if upcoming[0] < UNITS:
                    c.load_unit(sp, upcoming[0])
                upcoming[0] += 1

        def rows(dram, t):
            keys = CLASSES[t // 4][1]
            return dram[t, :, 0:keys], key[t % 2][:, 0:keys]

        for t in range(TILES + 1):
            p = t % 2
            if t < TILES:
                dram, sbuf = rows(c.SC_dram, t)
                sp.wait_ge(stored[p], t // 2 * 16)
                sp.dma_start(sbuf, dram.bitcast(I32)).then_inc(full[p], 16)
            units(sum(columns[:t]))
            if t > 0:
                dram, sbuf = rows(c.ND_dram, t - 1)
                sp.wait_ge(done[1 - p], (t - 1) // 2 + 1)
                sp.dma_start(dram, f32(sbuf)).then_inc(stored[1 - p], 16)
        units(float("inf"))
        for p in range(2):
            sp.wait_ge(stored[p], 16 * (DT // 2 + 1 - p))

    def gpsimd(pool):
        for s, n in c.scores_stored:
            pool.wait_ge(s, n)
        pool.iota(iota[:], pattern=[[1, SEQ]], base=0, channel_multiplier=0).then_inc(iota_made, 1)

    def vector(vec):
        steps = Steps(vec, own_steps)
        do = steps.did_wait

        def search(src, first, k):
            do(vec.tensor_scalar(cand[:], c.zero[:], float(first + 2 ** 15), None, ALU.add))
            for b in reversed(range(16)):
                do(vec.tensor_scalar(junk[:, 0:src.shape[1]], src, cand[:], 0.0, ALU.is_ge, ALU.add, accum_out=cnt[:]))
                do(vec.tensor_scalar(g[:], cnt[:], k, float(2 ** b), ALU.is_ge, ALU.mult))
                do(vec.scalar_tensor_tensor(out=cand[:], in0=g[:], scalar=-(2.0 ** (b - 1)) if b else -1.0,
                                            in1=cand[:], op0=ALU.add, op1=ALU.add))

        def select(j, t, m, p):
            n = CLASSES[j][1]
            lo = max(0, n - 512)
            tail = slice(lo, n)
            K, M, Hn, e, o = key[p][:, 0:n], mask[:, 0:n], H[:, 0:n], eq[:, 0:n], order[:, 0:n]
            high = key[p][:].bitcast(I16)[:, 1:2 * n:2]
            low = key[p][:].bitcast(U16)[:, 0:2 * n:2]
            lim, qpos = c.lim[:, at(t, 1)], c.qpos[:, at(t, 1)]
            vec.wait_ge(full[p], m * 16 + 16)
            do(vec.tensor_scalar(M, K, 31, 0x7FFFFFFF, ALU.arith_shift_right, ALU.bitwise_and))
            do(vec.tensor_tensor(K, M, K, ALU.bitwise_xor))
            do(vec.tensor_scalar(junk[:, 0:n - lo], iota[:, tail], lim, None, ALU.is_lt))
            if lo:
                do(vec.tensor_scalar(Hn[:, 0:lo], high[:, 0:lo], 32768.0, None, ALU.add))
            else:
                steps.did(vec.tensor_scalar(g[:], c.zero[:], 0.0, None, ALU.add))
            do(vec.scalar_tensor_tensor(out=Hn[:, tail], in0=high[:, tail], scalar=32768.0, in1=junk[:, 0:n - lo],
                                        op0=ALU.add, op1=ALU.mult))
            search(Hn, 0, float(TOPK))
            do(vec.tensor_scalar(th[:], cand[:], 0.0, None, ALU.add))
            do(vec.tensor_scalar(th1[:], cand[:], 1.0, None, ALU.add))
            do(vec.tensor_scalar(junk[:, 0:n], Hn, th1[:], 0.0, ALU.is_ge, ALU.add, accum_out=cnt[:]))
            do(vec.tensor_scalar(need[:], cnt[:], -1.0, float(TOPK), ALU.mult, ALU.add))
            do(vec.tensor_scalar(e, Hn, th[:], None, ALU.is_equal))
            do(vec.scalar_tensor_tensor(out=f32(K), in0=low, scalar=1.0, in1=e, op0=ALU.add, op1=ALU.mult))
            search(f32(K), 1, need[:])
            do(vec.tensor_scalar(u[:], cand[:], 1.0, None, ALU.add))
            do(vec.tensor_scalar(junk[:, 0:n], f32(K), u[:], 0.0, ALU.is_ge, ALU.add, accum_out=cnt[:]))
            do(vec.tensor_tensor(need[:], need[:], cnt[:], ALU.subtract))
            do(vec.tensor_scalar(e, f32(K), cand[:], None, ALU.is_equal))
            do(vec.tensor_tensor_scan(o, e, e, 0.0, ALU.add, ALU.max))
            do(vec.scalar_tensor_tensor(out=e, in0=o, scalar=need[:], in1=e, op0=ALU.is_le, op1=ALU.mult))
            do(vec.scalar_tensor_tensor(out=e, in0=f32(K), scalar=u[:], in1=e, op0=ALU.is_ge, op1=ALU.add))
            do(vec.scalar_tensor_tensor(out=e, in0=Hn, scalar=th1[:], in1=e, op0=ALU.is_ge, op1=ALU.add))
            do(vec.scalar_tensor_tensor(out=e[:, tail], in0=iota[:, tail], scalar=lim, in1=e[:, tail],
                                        op0=ALU.is_lt, op1=ALU.mult))
            do(vec.tensor_scalar(f32(K), e, -1.0, MASKED, ALU.add, ALU.mult))
            do(vec.scalar_tensor_tensor(out=f32(K), in0=iota[:, 0:n], scalar=qpos, in1=f32(K),
                                        op0=ALU.subtract, op1=ALU.min))
            do(vec.tensor_scalar(o[:, tail], iota[:, tail], -1.0, qpos, ALU.mult, ALU.add))
            vec.tensor_tensor(f32(K[:, tail]), o[:, tail], f32(K[:, tail]), ALU.min).then_inc(done[p], 1)

        vec.wait_ge(iota_made, 1)
        query_tiles(lambda j: steps.turns(2, 2 * SELECT_STEPS), select)

    c.selected = (stored[0], 16 * (DT // 2 + 1)), (stored[1], 16 * (DT // 2))
    return Programs(sync=sync, vector=vector, gpsimd=gpsimd)


def token_tiles(eng, body, turns=None):
    with (turns or eng.Fori(0, DT // 2)) as i:
        body(i * 2, i, 0)
        body(i * 2 + 1, i, 1)
    body(DT, DT // 2, 0)


GMLP_STEPS = 7 + RSQRT_STEPS + 4


def stage_gmlp(c):
    nc, sb = c.nc, Sbuf(c.nc, c.first)
    w_raw = sb("g_wraw", [P, 4, P])
    wT = sb("g_wT", [P, 4, P])
    bias = sb("g_bias", [P, 4, P])
    ln_g = sb("g_lng", [P, BW])
    ln_b = sb("g_lnb", [P, BW])
    vT, uT, zT, vn, ob = ([sb(f"g_{n}{p}", [P, 4, P]) for p in range(2)] for n in ("vT", "uT", "zT", "vn", "ob"))
    stats = sb("g_stats", [P, 6])
    mv = sb("g_mv", [P, 2])
    mean = sb("g_mean", [P, 1])
    var, rstd, tmp = sb("g_var", [P, 1]), sb("g_rstd", [P, 1]), sb("g_tmp", [P, 1])
    S = c.sem
    own_steps = S("g_steps")
    const_full = S("g_const_full")
    w_turned = S("g_w_turned")
    w_ready = S("g_w_ready")
    v_full = [S(f"g_v_full{p}") for p in range(2)]
    uz_full = [S(f"g_uz_full{p}") for p in range(2)]
    turned = [S(f"g_turned{p}") for p in range(2)]
    normed = [S(f"g_normed{p}") for p in range(2)]
    mixed = [S(f"g_mixed{p}") for p in range(2)]
    gated = [S(f"g_gated{p}") for p in range(2)]
    stored = [S(f"g_stored{p}") for p in range(2)]
    v_stored = S("g_v_stored")
    slot = lambda s, t: c.T_dram[s:s + 4, :, at(t)].rearrange("s q t -> q s t")

    def sync(sp):
        for s, n in c.T_stored + list(c.selected):
            sp.wait_ge(s, n)
        sp.dma_start(w_raw[:], c.I["gmlp_ws"].rearrange("(g i) j -> i g j", g=4)).then_inc(const_full, 16)
        sp.dma_start(bias[:].rearrange("q g i -> q (g i)"),
                     c.I["gmlp_bs"].rearrange("g i -> (g i)").partition_broadcast(P)).then_inc(const_full, 16)
        sp.dma_start(ln_g[:], c.I["gmlp_ln_g"].partition_broadcast(P)).then_inc(const_full, 16)
        sp.dma_start(ln_b[:], c.I["gmlp_ln_b"].partition_broadcast(P)).then_inc(const_full, 16)

        def load(t, m, p):
            sp.wait_ge(turned[p], m)
            sp.dma_start(vT[p][:, :, 0:real(t)], slot(S_GV, t)).then_inc(v_full[p], 16)
            sp.wait_ge(gated[p], m)
            sp.dma_start(uT[p][:, :, 0:real(t)], slot(S_U, t)).then_inc(uz_full[p], 16)
            sp.dma_start(zT[p][:, :, 0:real(t)], slot(S_ZB, t)).then_inc(uz_full[p], 16)
        token_tiles(sp, load)

    def tensor(pe):
        pe.wait_ge(const_full, 64)
        for g in range(4):
            last = pe.transpose(c.psum[:, 4, g * P:(g + 1) * P], w_raw[:, g, :], c.ident[:])
        last.then_inc(w_turned, 1)
        pe.wait_ge(w_ready, 2)

        def turn(t, m, p):
            pe.wait_ge(v_full[p], m * 16 + 16)
            pe.wait_ge(normed[p], m)
            for s in range(4):
                last = pe.transpose(c.psum[:, p, s * P:(s + 1) * P], vT[p][:, s, :], c.ident[:])
            last.then_inc(turned[p], 1)

        def mix(t, m, p):
            rows = DEC if isinstance(t, int) else P
            pe.wait_ge(normed[p], m + 1)
            pe.wait_ge(gated[p], m)
            for g in range(4):
                last = pe.matmul(c.psum[:, 2 + p, g * P:(g + 1) * P], vn[p][0:rows, g, :], wT[0:rows, g, :],
                                 start=True, stop=True)
            last.then_inc(mixed[p], 1)

        turn(0, 0, 0)
        with pe.Fori(0, DT // 2) as i:
            turn(i * 2 + 1, i, 1)
            mix(i * 2, i, 0)
            turn(i * 2 + 2, i + 1, 0)
            mix(i * 2 + 1, i, 1)
        mix(DT, DT // 2, 0)

    def vector(vec):
        steps = Steps(vec, own_steps)
        do = steps.did_wait
        vec.wait_ge(w_turned, 1)
        vec.tensor_copy(wT[:], c.psum[:, 4, :].rearrange("q (g i) -> q g i", g=4)).then_inc(w_ready, 1)
        vec.wait_ge(w_ready, 1)
        vec.memset(wT[CHUNK:P, :, 0:CHUNK], 0.0).then_inc(w_ready, 1)

        def norm(t, m, p):
            vec.wait_ge(turned[p], m + 1)
            vec.wait_ge(mixed[p], m)
            v = c.psum[:, p, :]
            do(vec.bn_stats(stats[:], v))
            do(vec.tensor_tensor(mv[:], stats[:, 1:3], stats[:, 4:6], ALU.add))
            do(vec.tensor_tensor(tmp[:], stats[:, 1:2], stats[:, 4:5], ALU.subtract))
            do(vec.tensor_scalar(mean[:], mv[:, 0:1], 0.5, None, ALU.mult))
            do(vec.scalar_tensor_tensor(out=tmp[:], in0=tmp[:], scalar=0.25, in1=tmp[:], op0=ALU.mult, op1=ALU.mult))
            do(vec.scalar_tensor_tensor(out=var[:], in0=mv[:, 1:2], scalar=1.0 / BW, in1=tmp[:], op0=ALU.mult, op1=ALU.add))
            do(vec.tensor_scalar(var[:], var[:], EPS, None, ALU.add))
            rsqrt(steps, rstd[:], var[:], tmp[:])
            flat = vn[p][:].rearrange("q g n -> q (g n)")
            do(vec.tensor_scalar(flat, v, mean[:], rstd[:], ALU.subtract, ALU.mult))
            do(vec.tensor_tensor(flat, flat, ln_g[:], ALU.mult))
            vec.tensor_tensor(flat, flat, ln_b[:], ALU.add).then_inc(normed[p], 1)

        def gate(t, m, p):
            vec.wait_ge(mixed[p], m + 1)
            vec.wait_ge(uz_full[p], m * 32 + 32)
            vec.wait_ge(stored[p], m * 16)
            mix = c.psum[:, 2 + p, :].rearrange("q (g i) -> q g i", g=4)
            do(vec.tensor_tensor(ob[p][:], mix, bias[:], ALU.add))
            do(vec.tensor_tensor(ob[p][:], ob[p][:], uT[p][:], ALU.mult))
            vec.tensor_tensor(ob[p][:], ob[p][:], zT[p][:], ALU.mult).then_inc(gated[p], 1)

        vec.wait_ge(const_full, 64)
        norm(0, 0, 0)
        with steps.turns(DT // 2, 2 * GMLP_STEPS) as i:
            norm(i * 2 + 1, i, 1)
            gate(i * 2, i, 0)
            norm(i * 2 + 2, i + 1, 0)
            gate(i * 2 + 1, i, 1)
        gate(DT, DT // 2, 0)

    def scalar(act):
        def store(t, m, p):
            act.wait_ge(gated[p], m + 1)
            act.dma_start(c.B_dram[1, :, :, at(t)].rearrange("s q t -> q s t"), ob[p][:, :, 0:real(t)]).then_inc(stored[p], 16)
        token_tiles(act, store)
        act.wait_ge(normed[0], DT // 2 + 1)
        act.dma_start(c.O["gmlp_sample"], vn[0][0:DEC].rearrange("q g n -> q (g n)")).then_inc(v_stored, 16)
        act.wait_ge(v_stored, 16)
        for p in range(2):
            act.wait_ge(stored[p], 16 * (DT // 2 + 1 - p))

    c.gmlp_done = (stored[0], 16 * (DT // 2 + 1)), (stored[1], 16 * (DT // 2)), (v_stored, 16)
    return Programs(sync=sync, scalar=scalar, vector=vector, tensor=tensor)


LEFT = CONV - 1
EXT = LEFT + SEQ + LEFT + DEC
CONVS = EXT - LEFT
DEC_AT = SEQ + LEFT
CW_SPAN = CONVS // 5
CONV_SPANS = [(a, CW_SPAN) for a in range(0, CONVS, CW_SPAN)]
UNITS = 4 * len(CONV_SPANS)


def stage_convolve(c):
    nc, sb = c.nc, Sbuf(c.nc, c.after_project)
    W = CW_SPAN + LEFT
    parT = c.parT
    stateT = sb("v_stateT", [P, 4, LEFT])
    zeros, ones = sb("v_zeros", [P, LEFT]), sb("v_ones", [P, LEFT])
    start = sb.at
    a, g, y, taps = (sb(f"v_{n}", [P, w]) for n, w in (("a", W), ("g", W), ("y", CW_SPAN), ("taps", CONV + 1)))
    RING = 4
    product = [sb(f"v_product{r}", [P, CW_SPAN]) for r in range(RING)]
    c.after_convolve = sb.at
    under = Sbuf(nc, start)
    par = under("v_par", [P, CW])
    state = under("v_state", [LEFT, CW])
    assert under.at <= sb.at
    S = c.sem
    par_full, par_turned, par_ready, fills_made = (S("v_" + n) for n in ("par_full", "par_turned", "par_ready", "fills_made"))
    full, unit_full, glu_done, y_started, made, added, moved, unit_moved = (
        S("v_" + n) for n in ("full", "unit_full", "glu_done", "y_started", "made", "added", "moved", "unit_moved"))

    counts = {"full": 0, "moved": 0}

    def load(sp, u):
        s, x = u // 5, u % 5
        if u == 0:
            sp.wait_ge(par_ready, 2)
            sp.wait_ge(fills_made, 2)
            for sem, n in c.conv_inputs_stored:
                sp.wait_ge(sem, n)
        first = x * CW_SPAN - LEFT
        n = SEQ - first
        pieces = [(taps[:], parT[:, s, 0:CONV + 1])]
        for buf, slot, between in ((a, S_GA, stateT[:, s, :]), (g, S_GG, ones[:])):
            src = c.T_dram[slot + s]
            if x == 0:
                pieces += [(buf[:, 0:LEFT], zeros[:]), (buf[:, LEFT:W], src[:, 0:CW_SPAN])]
            elif x < 4:
                pieces += [(buf[:], src[:, first:first + W])]
            else:
                pieces += [(buf[:, 0:n], src[:, first:SEQ]), (buf[:, n:n + LEFT], between), (buf[:, n + LEFT:W], src[:, SEQ:TOK])]
        for dst, src in pieces:
            sp.dma_start(dst, src).then_inc(full, 16)
            counts["full"] += 16
        sp.wait_ge(full, counts["full"])
        sp.sem_inc(unit_full, 1)

    def move(sp, u):
        s, x = u // 5, u % 5
        pieces = [(c.Y_dram[s, :, x * CW_SPAN:(x + 1) * CW_SPAN], y[:])]
        if x == 4:
            pieces += [(c.tailsT[:, s, 0, :], a[:, W - DEC - 2 * LEFT:W - DEC - LEFT]), (c.tailsT[:, s, 1, :], a[:, W - LEFT:W])]
        sp.wait_ge(added, (u + 1) * (CONV - 1))
        for dst, src in pieces:
            sp.dma_start(dst, src).then_inc(moved, 16)
            counts["moved"] += 16
        sp.wait_ge(moved, counts["moved"])
        sp.sem_inc(unit_moved, 1)

    def make_taps(act, u, half, b):
        for k in range(16 * half + 4 * b, min(16 * half + 4 * b + 4, CONV)) if b < 4 else ():
            if k == 0:
                act.wait_ge(glu_done, u + 1)
                act.wait_ge(unit_moved, u)
                act.activation(y[:], a[:, 0:CW_SPAN], ACT.Identity, scale=taps[:, 0:1], bias=taps[:, CONV:CONV + 1]
                               ).then_inc(y_started, 1)
                continue
            n = k - 1
            if n >= RING:
                act.wait_ge(added, u * (CONV - 1) + (n - RING + 1))
            act.activation(product[n % RING][:], a[:, k:k + CW_SPAN], ACT.Identity, scale=taps[:, k:k + 1]).then_inc(made, 1)

    def add_taps(pool, u, half):
        if half == 0:
            pool.wait_ge(unit_full, u + 1)
            pool.tensor_tensor(a[:], a[:], g[:], ALU.mult).then_inc(glu_done, 1)
        for k in range(max(1, 16 * half), min(16 * half + 16, CONV)):
            n = k - 1
            if n == 0:
                pool.wait_ge(y_started, u + 1)
            else:
                pool.wait_ge(added, u * (CONV - 1) + n)
            pool.wait_ge(made, u * (CONV - 1) + (n + 1))
            pool.tensor_tensor(y[:], y[:], product[n % RING][:], ALU.add).then_inc(added, 1)

    def sync(sp):
        for s, n in c.scores_stored:
            sp.wait_ge(s, n)
        for row, name, n in ((0, "conv_w", CONV), (CONV, "conv_b", 1), (CONV + 1, "conv_ln_g", 1), (CONV + 2, "conv_ln_b", 1)):
            sp.dma_start(par[row:row + n, :], c.I[name]).then_inc(par_full, 16)
        sp.dma_start(state[:], c.I["state_conv"]).then_inc(par_full, 16)

    def tensor(pe):
        for s, n in c.scores_stored:
            pe.wait_ge(s, n)
        pe.wait_ge(par_full, 80)
        for s in range(4):
            pe.transpose(c.psum[:, 5, s * 64:s * 64 + CONV + 3], par[0:CONV + 3, s * P:(s + 1) * P], c.ident[0:CONV + 3, 0:CONV + 3])
            last = pe.transpose(c.psum[:, 6, s * 64:s * 64 + LEFT], state[:, s * P:(s + 1) * P], c.ident[0:LEFT, 0:LEFT])
        last.then_inc(par_turned, 1)

    def scalar(act):
        for s, n in c.scores_stored:
            act.wait_ge(s, n)
        act.wait_ge(par_turned, 1)
        act.copy(parT[:], c.psum[:, 5, 0:256].rearrange("q (s n) -> q s n", s=4)[:, :, 0:CONV + 3]).then_inc(par_ready, 1)
        act.copy(stateT[:], c.psum[:, 6, 0:256].rearrange("q (s n) -> q s n", s=4)[:, :, 0:LEFT]).then_inc(par_ready, 1)

    def gpsimd(pool):
        for s, n in c.scores_stored:
            pool.wait_ge(s, n)
        pool.memset(zeros[:], 0.0).then_inc(fills_made, 1)
        pool.memset(ones[:], 1.0).then_inc(fills_made, 1)

    c.make_taps, c.add_taps, c.load_unit, c.move_unit = make_taps, add_taps, load, move
    return Programs(sync=sync, scalar=scalar, tensor=tensor, gpsimd=gpsimd)


def stage_swish(c):
    nc, sb = c.nc, Sbuf(c.nc, c.first)
    ones = sb("w_ones", [P, P])
    gate = [sb(f"w_gate{p}", [P, TOK]) for p in range(2)]
    y = [sb(f"w_y{s}", [P, CONVS]) for s in range(4)]
    rstd = sb("w_rstd", [P, CONVS])
    tmp = sb("w_tmp", [P, CONVS])
    tails = sb("w_tails", [LEFT, 2, CW])
    S = c.sem
    own_steps = S("w_steps")
    y_full, ones_made, tail_turned, tail_copied = S("w_y_full"), S("w_ones"), S("w_tail_turned"), S("w_tail_copied")
    tails_stored = S("w_tails_stored")
    summed, var_summed, centred, rooted, normed = S("w_summed"), S("w_var_summed"), S("w_centred"), S("w_rooted"), S("w_normed")
    acted, gated, stored = S("w_acted"), S("w_gated"), S("w_stored")
    z_full = [S(f"w_z_full{p}") for p in range(2)]
    squared = S("w_squared")

    def sync(sp):
        for s, n in c.gmlp_done:
            sp.wait_ge(s, n)
        for s in range(4):
            sp.dma_start(y[s][:], c.Y_dram[s]).then_inc(y_full, 16)
        for s in range(4):
            if s >= 2:
                sp.wait_ge(gated, s - 1)
            sp.dma_start(gate[s % 2][:], c.T_dram[S_ZC + s]).then_inc(z_full[s % 2], 16)
        for s in range(4):
            sp.wait_ge(gated, s + 1)
            sp.dma_start(c.B_dram[2, s, :, 0:SEQ], y[s][:, 0:SEQ]).then_inc(stored, 16)
            sp.dma_start(c.B_dram[2, s, :, SEQ:SEQ + DEC], y[s][:, DEC_AT:CONVS]).then_inc(stored, 16)
        sp.wait_ge(tail_copied, 4)
        sp.dma_start(c.O["conv_prompt"], tails[:, 0, :]).then_inc(tails_stored, 16)
        sp.dma_start(c.O["conv_sample"], tails[:, 1, :]).then_inc(tails_stored, 16)
        sp.wait_ge(tails_stored, 32)
        sp.wait_ge(stored, 128)

    def tensor(pe):
        for s, n in c.gmlp_done:
            pe.wait_ge(s, n)
        for s in range(4):
            if s >= 1:
                pe.wait_ge(tail_copied, s)
            for u in range(2):
                last = pe.transpose(c.psum[0:LEFT, 2, u * P:(u + 1) * P], c.tailsT[:, s, u, :], c.ident[:])
            last.then_inc(tail_turned, 1)
        pe.wait_ge(ones_made, 1)
        pe.wait_ge(y_full, 64)
        for b, (a, w) in enumerate(CONV_SPANS):
            for s in range(4):
                last = pe.matmul(c.psum[:, 3 + b, 0:w], ones[:], y[s][:, a:a + w], start=(s == 0), stop=(s == 3))
        last.then_inc(summed, 1)
        pe.wait_ge(centred, 4)
        for s in range(4):
            pe.wait_ge(squared, s + 1)
            for b, (a, w) in enumerate(CONV_SPANS):
                last = pe.matmul(c.psum[:, 3 + b, 0:w], ones[:], tmp[:, a:a + w], start=(s == 0), stop=(s == 3))
            last.then_inc(var_summed, 1)

    def vector(vec):
        steps = Steps(vec, own_steps)
        do = steps.did_wait
        for s, n in c.gmlp_done:
            vec.wait_ge(s, n)
        vec.memset(ones[:], 1.0 / CW).then_inc(ones_made, 1)
        for s in range(4):
            vec.wait_ge(tail_turned, s + 1)
            vec.tensor_copy(tails[:, :, s * P:(s + 1) * P], c.psum[0:LEFT, 2, 0:2 * P].rearrange("q (u n) -> q u n", u=2)
                            ).then_inc(tail_copied, 1)
        mean = c.psum[:, 3:8, 0:CW_SPAN]
        spans = lambda x: x[:].rearrange("q (b n) -> q b n", b=len(CONV_SPANS))
        vec.wait_ge(summed, 1)
        for s in range(4):
            vec.tensor_tensor(spans(y[s]), spans(y[s]), mean, ALU.subtract).then_inc(centred, 1)
        vec.wait_ge(centred, 4)
        for s in range(4):
            if s:
                vec.wait_ge(var_summed, s)
            vec.tensor_tensor(tmp[:], y[s][:], y[s][:], ALU.mult).then_inc(squared, 1)
        vec.wait_ge(var_summed, 4)
        do(vec.tensor_scalar(spans(tmp), mean, EPS, None, ALU.add))
        vec.sem_inc(rooted, 1)
        vec.wait_ge(acted, 1)
        do(vec.reciprocal(rstd[:], rstd[:]))
        do(vec.tensor_tensor(tmp[:], tmp[:], rstd[:], ALU.mult))
        do(vec.tensor_tensor(tmp[:], tmp[:], rstd[:], ALU.mult))
        do(vec.tensor_scalar(tmp[:], tmp[:], -0.5, 1.5, ALU.mult, ALU.add))
        do(vec.tensor_tensor(rstd[:], rstd[:], tmp[:], ALU.mult))
        for s in range(4):
            vec.tensor_tensor(y[s][:], y[s][:], rstd[:], ALU.mult).then_inc(normed, 1)
        for s in range(4):
            vec.wait_ge(acted, s + 2)
            vec.wait_ge(z_full[s % 2], (s // 2 + 1) * 16)
            z = gate[s % 2]
            do(vec.tensor_tensor(y[s][:, 0:SEQ], y[s][:, 0:SEQ], z[:, 0:SEQ], ALU.mult))
            vec.tensor_tensor(y[s][:, DEC_AT:CONVS], y[s][:, DEC_AT:CONVS], z[:, SEQ:SEQ + DEC], ALU.mult).then_inc(gated, 1)

    def scalar(act):
        act.wait_ge(rooted, 1)
        act.activation(rstd[:], tmp[:], ACT.Sqrt).then_inc(acted, 1)
        for s in range(4):
            act.wait_ge(normed, s + 1)
            act.activation(y[s][:], y[s][:], ACT.Silu, scale=c.parT[:, s, CONV + 1:CONV + 2],
                           bias=c.parT[:, s, CONV + 2:CONV + 3]).then_inc(acted, 1)

    c.conv_done = (stored, 128), (tails_stored, 32)
    return Programs(sync=sync, scalar=scalar, vector=vector, tensor=tensor)


LOWEST = -3.0e38


class Actions:

    def __init__(self, start=None, turned=None, unit=None, head=None, weigh=None, all_weighed=None, finish=None):
        nothing = lambda *_: None
        self.start, self.turned, self.unit, self.head = start or nothing, turned or nothing, unit or nothing, head or nothing
        self.weigh, self.all_weighed, self.finish = weigh or nothing, all_weighed or nothing, finish or nothing


def stage_attend(c):
    nc, sb = c.nc, Sbuf(c.nc, c.first)
    NS, NV = PAST + DEC, PAST // P + 1
    QK, PT, PO, PB = 2, (2, 3, 4), (5, 6), 7
    RING = len(PT)
    k_hi, k_lo, ks_hi, ks_lo = ([sb(f"a_{n}{g}", [P, w], F32R) for g in range(KVH)]
                                for n, w in (("khi", SEQ), ("klo", SEQ), ("kshi", NS), ("kslo", NS)))
    v_p = sb("a_vp", [P, DT, KVH, P], F32R)
    v_s = sb("a_vs", [P, NV, KVH, P], F32R)
    nd = [sb(f"a_nd{p}", [P, SEQ]) for p in range(2)]
    L = [sb(f"a_l{h}", [P, SEQ]) for h in range(HEADS)]
    q2 = [sb(f"a_q2{p}", [P, HEADS, P]) for p in range(2)]
    qs = [sb(f"a_qs{p}", [P, HEADS, P], F32R) for p in range(2)]
    scale = sb("a_scale", [P, HEADS])
    pT_hi = [sb(f"a_pthi{u}", [P, 512], F32R) for u in range(RING)]
    pT_lo = [sb(f"a_ptlo{u}", [P, 512], F32R) for u in range(RING)]
    za = [sb(f"a_za{p}", [HD, HEADS, P]) for p in range(2)]
    oa = [sb(f"a_oa{p}", [HD, HEADS, P]) for p in range(2)]
    o_low = sb("a_olow", [HD, 512])
    peaks = sb("a_peaks", [P, HEADS, 4])
    peak = sb("a_peak", [P, HEADS])
    nbias = sb("a_nbias", [P, HEADS])
    sums = sb("a_sums", [P, HEADS])
    rs = sb("a_rs", [P, HEADS])
    S = c.sem
    own_steps = S("a_steps")
    k_full, v_full, cache_full, vs_full, cache_turned = (S("a_" + n) for n in ("k_full", "v_full", "cache_full", "vs_full", "cache_turned"))
    operands = S("a_operands")
    scale_set = S("a_scale_set")
    nd_full, q_full, za_full, q_scaled, q_hi, q_ready, o_done, stored = (
        [S(f"a_{n}{p}") for p in range(2)] for n in ("nd_full", "q_full", "za_full", "q_scaled", "q_hi", "q_ready", "o_done", "stored"))
    qk_full = S("a_qk_full")
    qk_read = [S(f"a_qk_read{b}") for b in range(QK)]
    po_read = [S(f"a_po_read{g}") for g in range(KVH)]
    mark = S("a_mark")
    head_ready, exp_done, rs_ready, pt_full, pt_hi, bc_full, o_copied = (
        S("a_" + n) for n in ("head_ready", "exp_done", "rs_ready", "pt_full", "pt_hi", "bc_full", "o_copied"))
    pt_lo = [S(f"a_pt_lo{u}") for u in range(RING)]
    pv_used = [S(f"a_pv_used{u}") for u in range(RING)]
    kraw = [L[g] for g in range(KVH)]
    vraw = L[2][:].rearrange("q (t n) -> q t n", t=DT)
    vsraw = L[3][:, 0:NV * P].rearrange("q (t n) -> q t n", t=NV)
    cache = L[4][:].rearrange("q (t g u d) -> q t g u d", t=PAST // P, g=KVH, u=2)
    new_k = [L[5 + g][:, 0:DEC] for g in range(KVH)]

    per_tile = [HEADS * len(pieces(keys)) for _, keys in CLASSES]
    before = [4 * sum(per_tile[:j]) for j in range(len(CLASSES))]
    ktiles = [-(-keys // P) for _, keys in CLASSES]
    kt_before = [4 * 2 * sum(ktiles[:j]) for j in range(len(CLASSES))]

    def turn_of(j, m):
        return m - CLASSES[j][0] // 2 if not isinstance(m, int) else 0

    def slot_uses(units, j, slot, slots):
        uses = [len(range(slot, n, slots)) for n in units]
        return uses[j], 2 * sum(uses[:j])

    def score_units(j, t, m, p, g):
        i = turn_of(j, m)
        spans = pieces(CLASSES[j][1])
        for n, (r, (s, (a, w))) in enumerate((r, s) for r in range(4) for s in enumerate(spans)):
            u = before[j] + p * per_tile[j] + g * 4 * len(spans) + n
            x = (2 * p + g) * 4 * len(spans) + n
            turns, before_it = slot_uses([2 * n for n in per_tile], j, x % QK, QK)
            yield 4 * g + r, s, a, w, x % QK, i * turns + (before_it + x // QK), i * (2 * per_tile[j]) + u

    def key_units(j, t, m, p, g):
        i = turn_of(j, m)
        for kt in range(ktiles[j]):
            x = (2 * p + g) * ktiles[j] + kt
            turns, before_it = slot_uses([4 * n for n in ktiles], j, x % RING, RING)
            yield (kt, min(P, CLASSES[j][1] - kt * P), x % RING, i * turns + (before_it + x // RING),
                   i * (4 * ktiles[j]) + (kt_before[j] + x))

    def together(e, weighed, scored, before):
        units = list(score_units(*scored)) if scored else []
        keys = list(key_units(*weighed)) if weighed else []
        if weighed:
            e.start(weighed, keys, before is None)
        issued, heads = 0, []
        for x in range(max(1, len(keys))):
            if weighed:
                e.turned(weighed, keys, x)
            if x == 0 and before:
                e.finish(before)
            for h, at_x in heads:
                if at_x + 2 <= x:
                    e.head(scored, h)
            heads = [(h, at_x) for h, at_x in heads if at_x + 2 > x]
            for unit in units[issued:-(-len(units) * 4 * (x + 1) // (3 * len(keys))) if weighed else None]:
                e.unit(scored, unit)
                issued += 1
                if issued % (len(units) // 4) == 0:
                    heads.append((unit[0], x))
            if weighed:
                e.weigh(weighed, keys, x, scored)
        for h, _ in heads:
            e.head(scored, h)
        if weighed:
            e.all_weighed(weighed, keys)

    def group_order(e, loop):
        def chain(groups):
            together(e, None, groups[0], None)
            for n, group in enumerate(groups):
                together(e, group, groups[n + 1] if n + 1 < len(groups) else None, groups[n - 1] if n else None)
            e.finish(groups[-1])

        for j, (t0, _) in enumerate(CLASSES):
            if t0 == DT:
                chain([(j, DT, DT // 2, 0, g) for g in range(KVH)])
                continue
            with loop(j) as i:
                chain([(j, i * 2 + (t0 + p), i + t0 // 2, p, g) for p in range(2) for g in range(KVH)])

    def by_head(slot):
        return c.T_dram[slot:slot + 4].rearrange("s q t -> (s q) t").rearrange("(h d) t -> d h t", d=HD)

    def sync(sp):
        for g in range(KVH):
            doubled(sp, kraw[g], c.T_dram[S_K, g * HD:(g + 1) * HD, 0:SEQ], k_full)
            doubled(sp, new_k[g], c.T_dram[S_K, g * HD:(g + 1) * HD, SEQ:SEQ + DEC], k_full)
            for u in range(2):
                sp.dma_start(cache[:, :, g, u, :],
                             c.I["cache_k"].rearrange("(t q g) d -> q t g d", q=P, g=KVH)[:, :, g, :]).then_inc(cache_full, 16)
        sp.dma_start(vraw, c.O["v_prompt"].rearrange("(t q g) d -> q t (g d)", q=P, g=KVH)).then_inc(v_full, 16)
        sp.dma_start(vsraw[:, 0:NV - 1, :], c.I["cache_v"].rearrange("(t q g) d -> q t (g d)", q=P, g=KVH)).then_inc(vs_full, 16)
        sp.dma_start(vsraw[0:DEC, NV - 1, :], c.O["v_sample"].rearrange("(q g) d -> q (g d)", g=KVH)).then_inc(vs_full, 16)

        def load(j, t, m, p):
            keys = CLASSES[j][1]
            sp.wait_ge(q_ready[p], m)
            doubled(sp, q2[p][:, :, 0:real(t)], by_head(S_Q)[:, :, at(t)], q_full[p])
            sp.wait_ge(o_done[p], m * 2)
            sp.dma_start(nd[p][:, 0:keys], c.ND_dram[at(t, 1), :, 0:keys].rearrange("a q n -> q (a n)")).then_inc(nd_full[p], 16)
            sp.dma_start(za[p][:, :, 0:real(t)], by_head(S_ZA)[:, :, at(t)]).then_inc(za_full[p], 16)
        query_tiles(lambda j: sp.Fori(0, 2), load)

    def gpsimd(pool):
        for h in range(HEADS):
            pool.memset(scale[:, h:h + 1], HD ** -0.5 * 2.0 ** (h + 1)).then_inc(scale_set, 1)
        pool.wait_ge(scale_set, HEADS)
        scales = scale[:].unsqueeze(2).to_broadcast([P, HEADS, P])
        zeros = c.zero[:].unsqueeze(1).to_broadcast([P, HEADS, P])

        def split(t, m, p):
            pool.wait_ge(q_ready[1 - p], m + p)
            pool.wait_ge(q_full[p], m * 32 + 32)
            pool.wait_ge(o_done[p], m * 2)
            pool.tensor_tensor(q2[p][:], q2[p][:], scales, ALU.mult).then_inc(q_scaled[p], 1)
            pool.wait_ge(q_scaled[p], m + 1)
            pool.tensor_tensor(qs[p][:], q2[p][:], zeros, ALU.add).then_inc(q_hi[p], 1)
            pool.wait_ge(q_hi[p], m + 1)
            pool.tensor_tensor(qs[p][HD:P], q2[p][HD:P], f32(qs[p][HD:P]), ALU.subtract).then_inc(q_ready[p], 1)

        def store(t, m, p):
            pool.wait_ge(o_done[p], m * 2 + 2)
            pool.dma_start(c.B_dram[0].rearrange("s q t -> (s q) t").rearrange("(h d) t -> d h t", d=HD)[:, :, at(t)],
                           oa[p][:, :, 0:real(t)]).then_inc(stored[p], 16)

        split(0, 0, 0)
        with pool.Fori(0, DT // 2) as i:
            split(i * 2 + 1, i, 1)
            store(i * 2, i, 0)
            split(i * 2 + 2, i + 1, 0)
            store(i * 2 + 1, i, 1)
        store(DT, DT // 2, 0)
        for p in range(2):
            pool.wait_ge(stored[p], 16 * (DT // 2 + 1 - p))

    cacheT = [c.psum[:, 2 * g:2 * g + 2, :].rearrange("q b n -> q (b n)") for g in range(KVH)]

    def tensor(pe):
        pe.wait_ge(cache_full, 64)
        for g in range(KVH):
            for t in range(PAST // P):
                last = pe.transpose(cacheT[g][:, t * P:(t + 1) * P], cache[:, t, g].rearrange("q u d -> q (u d)"), c.ident[:])
        last.then_inc(cache_turned, 1)
        pe.wait_ge(operands, 1)

        def turn(group, kt, w, u, nu, n):
            g = group[4]
            pe.wait_ge(pt_lo[u], nu)
            for r in range(4):
                last = pe.transpose(c.psum[0:w, PT[u], r * P:(r + 1) * P], L[4 * g + r][:, kt * P:kt * P + w], c.ident[:])
            last.then_inc(pt_full, 1)

        def start(group, keys, first):
            if first:
                turn_head(group)

        def turn_head(group, wanted=range(RING - 1)):
            j, t, m, p, g = group
            for x, key in enumerate(key_units(*group)):
                if x in wanted:
                    if x == 0:
                        pe.wait_ge(exp_done, t * 8 + (4 * g + 4))
                    turn(group, *key)

        def turned(group, keys, x):
            if x + RING - 1 < len(keys):
                turn(group, *keys[x + RING - 1])

        def unit(group, unit):
            (j, t, m, p, g), (h, s, a, w, b, nb, n) = group, unit
            hi, lo = (ks_hi[g], ks_lo[g]) if t is DT else (k_hi[g], k_lo[g])
            if s == 0 and h == 4 * g:
                pe.wait_ge(q_ready[p], m + 1)
            pe.wait_ge(qk_read[b], nb)
            pe.matmul(c.psum[:, b, 0:w], qs[p][:, h, :], hi[:, a:a + w], start=True, stop=False)
            pe.matmul(c.psum[:, b, 0:w], qs[p][:, h, :], lo[:, a:a + w], start=False, stop=True).then_inc(qk_full, 1)

        def weigh(group, keys, x, following):
            j, t, m, p, g = group
            kt, w, u, nu, n = keys[x]
            v = v_s if t is DT else v_p
            pe.wait_ge(pt_lo[u], nu + 1)
            if x == 0:
                pe.wait_ge(po_read[g], t)
            pe.matmul(c.psum[:, PO[g], :], v[0:w, kt, g, :], pT_hi[u][0:w, :], start=(x == 0), stop=False)
            pe.matmul(c.psum[:, PO[g], :], v[0:w, kt, g, :], pT_lo[u][0:w, :], start=False,
                      stop=(x == len(keys) - 1)).then_inc(pv_used[u], 1)
            if following:
                turn_head(following, [x + RING - 1 - len(keys)])

        def all_weighed(group, keys):
            j, t, m, p, g = group
            pe.wait_ge(rs_ready, t * 2 + (g + 1))
            if g:
                pe.wait_ge(o_done[p], m * 2 + 1)
            else:
                pe.wait_ge(o_done[1 - p], (m + p) * 2)
            for r in range(4):
                last = pe.matmul(c.psum[:, PB, r * P:(r + 1) * P], rs[:, 4 * g + r:4 * g + r + 1].to_broadcast([P, P]),
                                 c.ident[:], start=True, stop=True)
            last.then_inc(bc_full, 1)
        group_order(Actions(start=start, turned=turned, unit=unit, weigh=weigh, all_weighed=all_weighed),
                    lambda j: pe.Fori(0, 2))

    def scalar(act):
        def head(group, h):
            j, t, m, p, g = group
            n = CLASSES[j][1]
            act.wait_ge(head_ready, t * 8 + (h + 1))
            act.activation(L[h][:, 0:n], L[h][:, 0:n], ACT.Exp, bias=nbias[:, h:h + 1],
                           accum_out=sums[:, h:h + 1]).then_inc(exp_done, 1)

        def turned(group, keys, x):
            kt, w, u, nu, n = keys[x]
            act.wait_ge(pt_full, n + 1)
            act.wait_ge(pv_used[u], nu)
            act.activation(pT_hi[u][0:w, :], c.psum[0:w, PT[u], :], ACT.Copy).then_inc(pt_hi, 1)

        def finish(group):
            j, t, m, p, g = group
            kt, w, u, nu, n = list(key_units(*group))[-1]
            act.wait_ge(pv_used[u], nu + 1)
            act.wait_ge(po_read[1 - g], t + g)
            act.activation(o_low[:], c.psum[HD:P, PO[g], :], ACT.Copy).then_inc(o_copied, 1)
        group_order(Actions(head=head, turned=turned, finish=finish), lambda j: act.Fori(0, 2))

    def vector(vec):
        steps = Steps(vec, own_steps)
        do = steps.did_wait
        vec.wait_ge(k_full, 128)
        vec.wait_ge(cache_turned, 1)
        for g in range(KVH):
            for hi, lo, src in ((k_hi[g][:], k_lo[g][:], kraw[g][:]),
                                (ks_hi[g][:, 0:PAST], ks_lo[g][:, 0:PAST], cacheT[g]),
                                (ks_hi[g][:, PAST:], ks_lo[g][:, PAST:], new_k[g])):
                do(vec.tensor_copy(hi, src))
                do(vec.tensor_tensor(lo, src, f32(hi), ALU.subtract))
        for full, n, v, raw, rows, tiles in ((v_full, 16, v_p, vraw, P, slice(0, DT)),
                                             (vs_full, 32, v_s, vsraw, P, slice(0, NV - 1)),
                                             (vs_full, 32, v_s, vsraw, DEC, slice(NV - 1, NV))):
            vec.wait_ge(full, n)
            for g in range(KVH):
                src, dst = raw[0:rows, tiles, g * HD:(g + 1) * HD], v[0:rows, tiles, g, :]
                do(vec.tensor_copy(dst[:, :, 0:HD], src))
                do(vec.tensor_tensor(dst[:, :, HD:P], src, f32(dst[:, :, 0:HD]), ALU.subtract))
        vec.sem_inc(operands, 1)

        def unit(group, unit):
            (j, t, m, p, g), (h, s, a, w, b, nb, n) = group, unit
            spans = len(pieces(CLASSES[j][1]))
            if s == 0 and h == 0:
                vec.wait_ge(nd_full[p], m * 16 + 16)
            vec.wait_ge(qk_full, n + 1)
            vec.sem_inc(mark, 1)
            vec.tensor_tensor_reduce(out=L[h][:, a:a + w], in0=nd[p][:, a:a + w], in1=c.psum[:, b, 0:w],
                                     scale=2.0 ** -(h + 1), scalar=LOWEST, op0=ALU.add, op1=ALU.max,
                                     accum_out=peaks[:, h, s:s + 1]).then_inc(qk_read[b], 1)
            if s == spans - 1:
                vec.wait_ge(qk_read[b], nb + 1)
                top = peaks[:, h, 0:1]
                if spans > 1:
                    top = peak[:, h:h + 1]
                    do(vec.tensor_reduce(top, peaks[:, h, 0:spans], AX.X, ALU.max))
                vec.tensor_scalar(nbias[:, h:h + 1], top, -1.0, None, ALU.mult).then_inc(head_ready, 1)

        def start(group, keys, first):
            j, t, m, p, g = group
            vec.wait_ge(exp_done, t * 8 + (4 * g + 4))
            vec.reciprocal(rs[:, 4 * g:4 * g + 4], sums[:, 4 * g:4 * g + 4]).then_inc(rs_ready, 1)

        def turned(group, keys, x):
            kt, w, u, nu, n = keys[x]
            vec.wait_ge(pt_hi, n + 1)
            vec.tensor_tensor(pT_lo[u][0:w, :], c.psum[0:w, PT[u], :], f32(pT_hi[u][0:w, :]), ALU.subtract
                              ).then_inc(pt_lo[u], 1)

        def finish(group):
            j, t, m, p, g = group
            o = oa[p][:, 4 * g:4 * g + 4, :].rearrange("d h t -> d (h t)")
            vec.wait_ge(o_copied, t * 2 + (g + 1))
            vec.wait_ge(bc_full, t * 2 + (g + 1))
            vec.wait_ge(stored[p], m * 16)
            vec.wait_ge(za_full[p], m * 16 + 16)
            vec.tensor_tensor(o, c.psum[0:HD, PO[g], :], o_low[:], ALU.add).then_inc(po_read[g], 1)
            vec.wait_ge(po_read[g], t + 1)
            do(vec.tensor_tensor(o, c.psum[0:HD, PB, :], o, ALU.mult))
            vec.tensor_tensor(o, o, za[p][:, 4 * g:4 * g + 4, :].rearrange("d h t -> d (h t)"), ALU.mult).then_inc(o_done[p], 1)

        def per_turn(j):
            return 2 * (8 * (len(pieces(CLASSES[j][1])) > 1) + 2)
        group_order(Actions(start=start, turned=turned, unit=unit, finish=finish), lambda j: steps.turns(2, per_turn(j)))

    c.attended = (stored[0], 16 * (DT // 2 + 1)), (stored[1], 16 * (DT // 2))
    return Programs(sync=sync, scalar=scalar, vector=vector, tensor=tensor, gpsimd=gpsimd)


def split_weights(c, prefix, plan, buffers):
    raw, n_raw = buffers, len(buffers)
    full, hi_done, lo_done = [], [], []
    for r in range(n_raw):
        full.append(c.sem(f"{prefix}w_full{r}"))
        hi_done.append(c.sem(f"{prefix}w_hi{r}"))
        lo_done.append(c.sem(f"{prefix}w_lo{r}"))

    def scalar(act):
        def load(n):
            act.wait_ge(lo_done[n % n_raw], n // n_raw)
            act.dma_start(raw[n % n_raw][:], plan[n][0]).then_inc(full[n % n_raw], 16)

        for n in range(n_raw):
            load(n)
        for n, (src, hi, lo) in enumerate(plan):
            r = n % n_raw
            act.wait_ge(full[r], 16 * (n // n_raw + 1))
            act.copy(hi, raw[r][:]).then_inc(hi_done[r], 1)
            if n and n - 1 + n_raw < len(plan):
                load(n - 1 + n_raw)

    def vector(vec):
        for n, (src, hi, lo) in enumerate(plan):
            r = n % n_raw
            vec.wait_ge(hi_done[r], n // n_raw + 1)
            vec.tensor_tensor(lo, raw[r][:], f32(hi), ALU.subtract).then_inc(lo_done[r], 1)

    def ready(eng, n=len(plan)):
        for r in range(n_raw):
            eng.wait_ge(lo_done[r], len(range(r, n, n_raw)))
    return Programs(scalar=scalar, vector=vector, ready=ready)


def stage_merge(c):
    nc, sb = c.nc, Sbuf(c.nc, c.first)
    names = ("w_branch_a", "w_branch_b", "w_branch_c")
    w_hi = sb("m_whi", [P, 3, 4, D], F32R)
    w_lo = sb("m_wlo", [P, 3, 4, D], F32R)
    weights = split_weights(c, "m_", [(c.I[names[b]][k * P:(k + 1) * P, :], w_hi[:, b, k, :], w_lo[:, b, k, :])
                                      for b in range(3) for k in range(4)], [sb(f"m_raw{r}", [P, D]) for r in range(4)])
    o_raw = [sb(f"m_oraw{x}", [P, 4, SPAN]) for x in range(2)]
    o_hi = [sb(f"m_ohi{x}", [P, 4, SPAN], F32R) for x in range(2)]
    o_lo = [sb(f"m_olo{x}", [P, 4, SPAN], F32R) for x in range(2)]
    gate = [sb(f"m_gate{x}", [P, 2, SPAN]) for x in range(4)]
    merged = sb("m_merged", [P, 8, SPAN])
    tmp = [sb(f"m_tmp{x}", [P, SPAN]) for x in range(2)]
    S = c.sem
    o_full = [S(f"m_o_full{x}") for x in range(2)]
    o_hi_done = [S(f"m_o_hi{x}") for x in range(2)]
    o_lo_done = [S(f"m_o_lo{x}") for x in range(2)]
    g_full = [S(f"m_g_full{x}") for x in range(4)]
    product, gated, added, stored = S("m_product"), S("m_gated"), S("m_added"), S("m_stored")

    def spans(eng, body):
        with eng.Fori(0, len(SPANS) // 2) as i:
            for y in range(2):
                for b in range(3):
                    body(i, y, b, bass.ds(i * 2 * SPAN + y * SPAN, SPAN))
        for b in range(3):
            body(2, 0, b, slice(4 * SPAN, TOK))

    def wait(eng, sem, i, y, n, per=24):
        n += per * y
        eng.wait_ge(sem, i * (2 * per) + (n if isinstance(i, int) else max(0, n)))

    def buffer(i, y, b):
        return (3 * y + b) % 2, i * 3 + (3 * y + b) // 2

    def sync(sp):
        for s, n in c.attended:
            sp.wait_ge(s, n)

        def load(i, y, b, cols):
            u, nu = buffer(i, y, b)
            sp.wait_ge(o_lo_done[u], nu)
            sp.dma_start(o_raw[u][:], c.B_dram[b, :, :, cols].rearrange("s q t -> q s t")).then_inc(o_full[u], 16)
            for n in range(4):
                wait(sp, gated, i, y, 8 * b - 8 + 2 * n + 2)
                slot = S_G + 8 * b + 2 * n
                sp.dma_start(gate[n][:], c.T_dram[slot:slot + 2, :, cols].rearrange("s q t -> q s t")).then_inc(g_full[n], 16)
        spans(sp, load)

    def gpsimd(pool):
        def split(i, y, b, cols):
            u, nu = buffer(i, y, b)
            zeros = c.zero[:].unsqueeze(1).to_broadcast([P, 4, SPAN])
            pool.wait_ge(o_full[u], nu * 16 + 16)
            wait(pool, product, i, y, 8 * b - 8)
            pool.tensor_tensor(o_hi[u][:], o_raw[u][:], zeros, ALU.add).then_inc(o_hi_done[u], 1)
            pool.wait_ge(o_hi_done[u], nu + 1)
            pool.tensor_tensor(o_lo[u][:], o_raw[u][:], f32(o_hi[u][:]), ALU.subtract
                               ).then_inc(o_lo_done[u], 1)
        for s, n in c.attended:
            pool.wait_ge(s, n)
        spans(pool, split)

    def tensor(pe):
        weights.ready(pe)

        def products(i, y, b, cols):
            u, nu = buffer(i, y, b)
            pe.wait_ge(o_lo_done[u], nu + 1)
            for n in range(8):
                wait(pe, gated, i, y, 8 * b - 8 + n + 1)
                for k in range(4):
                    for q, (wt, o) in enumerate(((w_hi, o_hi), (w_hi, o_lo), (w_lo, o_hi))):
                        last = pe.matmul(c.psum[:, n, 0:SPAN], wt[:, b, k, n * P:(n + 1) * P], o[u][:, k, :],
                                         start=(k == 0 and q == 0), stop=(k == 3 and q == 2))
                last.then_inc(product, 1)
        spans(pe, products)

    def scalar(act):
        for s, n in c.attended:
            act.wait_ge(s, n)
        weights.scalar(act)

        def store(i, y, b, cols):
            if b == 2:
                act.wait_ge(added, i * 32 + (16 * y + 16))
                act.dma_start(c.M_dram[:, :, cols].rearrange("s q t -> q s t"), merged[:]).then_inc(stored, 16)
        spans(act, store)
        act.wait_ge(stored, 80)

    def vector(vec):
        weights.vector(vec)

        def gating(i, y, b, cols):
            for n in range(8):
                wait(vec, product, i, y, 8 * b + n + 1)
                if n % 2 == 0:
                    vec.wait_ge(g_full[n // 2], i * 96 + (48 * y + 16 * b + 16))
                dst = merged[:, n, :] if b == 0 else tmp[n % 2][:, :]
                if b == 0:
                    vec.wait_ge(stored, i * 32 + 16 * y)
                else:
                    vec.wait_ge(added, i * 32 + (16 * y + 8 * (b - 1) + n))
                vec.tensor_tensor(dst, c.psum[:, n, 0:SPAN], gate[n // 2][:, n % 2, :], ALU.mult).then_inc(gated, 1)
                if b:
                    wait(vec, gated, i, y, 8 * b + n + 1)
                    vec.tensor_tensor(merged[:, n, :], merged[:, n, :], dst, ALU.add).then_inc(added, 1)
        spans(vec, gating)

    c.merged_stored = ((stored, 80),)
    return Programs(sync=sync, scalar=scalar, vector=vector, tensor=tensor, gpsimd=gpsimd)


FINISH_STEPS = 2 * (1 + RSQRT_STEPS) + 1


def stage_finish(c):
    nc, sb = c.nc, Sbuf(c.nc, c.first)
    KP = 2
    wo_hi, wo_lo, wg_hi, wg_lo = (sb(f"f_{n}", [P, KD, D], F32R) for n in ("wohi", "wolo", "wghi", "wglo"))
    wp_hi, wp_lo = (sb(f"f_{n}", [P, KP, D], F32R) for n in ("wphi", "wplo"))
    ple_g = sb("f_pleg", [P, D])
    fin_g = sb("f_fing", [P, D])
    m_raw = sb("f_mraw", [P, KD, P])
    m_hi = sb("f_mhi", [P, KD, P], F32R)
    m_lo = sb("f_mlo", [P, KD, P], F32R)
    x = [sb(f"f_x{p}", [P, D]) for p in range(2)]
    pl = [sb(f"f_p{p}", [P, KP * P]) for p in range(2)]
    p_hi = sb("f_phi", [P, KP, P], F32R)
    p_lo = sb("f_plo", [P, KP, P], F32R)
    xn = sb("f_xn", [P, D])
    y = [sb(f"f_y{p}", [P, D]) for p in range(2)]
    h_hi = sb("f_hhi", [P, KD, P], F32R)
    h_lo = sb("f_hlo", [P, KD, P], F32R)
    sig = sb("f_sig", [P, D])
    weights = split_weights(c, "f_", [(c.I[name][k * P:(k + 1) * P, :], hi[:, k, :], lo[:, k, :])
                                      for name, hi, lo, ks in (("w_out", wo_hi, wo_lo, KD), ("w_ple_gate", wg_hi, wg_lo, KD),
                                                               ("w_ple", wp_hi, wp_lo, KP)) for k in range(ks)],
                            y + [sb("f_raw", [P, D])])
    ssq = sb("f_ssq", [P, 2])
    var, rstd, tmp = sb("f_var", [P, 1]), sb("f_rstd", [P, 1]), sb("f_tmp", [P, 1])
    S = c.sem
    own_steps = S("f_steps")
    g_full = S("f_g_full")
    m_full, m_hi_done, m_lo_done = S("f_m_full"), S("f_m_hi"), S("f_m_lo")
    x_full = [S(f"f_x_full{p}") for p in range(2)]
    p_full = [S(f"f_p_full{p}") for p in range(2)]
    out_product, added, squared, normed, x_turned, h_hi_done, h_lo_done, p_turned = (
        S("f_" + n) for n in ("out_product", "added", "squared", "normed", "x_turned", "h_hi", "h_lo", "p_turned"))
    p_hi_done, p_lo_done, ple_product, gate_product, sig_done, summed, last_squared = (
        S("f_" + n) for n in ("p_hi", "p_lo", "ple_product", "gate_product", "sig_done", "summed", "last_squared"))
    finished = [S(f"f_finished{p}") for p in range(2)]
    stored = [S(f"f_stored{p}") for p in range(2)]
    pair = lambda b: c.psum[:, b:b + 2, :].rearrange("q b n -> q (b n)")
    b_out, b_turn, b_gate, b_ple = 0, 2, 4, 6
    xT = pair(b_turn).rearrange("q (k n) -> q k n", k=KD)
    pT = pair(b_turn)[:, 0:KP * P].rearrange("q (k n) -> q k n", k=KP)

    def pipelined(loop, body):
        body(0, 0, 0, True, False)
        with loop as i:
            body(i * 2 + 1, i, 1, False, False)
            body(i * 2 + 2, i + 1, 0, False, False)
        body(DT - 1, DT // 2 - 1, 1, False, False)
        body(DT, DT // 2, 0, False, True)

    def sync(sp):
        for s, n in c.merged_stored:
            sp.wait_ge(s, n)
        sp.dma_start(ple_g[:], c.I["ple_norm_g"].partition_broadcast(P)).then_inc(g_full, 16)
        sp.dma_start(fin_g[:], c.I["final_norm_g"].partition_broadcast(P)).then_inc(g_full, 16)

        def load(t, m, p):
            last = isinstance(t, int)
            n, rows, r = ("sample", slice(0, DEC), DEC) if last else ("prompt", at(t), P)
            sp.wait_ge(m_lo_done, t)
            sp.dma_start(m_raw[:, :, 0:r], c.M_dram[:, :, at(t)].rearrange("s q t -> q s t")).then_inc(m_full, 16)
            sp.wait_ge(finished[p], m)
            sp.dma_start(x[p][0:r, :], c.I["x_" + n][rows, :]).then_inc(x_full[p], 16)
            sp.dma_start(pl[p][0:r, :], c.I["p_" + n][rows, :]).then_inc(p_full[p], 16)
        token_tiles(sp, load)

    def tensor(pe):
        def three(bank, lhs_hi, lhs_lo, w_hi, w_lo, ks):
            for half in range(2):
                cols = slice(half * 512, half * 512 + 512)
                for k in range(ks):
                    for q, (a, w) in enumerate(((lhs_hi, w_hi), (lhs_lo, w_hi), (lhs_hi, w_lo))):
                        last = pe.matmul(pair(bank)[:, cols], a[:, k, :], w[:, k, cols],
                                         start=(k == 0 and q == 0), stop=(k == ks - 1 and q == 2))
            return last

        def out(t):
            pe.wait_ge(m_lo_done, t + 1)
            if not (isinstance(t, int) and t == 0):
                pe.wait_ge(added, t)
            three(b_out, m_hi, m_lo, wo_hi, wo_lo, KD).then_inc(out_product, 1)

        def body(t, m, p, first, last):
            pe.wait_ge(normed, t + 1)
            if not first:
                pe.wait_ge(p_lo_done, t)
            for k in range(KD):
                ins = pe.transpose(xT[:, k, :], xn[:, k * P:(k + 1) * P], c.ident[:])
            ins.then_inc(x_turned, 1)
            if not last:
                out(t + 1)
            pe.wait_ge(p_full[p], m * 16 + 16)
            pe.wait_ge(h_lo_done, t + 1)
            for k in range(KP):
                ins = pe.transpose(pT[:, k, :], pl[p][:, k * P:(k + 1) * P], c.ident[:])
            ins.then_inc(p_turned, 1)
            if first:
                weights.ready(pe)
            else:
                pe.wait_ge(sig_done, t)
            three(b_gate, h_hi, h_lo, wg_hi, wg_lo, KD).then_inc(gate_product, 1)
            pe.wait_ge(p_lo_done, t + 1)
            if not first:
                pe.wait_ge(summed, t)
            three(b_ple, p_hi, p_lo, wp_hi, wp_lo, KP).then_inc(ple_product, 1)

        weights.ready(pe, KD)
        out(0)
        pipelined(pe.Fori(0, DT // 2 - 1), body)

    def gpsimd(pool):
        zeros = c.zero[:].unsqueeze(1).to_broadcast([P, KD, P])

        def split(t, m, p):
            pool.wait_ge(m_full, t * 16 + 16)
            pool.wait_ge(out_product, t)
            pool.tensor_tensor(m_hi[:], m_raw[:], zeros, ALU.add).then_inc(m_hi_done, 1)
            pool.wait_ge(m_hi_done, t + 1)
            pool.tensor_tensor(m_lo[:], m_raw[:], f32(m_hi[:]), ALU.subtract).then_inc(m_lo_done, 1)
        for s, n in c.merged_stored:
            pool.wait_ge(s, n)
        token_tiles(pool, split)

    def scalar(act):
        for s, n in c.merged_stored:
            act.wait_ge(s, n)
        weights.scalar(act)

        def square(t, p, first=False):
            act.wait_ge(added, t + 1)
            if not first:
                act.wait_ge(summed, t - 1)
            act.activation(sig[:], x[p][:], ACT.Square, accum_out=ssq[:, 0:1]).then_inc(squared, 1)

        def last_square(t, m, p):
            act.wait_ge(summed, t + 1)
            act.wait_ge(stored[p], m * 16)
            act.activation(y[p][:], x[p][:], ACT.Square, accum_out=ssq[:, 1:2]).then_inc(last_squared, 1)

        def store(t, m, p, last=False):
            act.wait_ge(finished[p], m + 1)
            act.dma_start(c.O["y_sample"] if last else c.O["y_prompt"][at(t), :], y[p][0:DEC if last else P, :]
                          ).then_inc(stored[p], 16)

        def body(t, m, p, first, last):
            act.wait_ge(x_turned, t + 1)
            if not first:
                act.wait_ge(gate_product, t)
            act.copy(h_hi[:], xT).then_inc(h_hi_done, 1)
            if not first:
                last_square(t - 1, m - 1 + p, 1 - p)
            act.wait_ge(p_turned, t + 1)
            if not first:
                act.wait_ge(ple_product, t)
            act.copy(p_hi[:], pT).then_inc(p_hi_done, 1)
            if not last:
                square(t + 1, 1 - p, first)
            if not first:
                store(t - 1, m - 1 + p, 1 - p)
            act.wait_ge(squared, t + (1 if last else 2))
            act.wait_ge(gate_product, t + 1)
            act.activation(sig[:], pair(b_gate), ACT.Sigmoid).then_inc(sig_done, 1)

        square(0, 0, True)
        pipelined(act.Fori(0, DT // 2 - 1), body)
        last_square(DT, DT // 2, 0)
        store(DT, DT // 2, 0, True)
        for p in range(2):
            act.wait_ge(stored[p], 16 * len(range(p, TILES, 2)))

    def vector(vec):
        weights.vector(vec)
        steps = Steps(vec, own_steps)
        do = steps.did_wait

        def root(col):
            do(vec.tensor_scalar(var[:], ssq[:, col:col + 1], 1.0 / D, EPS, ALU.mult, ALU.add))
            rsqrt(steps, rstd[:], var[:], tmp[:])

        def add(t, m, p):
            vec.wait_ge(out_product, t + 1)
            vec.wait_ge(x_full[p], m * 16 + 16)
            vec.tensor_tensor(x[p][:], x[p][:], pair(b_out), ALU.add).then_inc(added, 1)

        def norm(t, p):
            vec.wait_ge(squared, t + 1)
            root(0)
            vec.wait_ge(x_turned, t)
            vec.scalar_tensor_tensor(out=xn[:], in0=x[p][:], scalar=rstd[:], in1=ple_g[:], op0=ALU.mult,
                                     op1=ALU.mult).then_inc(normed, 1)
            vec.wait_ge(normed, t + 1)

        def end(t, p):
            vec.wait_ge(sig_done, t + 1)
            vec.wait_ge(ple_product, t + 1)
            do(vec.tensor_tensor(sig[:], pair(b_ple), sig[:], ALU.mult))
            vec.tensor_tensor(x[p][:], x[p][:], sig[:], ALU.add).then_inc(summed, 1)
            vec.wait_ge(last_squared, t + 1)
            root(1)
            vec.scalar_tensor_tensor(out=y[p][:], in0=x[p][:], scalar=rstd[:], in1=fin_g[:], op0=ALU.mult,
                                     op1=ALU.mult).then_inc(finished[p], 1)

        def body(t, m, p, first, last):
            vec.wait_ge(h_hi_done, t + 1)
            vec.tensor_tensor(h_lo[:], xT, f32(h_hi[:]), ALU.subtract).then_inc(h_lo_done, 1)
            if not first:
                end(t - 1, 1 - p)
            if not last:
                add(t + 1, m + p, 1 - p)
            vec.wait_ge(p_hi_done, t + 1)
            vec.tensor_tensor(p_lo[:], pT, f32(p_hi[:]), ALU.subtract).then_inc(p_lo_done, 1)
            if not first:
                vec.wait_ge(finished[1 - p], m + p)
            if not last:
                norm(t + 1, 1 - p)

        vec.wait_ge(g_full, 32)
        add(0, 0, 0)
        norm(0, 0)
        pipelined(steps.turns(DT // 2 - 1, 2 * FINISH_STEPS), body)
        end(DT, 0)

    return Programs(sync=sync, scalar=scalar, vector=vector, tensor=tensor, gpsimd=gpsimd)


def stage_turnover(c):
    arrived, cleared = c.lasting_sem("arrived"), c.lasting_sem("cleared")
    numbers = c.release_semaphores()

    def report(eng):
        eng.drain().then_inc(arrived, 1)
        eng.wait_ge(cleared, 1)

    def gpsimd(pool):
        pool.drain().then_inc(arrived, 1)
        pool.wait_ge(arrived, 5)
        pool.sem_clear(numbers).then_inc(cleared, 1)
        pool.wait_ge(cleared, 1)

    return Programs(sync=report, scalar=report, vector=report, tensor=report, gpsimd=gpsimd)


OUTPUTS = [("y_prompt", (1, SEQ, D)), ("y_sample", (1, DEC, D)),
           ("k_prompt", (1, 1, SEQ, KVH, HD)), ("v_prompt", (1, 1, SEQ, KVH, HD)),
           ("ik_prompt", (1, 1, SEQ, HD)), ("conv_prompt", (1, 1, CONV - 1, CW)),
           ("k_sample", (1, 1, DEC, KVH, HD)), ("v_sample", (1, 1, DEC, KVH, HD)),
           ("ik_sample", (1, 1, DEC, HD)), ("conv_sample", (1, 1, CONV - 1, CW)),
           ("gmlp_sample", (1, 1, DEC, BW))]


def build(nc, I, O, stages=None):
    with ExitStack() as ctx:
        c = Shared()
        c.nc, c.I, c.O = nc, I, O
        c.lasting_sem = lambda name: ctx.enter_context(nc.semaphore(name))
        passing, held = ExitStack(), []

        def sem(name):
            held.append(passing.enter_context(nc.semaphore(name)))
            return held[-1]

        def release_semaphores():
            numbers = sorted(s.num for s in held)
            held.clear()
            passing.close()
            assert numbers == list(range(numbers[0], numbers[-1] + 1)), numbers
            return range(numbers[0], numbers[-1] + 1)

        c.sem, c.release_semaphores = sem, release_semaphores
        c.psum = ctx.enter_context(nc.psum_tensor("psum", [P, 8, 512], F32))
        sb = Sbuf(nc, (nc.sbuf_base + 31) // 32 * 32)
        c.ident = sb("ident", [P, P])
        c.zero = sb("zero", [P, 1])
        c.ident_ready = c.lasting_sem("ident_ready")
        c.aw = sb("aw", [P, TILES, IH])
        c.sg = sb("sg", [P, TILES, IH])
        c.weights_ready = c.lasting_sem("weights_ready")
        c.w_full = c.lasting_sem("j_w_full")
        c.natural_stored = [c.lasting_sem(f"t_stored{p}") for p in range(2)]
        c.acc_stored = [c.lasting_sem(f"i_stored{p}") for p in range(2)]
        c.qpos = sb("qpos", [P, TILES])
        c.lim = sb("lim", [P, TILES])
        c.parT = sb("parT", [P, 4, CONV + 3])
        c.tailsT = sb("tailsT", [P, 4, 2, LEFT])
        c.first = sb.at
        c.hT_hi = sb("hT_hi", [P, KD, TOK], F32R)
        c.hT_lo = sb("hT_lo", [P, KD, TOK], F32R)
        c.after_hT = sb.at
        c.Y_dram = nc.dram_tensor("Y_dram", [4, P, CONVS], F32).ap()
        c.ND_dram = nc.dram_tensor("ND_dram", [TILES, P, SEQ], F32).ap()
        c.M_dram = nc.dram_tensor("M_dram", [KD, P, TOK], F32).ap()
        c.B_dram = nc.dram_tensor("B_dram", [3, 4, P, TOK], F32).ap()
        c.SC_dram = nc.dram_tensor("SC_dram", [TILES, P, SEQ], F32).ap()
        c.T_dram = nc.dram_tensor("T_dram", [SLOTS, P, TOK], F32).ap()
        identity_step = c.lasting_sem("identity_step")
        parts = [s(c) for s in (stages or STAGES)]
        block = ctx.enter_context(nc.Block())

        @block.sync
        def _(sp):
            for s in parts:
                if s.sync:
                    s.sync(sp)

        @block.gpsimd
        def _(pool):
            pool.memset(c.zero[:], 0.0).then_inc(identity_step, 1)
            pool.memset(c.ident[:], 0.0).then_inc(identity_step, 1)
            pool.wait_ge(identity_step, 2)
            pool.affine_select(out=c.ident[:], in_=c.ident[:], compare_op=ALU.not_equal, fill=1.0, base=0,
                               pattern=[[-1, P]], channel_multiplier=1).then_inc(c.ident_ready, 1)
            for s in parts:
                if s.gpsimd:
                    s.gpsimd(pool)

        @block.scalar
        def _(act):
            for s in parts:
                if s.scalar:
                    s.scalar(act)

        @block.vector
        def _(vec):
            for s in parts:
                if s.vector:
                    s.vector(vec)

        @block.tensor
        def _(pe):
            for s in parts:
                if s.tensor:
                    s.tensor(pe)
        passing.close()


STAGES = [stage_constants, stage_norm, stage_project_first, stage_natural, stage_scores, stage_convolve, stage_select, stage_project_rest, stage_gmlp, stage_swish, stage_turnover, stage_attend, stage_merge, stage_finish]


def kernel(**inputs):
    import concourse.bacc as bacc
    from concourse.bass_utils import run_bass_kernel_spmd

    nc = bacc.Bacc("TRN2", target_bir_lowering=False, num_devices=1)
    arrays, I, O = {}, {}, {}
    for name, value in inputs.items():
        a = np.ascontiguousarray(value)
        arrays[f"in_{name}"] = a = a.reshape(-1, a.shape[-1])
        I[name] = nc.dram_tensor(f"in_{name}", a.shape, F32, kind="ExternalInput").ap()
    for name, shape in OUTPUTS:
        O[name] = nc.dram_tensor(f"out_{name}", (int(np.prod(shape[:-1])), shape[-1]), F32,
                                 kind="ExternalOutput").ap()
    build(nc, I, O)
    r = run_bass_kernel_spmd(nc, [arrays], core_ids=[0])
    return tuple(np.asarray(r.results[0][f"out_{name}"]).reshape(shape) for name, shape in OUTPUTS)
```

```python
from contextlib import ExitStack, contextmanager

import numpy as np

import concourse.bass as bass
import concourse.mybir as mybir
from concourse.alu_op_type import AluOpType as ALU

F32 = mybir.dt.float32
F32R = mybir.dt.float32r
BF16 = mybir.dt.bfloat16
I32 = mybir.dt.int32
I16 = mybir.dt.int16
U16 = mybir.dt.uint16
U8 = mybir.dt.uint8
ACT = mybir.ActivationFunctionType
AX = mybir.AxisListType

P = 128
D = 1024
KD = D // P
SEQ, DEC, PAST = 2048, 32, 1024
TILES = SEQ // P + 1
DT = TILES - 1
TOK = SEQ + DEC
SPAN = 416
EPS = 1e-6
HD = 64
HEADS, KVH, IH = 8, 2, 4
AW = HEADS * HD
BW = CW = 512
CONV = 31
CHUNK = 64
TOPK = 256
IN_COLS = 7748
IDX_W_SCALE = (IH * HD) ** -0.5
C_Q, C_K, C_V, C_IQ, C_IK, C_IW, C_ZA, C_U, C_GV, C_ZB, C_GA, C_GG, C_ZC, C_G = (
    0, 512, 640, 768, 1024, 1088, 1092, 1604, 2116, 2628, 3140, 3652, 4164, 4676)
SPANS = [(a, SPAN) for a in range(0, TOK, SPAN)]
assert TOK == len(SPANS) * SPAN


class Shared:
    pass


class Programs:

    def __init__(self, sync=None, gpsimd=None, scalar=None, vector=None, tensor=None, ready=None):
        self.sync, self.gpsimd, self.scalar, self.vector, self.tensor = sync, gpsimd, scalar, vector, tensor
        self.ready = ready


class Steps:

    def __init__(self, eng, sem):
        self.eng, self.sem, self.base, self.n = eng, sem, 0, 0

    def did(self, ins):
        ins.then_inc(self.sem, 1)
        self.n += 1

    def wait(self):
        self.eng.wait_ge(self.sem, self.base + self.n)

    def did_wait(self, ins):
        self.did(ins)
        self.wait()

    @contextmanager
    def turns(self, count, per):
        start = self.base + self.n
        with self.eng.Fori(0, count) as i:
            self.base, self.n = i * per + start, 0
            yield i
            assert self.n == per, (self.n, per)
        self.base, self.n = start + count * per, 0


RSQRT_STEPS = 11


def rsqrt(steps, y, v, t):
    vec = steps.eng
    yi, ti = y.bitcast(I32), t.bitcast(I32)
    steps.did_wait(vec.tensor_scalar(ti, v.bitcast(I32), 1, None, ALU.logical_shift_right))
    steps.did_wait(vec.tensor_scalar(yi, ti, -1.0, 1597463007.0, ALU.mult, ALU.add))
    for _ in range(3):
        if y.shape[-1] == 1:
            steps.did_wait(vec.scalar_tensor_tensor(out=t, in0=y, scalar=v, in1=y, op0=ALU.mult, op1=ALU.mult))
        else:
            steps.did_wait(vec.tensor_tensor(t, y, y, ALU.mult))
            steps.did_wait(vec.tensor_tensor(t, t, v, ALU.mult))
        steps.did_wait(vec.tensor_scalar(t, t, -0.5, 1.5, ALU.mult, ALU.add))
        steps.did_wait(vec.tensor_tensor(y, y, t, ALU.mult))


class Sbuf:

    def __init__(self, nc, at):
        self.nc, self.at = nc, at

    def __call__(self, name, shape, dt=F32):
        size = {F32: 4, F32R: 4, I32: 4, BF16: 2, I16: 2, U16: 2, U8: 1}[dt]
        n = int(np.prod(shape[1:])) * size
        n = (n + 31) // 32 * 32
        t = self.nc.alloc_sbuf_tensor_at(name, shape, dt, offset=self.at)
        self.at += n
        assert self.at <= self.nc.sbuf_usable_end, (name, self.at)
        return t


def f32(ap):
    return ap.bitcast(F32)


def at(t, n=P):
    return slice(t * n, min((t + 1) * n, TOK)) if isinstance(t, int) else bass.ds(t * n, n)


def real(t):
    return DEC if isinstance(t, int) and t == DT else P



def stage_norm(c):
    nc, sb = c.nc, Sbuf(c.nc, c.after_hT)
    x_in = [sb(f"n_x{p}", [P, D]) for p in range(2)]
    xn = [sb(f"n_xn{p}", [P, D]) for p in range(2)]
    junk = [sb(f"n_junk{p}", [P, D]) for p in range(2)]
    g_rows = sb("n_g", [P, D])
    ssq = [sb(f"n_ssq{p}", [P, 1]) for p in range(2)]
    var = sb("n_var", [P, 1])
    rstd = sb("n_rstd", [P, 1])
    tmp = sb("n_tmp", [P, 1])
    S = c.sem
    own_steps = S("n_steps")
    g_full = S("n_g_full")
    x_full = [S(f"n_x_full{p}") for p in range(2)]
    squared = [S(f"n_squared{p}") for p in range(2)]
    normed = [S(f"n_normed{p}") for p in range(2)]
    turned = [S(f"n_turned{p}") for p in range(2)]
    hi_done = [S(f"n_hi{p}") for p in range(2)]
    lo_done = [S(f"n_lo{p}") for p in range(2)]
    half = DT // 2
    pT = [c.psum[:, 2 * p:2 * p + 2, :].rearrange("q b (k t) -> q (b k) t", k=4) for p in range(2)]

    def cols(i, p):
        return bass.ds((i * 2 + p) * P, P) if not isinstance(i, int) else at(2 * i + p)

    def width(i, p):
        return real(2 * i + p) if isinstance(i, int) else P

    def sync(sp):
        sp.dma_start(g_rows[:], c.I["norm_g"].partition_broadcast(P)).then_inc(g_full, 16)

        def load(i, p, last=False):
            sp.wait_ge(squared[p], i)
            sp.wait_ge(normed[p], i)
            if last:
                sp.dma_start(x_in[p][0:DEC, :], c.I["x_sample"]).then_inc(x_full[p], 16)
            else:
                sp.dma_start(x_in[p][:], c.I["x_prompt"][cols(i, p), :]).then_inc(x_full[p], 16)

        with sp.Fori(0, half) as i:
            load(i, 0)
            load(i, 1)
        load(half, 0, last=True)

    def scalar(act):
        def square(i, p):
            act.wait_ge(x_full[p], i * 16 + 16)
            act.wait_ge(normed[p], i)
            act.wait_ge(squared[p], i)
            act.activation(junk[p][:], x_in[p][:], ACT.Square, accum_out=ssq[p][:]).then_inc(squared[p], 1)

        def high(i, p):
            act.wait_ge(turned[p], i + 1)
            act.copy(c.hT_hi[:, :, cols(i, p)], pT[p][:, :, 0:width(i, p)]).then_inc(hi_done[p], 1)

        square(0, 0)
        with act.Fori(0, half) as i:
            square(i, 1)
            high(i, 0)
            square(i + 1, 0)
            high(i, 1)
        high(half, 0)

    def vector(vec):
        steps = Steps(vec, own_steps)

        def norm(i, p):
            vec.wait_ge(squared[p], i + 1)
            vec.wait_ge(turned[p], i)
            steps.did_wait(vec.tensor_scalar(var[:], ssq[p][:], 1.0 / D, EPS, ALU.mult, ALU.add))
            rsqrt(steps, rstd[:], var[:], tmp[:])
            vec.scalar_tensor_tensor(out=xn[p][:], in0=x_in[p][:], scalar=rstd[:], in1=g_rows[:],
                                     op0=ALU.mult, op1=ALU.mult).then_inc(normed[p], 1)

        def low(i, p):
            vec.wait_ge(turned[p], i + 1)
            vec.wait_ge(hi_done[p], i + 1)
            vec.tensor_tensor(c.hT_lo[:, :, cols(i, p)], pT[p][:, :, 0:width(i, p)], f32(c.hT_hi[:, :, cols(i, p)]),
                              ALU.subtract).then_inc(lo_done[p], 1)

        per = 1 + RSQRT_STEPS
        vec.wait_ge(g_full, 16)
        norm(0, 0)
        with steps.turns(half, 2 * per) as i:
            norm(i, 1)
            low(i, 0)
            norm(i + 1, 0)
            low(i, 1)
        low(half, 0)

    def tensor(pe):
        def turn(i, p):
            pe.wait_ge(normed[p], i + 1)
            pe.wait_ge(hi_done[p], i)
            pe.wait_ge(lo_done[p], i)
            for k in range(KD):
                last = pe.transpose(pT[p][:, k, :], xn[p][:, k * P:(k + 1) * P], c.ident[:])
            last.then_inc(turned[p], 1)

        pe.wait_ge(c.ident_ready, 1)
        with pe.Fori(0, half) as i:
            turn(i, 0)
            turn(i, 1)
        turn(half, 0)

    c.hT_done = (hi_done[0], half + 1), (hi_done[1], half), (lo_done[0], half + 1), (lo_done[1], half)
    return Programs(sync=sync, scalar=scalar, vector=vector, tensor=tensor)


S_IKW, S_Q, S_K, S_V, S_IQ, S_GA, S_U, S_GV, S_ZA, S_ZB, S_ZC, S_GG, S_G = (
    0, 1, 5, 6, 7, 9, 13, 17, 21, 25, 29, 33, 37)
FIRST_RUNS = [(C_IK, 1, S_IKW, "copy"), (C_Q, 8, S_Q, "copy")]
REST_RUNS = [(C_GA, 4, S_GA, "copy"), (C_GG, 4, S_GG, "sigmoid"), (C_ZC, 4, S_ZC, "silu"), (C_G, 24, S_G, "sigmoid"),
             (C_ZA, 4, S_ZA, "silu"), (C_U, 8, S_U, "gelu"), (C_ZB, 4, S_ZB, "silu")]
CONV_RUN = 3
JUMP_RUN = 4
SLOTS = sum(r[1] for r in FIRST_RUNS + REST_RUNS)
FUNC = {"copy": ACT.Copy, "gelu": ACT.Gelu, "silu": ACT.Silu, "sigmoid": ACT.Sigmoid}
OUTS = 3
FIRST_JOBS = sum(r[1] for r in FIRST_RUNS)
FIRST_OF_CONV = FIRST_JOBS + sum(r[1] for r in REST_RUNS[:CONV_RUN])
FIRST_OF_JUMP = FIRST_JOBS + sum(r[1] for r in REST_RUNS[:JUMP_RUN])


def project(c, first):
    nc = c.nc
    if first:
        sb = Sbuf(nc, c.after_hT)
        c.w_raw = sb("j_w", [P, KD, P])
        c.w_hi = [sb(f"j_whi{p}", [P, KD, P], F32R) for p in range(2)]
        c.w_lo = [sb(f"j_wlo{p}", [P, KD, P], F32R) for p in range(2)]
        c.out = [sb(f"j_out{r}", [P, SPAN]) for r in range(OUTS)]
        c.after_project = sb.at
        S = c.sem
        c.w_hi_done, c.w_lo_done, c.bank_full, c.bank_read = (
            S("j_" + n) for n in ("w_hi_done", "w_lo_done", "bank_full", "bank_read"))
        c.stored = [S(f"j_stored{r}") for r in range(OUTS)]
    w_raw, w_hi, w_lo, out = c.w_raw, c.w_hi, c.w_lo, c.out
    w_full, hi_done, lo_done, bank_full, bank_read, stored = (
        c.w_full, c.w_hi_done, c.w_lo_done, c.bank_full, c.bank_read, c.stored)
    rest_full = None if first else c.sem("j_rest_full")
    uses = [len(range(r, len(SPANS), OUTS)) for r in range(OUTS)]
    w_in = c.I["w_in"].rearrange("(k q) n -> q k n", q=P)

    def pairs(eng, body, j, n, *starts, loop=True):
        def turn(i):
            for o in range(2):
                body(i * 2 + (j + o), (j + o) % 2, o, i, *(i * (2 * step) + (start + o * step) for start, step in starts))
        if loop:
            with eng.Fori(0, n // 2) as i:
                turn(i)
        else:
            turn(0)

    def jobs(eng, body, peel=False):
        j = 0 if first else FIRST_JOBS
        for col, n, slot, func in FIRST_RUNS if first else REST_RUNS:
            if n == 1:
                body(j, j % 2, 0, None, slot, func, None)
                j += n
                continue
            jump_to = {FIRST_OF_JUMP: C_ZA, SLOTS: C_Q}.get(j + n) if peel else None
            loops = [(n, True)] if jump_to is None else [(n - 2, True), (2, False)]
            for n, loop in loops:
                def one(job, p, o, i, slot, col):
                    unit = None
                    if j >= FIRST_OF_CONV:
                        unit = i + (j - FIRST_OF_CONV) // 2
                    body(job, p, o, unit, slot, func, jump_to if o and not loop else col + P)
                if n:
                    pairs(eng, one, j, n, (slot, 1), (col, P), loop=loop)
                j, slot, col = j + n, slot + n, col + n * P

    def load(eng, j, col):
        eng.wait_ge(lo_done, j)
        cols = bass.ds(col, P) if not isinstance(col, int) else slice(col, col + P)
        eng.dma_start(w_raw[:], w_in[:, :, cols]).then_inc(w_full if first else rest_full, 16)

    def low(pool, j, p):
        pool.wait_ge(hi_done, j + 1)
        pool.tensor_tensor(w_lo[p][:], w_raw[:], f32(w_hi[p][:]), ALU.subtract).then_inc(lo_done, 1)

    def gpsimd_first(pool):
        for s, n in c.hT_done:
            pool.wait_ge(s, n)
        zeros = c.zero[:].unsqueeze(1).to_broadcast([P, KD, P])

        def weights(j, p, o, i, col):
            load(pool, j, col)
            pool.wait_ge(w_full, j * 16 + 16)
            if not isinstance(j, int):
                pool.wait_ge(bank_full, j * 5 - 5)
            pool.tensor_tensor(w_hi[p][:], w_raw[:], zeros, ALU.add).then_inc(hi_done, 1)
            low(pool, j, p)
        weights(0, 0, 0, 0, FIRST_RUNS[0][0])
        pairs(pool, weights, 1, FIRST_JOBS - 1, (FIRST_RUNS[1][0], P))

    def gpsimd_rest(pool):
        for s, n in c.scores_stored:
            pool.wait_ge(s, n)

        def weights(j, p, o, i):
            pool.wait_ge(bank_full, j * 5 - 5)
            low(pool, j, p)

        def weights_and_unit(j, p, o, i):
            weights(j, p, o, i)
            c.add_taps(pool, i, o)

        pairs(pool, weights, FIRST_JOBS, FIRST_OF_CONV - FIRST_JOBS)
        pairs(pool, weights_and_unit, FIRST_OF_CONV, 2 * UNITS)
        pool.wait_ge(hi_done, SLOTS + 1)

    def tensor(pe):
        for s, n in c.hT_done:
            pe.wait_ge(s, n)
        if not first:
            for s, n in c.scores_stored:
                pe.wait_ge(s, n)

        def job(j, p, *_):
            pe.wait_ge(lo_done, j + 1)
            for b, (t0, n) in enumerate(SPANS):
                if not isinstance(j, int):
                    pe.wait_ge(bank_read, j * 5 + (b - 4))
                bank = c.psum[:, b, 0:n]
                for k in range(KD):
                    for q, (w, h) in enumerate(((w_hi, c.hT_hi), (w_hi, c.hT_lo), (w_lo, c.hT_hi))):
                        last = pe.matmul(bank, w[p][:, k, :], h[:, k, t0:t0 + n],
                                         start=(k == 0 and q == 0), stop=(k == KD - 1 and q == 2))
                last.then_inc(bank_full, 1)
        jobs(pe, job)

    def scalar(act):
        def high(j, p):
            act.wait_ge(rest_full, (j - FIRST_JOBS) * 16 + 16)
            act.wait_ge(bank_full, j * 5 - 5)
            act.copy(w_hi[p][:], w_raw[:]).then_inc(hi_done, 1)

        def evacuate(j, p, o, unit, slot, func, next_col):
            if not first:
                load(act, j + 1, next_col)
            for b, (t0, n) in enumerate(SPANS):
                if b == 2 and not first:
                    high(j + 1, 1 - p)
                if unit is not None:
                    c.make_taps(act, unit, o, b)
                r = b % OUTS
                act.wait_ge(bank_full, j * 5 + (b + 1))
                act.wait_ge(stored[r], j * (16 * uses[r]) + 16 * (b // OUTS))
                act.activation(out[r][:], c.psum[:, b, 0:n], FUNC[func]).then_inc(bank_read, 1)
                act.wait_ge(bank_read, j * 5 + (b + 1))
                act.dma_start(c.T_dram[at(slot, 1), :, t0:t0 + n].rearrange("a q t -> q (a t)"), out[r][:]).then_inc(stored[r], 16)
        if not first:
            for s, n in c.scores_stored:
                act.wait_ge(s, n)
            load(act, FIRST_JOBS, C_GA)
            high(FIRST_JOBS, FIRST_JOBS % 2)
        jobs(act, evacuate, peel=not first)

    done = [(s, 16 * uses[r] * (FIRST_JOBS if first else SLOTS)) for r, s in enumerate(stored)]
    if first:
        c.first_stored = done
        c.conv_inputs_stored = [(s, 16 * uses[r] * (FIRST_JOBS + 8)) for r, s in enumerate(stored)]
    else:
        c.T_stored = done
    return Programs(scalar=scalar, tensor=tensor, gpsimd=gpsimd_first if first else gpsimd_rest)


def stage_project_first(c):
    return project(c, True)


def stage_project_rest(c):
    return project(c, False)


CLASSES = [(4 * j, 512 * (j + 1)) for j in range(4)] + [(DT, PAST + DEC)]


def pieces(keys):
    return [(a, min(512, keys - a)) for a in range(0, keys, 512)]


def query_tiles(loop, body):
    for j, (t0, keys) in enumerate(CLASSES):
        if t0 == DT:
            body(j, DT, DT // 2, 0)
            continue
        with loop(j) as i:
            for p in range(2):
                body(j, i * 2 + (t0 + p), i + t0 // 2, p)


def doubled(eng, dst, src, sem):
    eng.dma_start(dst[0:HD], src).then_inc(sem, 16)
    eng.dma_start(dst[HD:P], src).then_inc(sem, 16)


def stage_natural(c):
    nc, sb = c.nc, Sbuf(c.nc, c.after_hT)
    kvT = [sb(f"t_kvT{p}", [P, 3, P]) for p in range(2)]
    nat = [sb(f"t_nat{p}", [P, 3, P]) for p in range(2)]
    iw = sb("t_iw", [P, TILES, IH])
    S = c.sem
    own_steps = S("t_steps")
    full = [S(f"t_full{p}") for p in range(2)]
    turned = [S(f"t_turned{p}") for p in range(2)]
    copied = [S(f"t_copied{p}") for p in range(2)]
    iw_read = [S(f"t_iw_read{p}") for p in range(2)]
    stored = [S(f"t_stored{p}") for p in range(2)]
    half = DT // 2

    def tiles(eng, body):
        with eng.Fori(0, half) as i:
            body(i * 2, i, 0)
            body(i * 2 + 1, i, 1)
        body(DT, half, 0)

    def sync(sp):
        for s, n in c.first_stored:
            sp.wait_ge(s, n)

        def load(t, m, p):
            sp.wait_ge(turned[p], m)
            sp.dma_start(kvT[p][:, 0:2, 0:real(t)], c.T_dram[S_K:S_K + 2, :, at(t)].rearrange("s q t -> q s t")).then_inc(full[p], 16)
            sp.dma_start(kvT[p][:, 2, 0:real(t)], c.T_dram[S_IKW, :, at(t)]).then_inc(full[p], 16)
        tiles(sp, load)

    def tensor(pe):
        pe.wait_ge(c.bank_read, 5 * FIRST_JOBS)

        def turn(t, m, p):
            pe.wait_ge(full[p], m * 32 + 32)
            pe.wait_ge(copied[p], m)
            for s in range(3):
                last = pe.transpose(c.psum[:, p, s * P:(s + 1) * P], kvT[p][:, s, :], c.ident[:])
            last.then_inc(turned[p], 1)
        tiles(pe, turn)

    def vector(vec):
        steps = Steps(vec, own_steps)

        def copy(t, m, p):
            vec.wait_ge(turned[p], m + 1)
            vec.wait_ge(stored[p], m * 48)
            vec.wait_ge(iw_read[p], m)
            vec.tensor_copy(nat[p][:], c.psum[:, p, 0:3 * P].rearrange("q (s n) -> q s n", s=3)).then_inc(copied[p], 1)
            vec.wait_ge(copied[p], m + 1)
            vec.tensor_copy(iw[:, bass.ds(t, 1) if not isinstance(t, int) else slice(t, t + 1), :],
                            nat[p][:, 2:3, HD:HD + IH]).then_inc(iw_read[p], 1)
        tiles(vec, copy)
        for p in range(2):
            vec.wait_ge(iw_read[p], half + 1 - p)
        steps.did_wait(vec.tensor_scalar(c.sg[:], iw[:], 0.0, 2.0, ALU.is_ge, ALU.mult))
        steps.did_wait(vec.tensor_scalar(c.sg[:], c.sg[:], -1.0, None, ALU.add))
        steps.did_wait(vec.tensor_scalar(iw[:], iw[:], IDX_W_SCALE, 0.0, ALU.mult, ALU.add))
        vec.tensor_tensor(c.aw[:], iw[:], c.sg[:], ALU.mult).then_inc(c.weights_ready, 1)

    def scalar(act):
        def store(t, m, p):
            act.wait_ge(copied[p], m + 1)
            for s, n, name in ((0, P, "k"), (1, P, "v"), (2, HD, "ik")):
                if isinstance(t, int):
                    dst, rows = c.O[name + "_sample"].rearrange("(t h) d -> t (h d)", t=DEC), DEC
                else:
                    dst, rows = c.O[name + "_prompt"].rearrange("(t h) d -> t (h d)", t=SEQ)[at(t), :], P
                act.dma_start(dst, nat[p][0:rows, s, 0:n]).then_inc(stored[p], 16)
        tiles(act, store)
        for p in range(2):
            act.wait_ge(stored[p], 48 * (half + 1 - p))

    c.natural_freed = (stored[0], 48 * (half + 1)), (stored[1], 48 * half), (c.weights_ready, 1)
    return Programs(sync=sync, vector=vector, tensor=tensor, scalar=scalar)


def stage_scores(c):
    nc, sb = c.nc, Sbuf(c.nc, c.after_hT)
    NS = PAST + DEC
    ik_hi = sb("i_ikhi", [P, SEQ], F32R)
    ik_lo = sb("i_iklo", [P, SEQ], F32R)
    iks_hi = sb("i_ikshi", [P, NS], F32R)
    iks_lo = sb("i_ikslo", [P, NS], F32R)
    acc = [sb(f"i_acc{p}", [P, SEQ]) for p in range(2)]
    iq2 = [sb(f"i_iq{p}", [P, IH, P]) for p in range(2)]
    iqs = [sb(f"i_iqs{p}", [P, IH, P], F32R) for p in range(2)]
    R = [sb(f"i_r{r}", [P, 512]) for r in range(4)]
    aw = [sb(f"i_aw{p}", [P, IH]) for p in range(2)]
    S = c.sem
    own_steps = S("i_steps")
    raw_full = S("i_raw_full")
    raws_full = S("i_raws_full")
    cache_full = S("i_cache_full")
    cache_turned = S("i_cache_turned")
    ik_ready = S("i_ik_ready")
    iq_full = [S(f"i_iq_full{p}") for p in range(2)]
    iqs_ready = [S(f"i_iqs_ready{p}") for p in range(2)]
    product = S("i_product")
    bank_read = [S(f"i_bank_read{b}") for b in range(8)]
    r_used = [S(f"i_r_used{r}") for r in range(4)]
    acc_ready = [S(f"i_acc_ready{p}") for p in range(2)]
    stored = c.acc_stored
    cache = acc[1][:, 0:SEQ // 2].rearrange("q (t u d) -> q t u d", t=8, u=2)
    cacheT = c.psum[:, 0:2, :].rearrange("q b n -> q (b n)")
    new_ik = acc[1][:, SEQ // 2:SEQ // 2 + DEC]

    per_tile = [IH * len(pieces(keys)) for _, keys in CLASSES]
    before = [4 * sum(per_tile[:j]) for j in range(len(CLASSES))]

    def units(j, m, p):
        t0, keys = CLASSES[j]
        i = m - t0 // 2 if not isinstance(m, int) else 0
        for n, (h, (a, w)) in enumerate((h, s) for h in range(IH) for s in pieces(keys)):
            u = p * per_tile[j] + n
            start = before[j] + u
            turn = 2 * per_tile[j]
            back = start - len(pieces(keys))
            yield (h, a, w, u % 8, i * (turn // 8) + start // 8, u % 4, i * (turn // 4) + start // 4,
                   i * turn + start, back % 4, i * (turn // 4) + back // 4 + 1)

    def fori(eng):
        return lambda j: eng.Fori(0, 2)

    def sync(sp):
        for s, n in c.natural_freed:
            sp.wait_ge(s, n)
        doubled(sp, acc[0], c.T_dram[S_IKW, 0:HD, 0:SEQ], raw_full)
        doubled(sp, new_ik, c.T_dram[S_IKW, 0:HD, SEQ:SEQ + DEC], raws_full)
        for u in range(2):
            sp.dma_start(cache[:, :, u, :], c.I["cache_idx_k"].rearrange("(t q) d -> q t d", q=P)).then_inc(cache_full, 16)

        def load(j, t, m, p):
            sp.wait_ge(iqs_ready[p], m)
            rows = c.T_dram[S_IQ:S_IQ + 2].rearrange("s q t -> (s q) t").rearrange("(h d) t -> d h t", d=HD)
            doubled(sp, iq2[p][:, :, 0:real(t)], rows[:, :, at(t)], iq_full[p])
        query_tiles(fori(sp), load)

    def tensor(pe):
        pe.wait_ge(cache_full, 32)
        for s, n in c.natural_freed:
            pe.wait_ge(s, n)
        for t in range(8):
            last = pe.transpose(cacheT[:, t * P:(t + 1) * P], cache[:, t].rearrange("q u d -> q (u d)"), c.ident[:])
        last.then_inc(cache_turned, 1)
        pe.wait_ge(ik_ready, 1)

        def score(j, t, m, p):
            hi, lo = (iks_hi, iks_lo) if t is DT else (ik_hi, ik_lo)
            pe.wait_ge(iqs_ready[p], m + 1)
            for h, a, w, b, nb, *_ in units(j, m, p):
                pe.wait_ge(bank_read[b], nb)
                pe.matmul(c.psum[:, b, 0:w], iqs[p][:, h, :], hi[:, a:a + w], start=True, stop=False)
                pe.matmul(c.psum[:, b, 0:w], iqs[p][:, h, :], lo[:, a:a + w], start=False, stop=True).then_inc(product, 1)
        query_tiles(fori(pe), score)

    def scalar(act):
        act.wait_ge(c.weights_ready, 1)

        def relu(j, t, m, p):
            for h, a, w, b, _, r, nr, n, *_ in units(j, m, p):
                act.wait_ge(product, n + 1)
                act.wait_ge(r_used[r], nr)
                act.activation(R[r][:, 0:w], c.psum[:, b, 0:w], ACT.Relu,
                               scale=aw[p][:, h:h + 1]).then_inc(bank_read[b], 1)
        query_tiles(fori(act), relu)

    def vector(vec):
        steps = Steps(vec, own_steps)
        vec.wait_ge(raw_full, 32)
        steps.did_wait(vec.tensor_copy(ik_hi[:], acc[0][:]))
        steps.did_wait(vec.tensor_tensor(ik_lo[:], acc[0][:], f32(ik_hi[:]), ALU.subtract))
        vec.wait_ge(raws_full, 32)
        vec.wait_ge(cache_turned, 1)
        for dst, src in ((slice(0, PAST), cacheT), (slice(PAST, NS), new_ik)):
            steps.did_wait(vec.tensor_copy(iks_hi[:, dst], src))
            steps.did_wait(vec.tensor_tensor(iks_lo[:, dst], src, f32(iks_hi[:, dst]), ALU.subtract))
        vec.sem_inc(ik_ready, 1)

        def split(t, m, p):
            vec.wait_ge(iq_full[p], m * 32 + 32)
            steps.did(vec.tensor_scalar(aw[p][:], c.aw[:, at(t, 1), :], 1.0, None, ALU.mult))
            steps.did_wait(vec.tensor_copy(iqs[p][:], iq2[p][:]))
            vec.tensor_tensor(iqs[p][HD:P], iq2[p][HD:P], f32(iqs[p][HD:P]), ALU.subtract).then_inc(iqs_ready[p], 1)

        def add(j, t, m, p):
            if t is not DT:
                split(t + 1, m + p, 1 - p)
            vec.wait_ge(stored[p], m * 16)
            for h, a, w, b, nb, r, nr, n, r_before, n_before in units(j, m, p):
                vec.wait_ge(bank_read[b], nb + 1)
                sg = c.sg[:, at(t, 1), h]
                if h == 0:
                    ins = vec.tensor_scalar(acc[p][:, a:a + w], R[r][:, 0:w], sg, 0.0, ALU.mult, ALU.add)
                else:
                    vec.wait_ge(r_used[r_before], n_before)
                    ins = vec.scalar_tensor_tensor(out=acc[p][:, a:a + w], in0=R[r][:, 0:w], scalar=sg,
                                                   in1=acc[p][:, a:a + w], op0=ALU.mult, op1=ALU.add)
                ins.then_inc(r_used[r], 1)
            vec.wait_ge(r_used[r], nr + 1)
            vec.sem_inc(acc_ready[p], 1)
        split(0, 0, 0)
        query_tiles(lambda j: steps.turns(2, 4), add)

    def gpsimd(pool):
        def store(j, t, m, p):
            pool.wait_ge(acc_ready[p], m + 1)
            keys = CLASSES[j][1]
            dst = c.SC_dram[at(t, 1), :, 0:keys].rearrange("a q n -> q (a n)")
            pool.dma_start(dst, acc[p][:, 0:keys]).then_inc(stored[p], 16)
        query_tiles(fori(pool), store)

    c.scores_stored = (stored[0], 16 * (DT // 2 + 1)), (stored[1], 16 * (DT // 2))
    return Programs(sync=sync, scalar=scalar, vector=vector, tensor=tensor, gpsimd=gpsimd)


def stage_constants(c):
    nc, sb = c.nc, Sbuf(c.nc, c.after_hT)
    sb.at += 4 * 14 * 1024
    pos = sb("c_pos", [P, TILES], I32)
    chunk = sb("c_chunk", [P, TILES], I32)
    made, step = c.sem("c_made"), c.sem("c_step")

    def gpsimd(pool):
        pool.iota(pos[:, 0:DT], pattern=[[P, DT]], base=0, channel_multiplier=1).then_inc(made, 1)
        pool.iota(pos[:, DT:TILES], pattern=[[0, 1]], base=PAST, channel_multiplier=1).then_inc(made, 1)

    def vector(vec):
        steps = Steps(vec, step)
        vec.wait_ge(made, 2)
        steps.did_wait(vec.tensor_copy(c.qpos[:], pos[:]))
        steps.did_wait(vec.tensor_scalar(chunk[:], pos[:], 6, None, ALU.arith_shift_right))
        steps.did_wait(vec.tensor_scalar(c.lim[:], chunk[:], 1.0, float(CHUNK), ALU.add, ALU.mult))

    return Programs(gpsimd=gpsimd, vector=vector)


MASKED = 1e30
UNITS_FROM, UNIT_STEP = 0.15, 0.042
SELECT_STEPS = 2 * 49 + 23


def stage_select(c):
    nc, sb = c.nc, Sbuf(c.nc, c.after_convolve)
    key = [sb(f"s_key{p}", [P, SEQ], I32) for p in range(2)]
    mask = sb("s_mask", [P, SEQ], I32)
    order = sb("s_order", [P, SEQ], I16)
    junk = order[:].bitcast(BF16)
    iota = sb("s_iota", [P, SEQ], I16)
    cnt, g, cand, th, need, u, th1 = (sb(f"s_{n}", [P, 1]) for n in ("cnt", "g", "cand", "th", "need", "u", "th1"))
    H = mask[:, 0:SEQ // 2].bitcast(U16)
    eq = mask[:, SEQ // 2:].bitcast(BF16)
    S = c.sem
    own_steps = S("s_steps")
    full = [S(f"s_full{p}") for p in range(2)]
    done = [S(f"s_done{p}") for p in range(2)]
    stored = [S(f"s_stored{p}") for p in range(2)]
    iota_made = S("s_iota_made")

    def sync(sp):
        for s, n in c.scores_stored:
            sp.wait_ge(s, n)

        columns = [CLASSES[t // 4][1] + 200 if t > 1 else 100 for t in range(TILES)]

        def unit_due(u):
            return sum(columns) * (UNITS_FROM + UNIT_STEP * u)

        upcoming = [0]

        def units(until):
            while upcoming[0] <= UNITS + 1 and unit_due(upcoming[0]) < until:
                if upcoming[0] > 1:
                    c.move_unit(sp, upcoming[0] - 2)
                if upcoming[0] < UNITS:
                    c.load_unit(sp, upcoming[0])
                upcoming[0] += 1

        def rows(dram, t):
            keys = CLASSES[t // 4][1]
            return dram[t, :, 0:keys], key[t % 2][:, 0:keys]

        for t in range(TILES + 1):
            p = t % 2
            if t < TILES:
                dram, sbuf = rows(c.SC_dram, t)
                sp.wait_ge(stored[p], t // 2 * 16)
                sp.dma_start(sbuf, dram.bitcast(I32)).then_inc(full[p], 16)
            units(sum(columns[:t]))
            if t > 0:
                dram, sbuf = rows(c.ND_dram, t - 1)
                sp.wait_ge(done[1 - p], (t - 1) // 2 + 1)
                sp.dma_start(dram, f32(sbuf)).then_inc(stored[1 - p], 16)
        units(float("inf"))
        for p in range(2):
            sp.wait_ge(stored[p], 16 * (DT // 2 + 1 - p))

    def gpsimd(pool):
        for s, n in c.scores_stored:
            pool.wait_ge(s, n)
        pool.iota(iota[:], pattern=[[1, SEQ]], base=0, channel_multiplier=0).then_inc(iota_made, 1)

    def vector(vec):
        steps = Steps(vec, own_steps)
        do = steps.did_wait

        def search(src, first, k):
            do(vec.tensor_scalar(cand[:], c.zero[:], float(first + 2 ** 15), None, ALU.add))
            for b in reversed(range(16)):
                do(vec.tensor_scalar(junk[:, 0:src.shape[1]], src, cand[:], 0.0, ALU.is_ge, ALU.add, accum_out=cnt[:]))
                do(vec.tensor_scalar(g[:], cnt[:], k, float(2 ** b), ALU.is_ge, ALU.mult))
                do(vec.scalar_tensor_tensor(out=cand[:], in0=g[:], scalar=-(2.0 ** (b - 1)) if b else -1.0,
                                            in1=cand[:], op0=ALU.add, op1=ALU.add))

        def select(j, t, m, p):
            n = CLASSES[j][1]
            lo = max(0, n - 512)
            tail = slice(lo, n)
            K, M, Hn, e, o = key[p][:, 0:n], mask[:, 0:n], H[:, 0:n], eq[:, 0:n], order[:, 0:n]
            high = key[p][:].bitcast(I16)[:, 1:2 * n:2]
            low = key[p][:].bitcast(U16)[:, 0:2 * n:2]
            lim, qpos = c.lim[:, at(t, 1)], c.qpos[:, at(t, 1)]
            vec.wait_ge(full[p], m * 16 + 16)
            do(vec.tensor_scalar(M, K, 31, 0x7FFFFFFF, ALU.arith_shift_right, ALU.bitwise_and))
            do(vec.tensor_tensor(K, M, K, ALU.bitwise_xor))
            do(vec.tensor_scalar(junk[:, 0:n - lo], iota[:, tail], lim, None, ALU.is_lt))
            if lo:
                do(vec.tensor_scalar(Hn[:, 0:lo], high[:, 0:lo], 32768.0, None, ALU.add))
            else:
                steps.did(vec.tensor_scalar(g[:], c.zero[:], 0.0, None, ALU.add))
            do(vec.scalar_tensor_tensor(out=Hn[:, tail], in0=high[:, tail], scalar=32768.0, in1=junk[:, 0:n - lo],
                                        op0=ALU.add, op1=ALU.mult))
            search(Hn, 0, float(TOPK))
            do(vec.tensor_scalar(th[:], cand[:], 0.0, None, ALU.add))
            do(vec.tensor_scalar(th1[:], cand[:], 1.0, None, ALU.add))
            do(vec.tensor_scalar(junk[:, 0:n], Hn, th1[:], 0.0, ALU.is_ge, ALU.add, accum_out=cnt[:]))
            do(vec.tensor_scalar(need[:], cnt[:], -1.0, float(TOPK), ALU.mult, ALU.add))
            do(vec.tensor_scalar(e, Hn, th[:], None, ALU.is_equal))
            do(vec.scalar_tensor_tensor(out=f32(K), in0=low, scalar=1.0, in1=e, op0=ALU.add, op1=ALU.mult))
            search(f32(K), 1, need[:])
            do(vec.tensor_scalar(u[:], cand[:], 1.0, None, ALU.add))
            do(vec.tensor_scalar(junk[:, 0:n], f32(K), u[:], 0.0, ALU.is_ge, ALU.add, accum_out=cnt[:]))
            do(vec.tensor_tensor(need[:], need[:], cnt[:], ALU.subtract))
            do(vec.tensor_scalar(e, f32(K), cand[:], None, ALU.is_equal))
            do(vec.tensor_tensor_scan(o, e, e, 0.0, ALU.add, ALU.max))
            do(vec.scalar_tensor_tensor(out=e, in0=o, scalar=need[:], in1=e, op0=ALU.is_le, op1=ALU.mult))
            do(vec.scalar_tensor_tensor(out=e, in0=f32(K), scalar=u[:], in1=e, op0=ALU.is_ge, op1=ALU.add))
            do(vec.scalar_tensor_tensor(out=e, in0=Hn, scalar=th1[:], in1=e, op0=ALU.is_ge, op1=ALU.add))
            do(vec.scalar_tensor_tensor(out=e[:, tail], in0=iota[:, tail], scalar=lim, in1=e[:, tail],
                                        op0=ALU.is_lt, op1=ALU.mult))
            do(vec.tensor_scalar(f32(K), e, -1.0, MASKED, ALU.add, ALU.mult))
            do(vec.scalar_tensor_tensor(out=f32(K), in0=iota[:, 0:n], scalar=qpos, in1=f32(K),
                                        op0=ALU.subtract, op1=ALU.min))
            do(vec.tensor_scalar(o[:, tail], iota[:, tail], -1.0, qpos, ALU.mult, ALU.add))
            vec.tensor_tensor(f32(K[:, tail]), o[:, tail], f32(K[:, tail]), ALU.min).then_inc(done[p], 1)

        def select_all(t, m, p):
            n = CLASSES[0][1]
            K, e, o = f32(key[p][:, 0:n]), eq[:, 0:n], order[:, 0:n]
            lim, qpos = c.lim[:, t:t + 1], c.qpos[:, t:t + 1]
            vec.wait_ge(full[p], m * 16 + 16)
            do(vec.tensor_scalar(e, iota[:, 0:n], lim, None, ALU.is_lt))
            do(vec.tensor_scalar(K, e, -1.0, MASKED, ALU.add, ALU.mult))
            do(vec.scalar_tensor_tensor(out=K, in0=iota[:, 0:n], scalar=qpos, in1=K, op0=ALU.subtract, op1=ALU.min))
            do(vec.tensor_scalar(o, iota[:, 0:n], -1.0, qpos, ALU.mult, ALU.add))
            vec.tensor_tensor(K, o, K, ALU.min).then_inc(done[p], 1)

        vec.wait_ge(iota_made, 1)
        select_all(0, 0, 0)
        select_all(1, 0, 1)
        select(0, 2, 1, 0)
        select(0, 3, 1, 1)
        for j, (t0, _) in enumerate(CLASSES[1:-1], 1):
            with steps.turns(2, 2 * SELECT_STEPS) as i:
                for p in range(2):
                    select(j, i * 2 + (t0 + p), i + t0 // 2, p)
        select(len(CLASSES) - 1, DT, DT // 2, 0)

    c.selected = (stored[0], 16 * (DT // 2 + 1)), (stored[1], 16 * (DT // 2))
    return Programs(sync=sync, vector=vector, gpsimd=gpsimd)


def token_tiles(eng, body, turns=None):
    with (turns or eng.Fori(0, DT // 2)) as i:
        body(i * 2, i, 0)
        body(i * 2 + 1, i, 1)
    body(DT, DT // 2, 0)


def stage_gmlp(c):
    nc, sb = c.nc, Sbuf(c.nc, c.first)
    w_raw = sb("g_wraw", [P, 4, P])
    wT = sb("g_wT", [P, 4, P])
    bias = sb("g_bias", [P, 4, P])
    offset = sb("g_offset", [P, 4, P])
    gain = sb("g_gain", [P, 4])
    ln_g = sb("g_lng", [P, BW])
    ln_b = sb("g_lnb", [P, BW])
    vT = sb("g_vT", [P, 4, TILES * P])
    uT, zT, vn, ob = ([sb(f"g_{n}{p}", [P, 4, P]) for p in range(2)] for n in ("uT", "zT", "vn", "ob"))
    stats = sb("g_stats", [P, TILES, 6])
    mean, var, rstd, tmp = (sb(f"g_{n}", [P, TILES]) for n in ("mean", "var", "rstd", "tmp"))
    c.y, c.y_full = sb("g_y", [P, 4, CONVS]), c.sem("g_y_full")
    c.after_gmlp = sb.at
    S = c.sem
    own_steps = S("g_steps")
    const_full = S("g_const_full")
    w_turned = S("g_w_turned")
    w_ready = S("g_w_ready")
    offset_product = S("g_offset_product")
    v_full = [S(f"g_v_full{h}") for h in range(2)]
    uz_full, turned, measured, again, normed, mixed, mix_read, multiplied, gated, stored = (
        [S(f"g_{n}{p}") for p in range(2)]
        for n in ("uz_full", "turned", "measured", "again", "normed", "mixed", "mix_read", "multiplied", "gated", "stored"))
    v_stored, last_columns, parts = S("g_v_stored"), S("g_last_columns"), S("g_parts")
    slot = lambda s, t: c.T_dram[s:s + 4, :, at(t)].rearrange("s q t -> q s t")
    half = DT // 2

    def sync(sp):
        for s, n in c.T_stored + list(c.selected):
            sp.wait_ge(s, n)
        for h, (a, b) in enumerate(((0, SEQ // 2), (SEQ // 2, TOK))):
            sp.dma_start(vT[:, :, a:b], c.T_dram[S_GV:S_GV + 4, :, a:b].rearrange("s q t -> q s t")).then_inc(v_full[h], 16)
            if h == 0:
                sp.dma_start(w_raw[:], c.I["gmlp_ws"].rearrange("(g i) j -> i g j", g=4)).then_inc(const_full, 16)
                sp.dma_start(bias[:].rearrange("q g i -> q (g i)"),
                             c.I["gmlp_bs"].rearrange("g i -> (g i)").partition_broadcast(P)).then_inc(const_full, 16)
                sp.dma_start(ln_g[:], c.I["gmlp_ln_g"].partition_broadcast(P)).then_inc(const_full, 16)
                sp.dma_start(ln_b[:], c.I["gmlp_ln_b"].partition_broadcast(P)).then_inc(const_full, 16)

        for s in range(4):
            sp.dma_start(c.y[:, s, :], c.Y_dram[s]).then_inc(c.y_full, 16)

        def load(t, m, p):
            sp.wait_ge(multiplied[p], m)
            sp.dma_start(zT[p][:, :, 0:real(t)], slot(S_ZB, t)).then_inc(uz_full[p], 16)
            sp.wait_ge(gated[p], m)
            sp.dma_start(uT[p][:, :, 0:real(t)], slot(S_U, t)).then_inc(uz_full[p], 16)
        token_tiles(sp, load)

    def tensor(pe):
        for s, n in c.T_stored:
            pe.wait_ge(s, n)
        pe.wait_ge(v_full[0], 16)
        pe.wait_ge(v_full[1], 16)
        pe.wait_ge(last_columns, 1)

        def turn(p, t, sem):
            for s in range(4):
                last = pe.transpose(c.psum[:, p, s * P:(s + 1) * P], vT[:, s, t * P:(t + 1) * P], c.ident[:])
            last.then_inc(sem[p], 1)

        def first(t, m, p):
            pe.wait_ge(measured[p], m)
            turn(p, t, turned)

        def second(t, m, p):
            pe.wait_ge(normed[p], m)
            turn(p, t, again)

        def mix(t, m, p):
            rows = real(t)
            pe.wait_ge(normed[p], m + 1)
            pe.wait_ge(mix_read[p], m)
            for g in range(4):
                last = pe.matmul(c.psum[:, 2 + p, g * P:(g + 1) * P], vn[p][0:rows, g, :], wT[0:rows, g, :],
                                 start=True, stop=True)
            last.then_inc(mixed[p], 1)

        for t in range(TILES):
            first(t, t // 2, t % 2)
        pe.wait_ge(const_full, 64)
        for g in range(4):
            last = pe.transpose(c.psum[:, 4, g * P:(g + 1) * P], w_raw[:, g, :], c.ident[:])
        last.then_inc(w_turned, 1)
        pe.wait_ge(w_ready, 2)
        for g in range(4):
            pe.matmul(c.psum[:, 5, g * P:(g + 1) * P], ln_b[:, g * P:(g + 1) * P], wT[:, g, :], start=True, stop=True)
        for g in range(4):
            last = pe.transpose(c.psum[:, 6, g * P:(g + 1) * P], ln_g[:, g * P:(g + 1) * P], c.ident[:])
        last.then_inc(offset_product, 1)
        pe.wait_ge(measured[0], half + 1)
        pe.wait_ge(measured[1], half)
        second(0, 0, 0)
        for t in range(TILES):
            if t + 1 < TILES:
                second(t + 1, (t + 1) // 2, (t + 1) % 2)
            mix(t, t // 2, t % 2)

    def vector(vec):
        steps = Steps(vec, own_steps)
        do = steps.did_wait

        def measure(t, m, p):
            vec.wait_ge(turned[p], m + 1)
            vec.bn_stats(stats[:, at(t, 1), :].rearrange("q a n -> q (a n)"), c.psum[:, p, :]).then_inc(measured[p], 1)

        def norm(t, m, p):
            vec.wait_ge(again[p], m + 1)
            vec.wait_ge(mixed[p], m)
            flat = vn[p][:].rearrange("q g n -> q (g n)")
            ins = vec.tensor_scalar(flat, c.psum[:, p, :], mean[:, at(t, 1)], rstd[:, at(t, 1)], ALU.subtract, ALU.mult)
            if isinstance(t, int) and t == DT:
                do(ins)
                do(vec.tensor_tensor(flat, flat, ln_g[:], ALU.mult))
                ins = vec.tensor_tensor(flat, flat, ln_b[:], ALU.add)
            ins.then_inc(normed[p], 1)

        def shift(t, m, p):
            vec.wait_ge(mixed[p], m + 1)
            vec.wait_ge(stored[p], m * 16)
            mix = c.psum[:, 2 + p, :].rearrange("q (g i) -> q g i", g=4)
            if isinstance(t, int) and t == DT:
                vec.tensor_tensor(ob[p][:], mix, bias[:], ALU.add).then_inc(mix_read[p], 1)
                return
            for g in range(4):
                vec.scalar_tensor_tensor(out=ob[p][:, g, :], in0=mix[:, g, :], scalar=gain[:, g:g + 1], in1=offset[:, g, :],
                                         op0=ALU.mult, op1=ALU.add).then_inc(parts, 1)
            vec.wait_ge(parts, m * 8 + (4 * p + 4))
            vec.sem_inc(mix_read[p], 1)

        token_tiles(vec, measure)
        vec.wait_ge(const_full, 64)
        vec.wait_ge(w_turned, 1)
        vec.tensor_copy(wT[:], c.psum[:, 4, :].rearrange("q (g i) -> q g i", g=4)).then_inc(w_ready, 1)
        vec.wait_ge(w_ready, 1)
        vec.memset(wT[CHUNK:P, :, 0:CHUNK], 0.0).then_inc(w_ready, 1)
        for p in range(2):
            vec.wait_ge(measured[p], half + 1 - p)
        s = lambda n: stats[:, :, n]
        do(vec.tensor_tensor(mean[:], s(1), s(4), ALU.add))
        do(vec.tensor_tensor(var[:], s(2), s(5), ALU.add))
        do(vec.tensor_tensor(tmp[:], s(1), s(4), ALU.subtract))
        do(vec.tensor_scalar(mean[:], mean[:], 0.5, None, ALU.mult))
        do(vec.scalar_tensor_tensor(out=tmp[:], in0=tmp[:], scalar=0.25, in1=tmp[:], op0=ALU.mult, op1=ALU.mult))
        do(vec.scalar_tensor_tensor(out=var[:], in0=var[:], scalar=1.0 / BW, in1=tmp[:], op0=ALU.mult, op1=ALU.add))
        do(vec.tensor_scalar(var[:], var[:], EPS, None, ALU.add))
        rsqrt(steps, rstd[:], var[:], tmp[:])
        vec.wait_ge(offset_product, 1)
        do(vec.tensor_tensor(offset[:], c.psum[:, 5, :].rearrange("q (g i) -> q g i", g=4), bias[:], ALU.add))
        do(vec.tensor_copy(gain[:], c.psum[:, 6, :].rearrange("q (g i) -> q g i", g=4)[:, :, 0]))
        norm(0, 0, 0)
        with vec.Fori(0, half - 1) as i:
            norm(i * 2 + 1, i, 1)
            shift(i * 2, i, 0)
            norm(i * 2 + 2, i + 1, 0)
            shift(i * 2 + 1, i, 1)
        for t in range(DT - 2, TILES):
            if t < DT:
                norm(t + 1, (t + 1) // 2, (t + 1) % 2)
            shift(t, t // 2, t % 2)

    def gpsimd(pool):
        for s, n in c.T_stored + list(c.selected):
            pool.wait_ge(s, n)
        pool.memset(vT[:, :, TOK:], 0.0).then_inc(last_columns, 1)

        def gate(t, m, p):
            w = real(t)
            pool.wait_ge(uz_full[p], m * 32 + 32)
            pool.tensor_tensor(uT[p][:, :, 0:w], uT[p][:, :, 0:w], zT[p][:, :, 0:w], ALU.mult).then_inc(multiplied[p], 1)
            pool.wait_ge(multiplied[p], m + 1)
            pool.wait_ge(mix_read[p], m + 1)
            pool.tensor_tensor(ob[p][:, :, 0:w], ob[p][:, :, 0:w], uT[p][:, :, 0:w], ALU.mult).then_inc(gated[p], 1)
        token_tiles(pool, gate)

    def scalar(act):
        def store(t, m, p):
            act.wait_ge(gated[p], m + 1)
            act.dma_start(c.B_dram[1, :, :, at(t)].rearrange("s q t -> q s t"), ob[p][:, :, 0:real(t)]).then_inc(stored[p], 16)
        token_tiles(act, store)
        act.wait_ge(normed[0], half + 1)
        act.dma_start(c.O["gmlp_sample"], vn[0][0:DEC].rearrange("q g n -> q (g n)")).then_inc(v_stored, 16)
        act.wait_ge(v_stored, 16)
        for p in range(2):
            act.wait_ge(stored[p], 16 * (half + 1 - p))

    c.gmlp_done = (stored[0], 16 * (half + 1)), (stored[1], 16 * half), (v_stored, 16)
    return Programs(sync=sync, scalar=scalar, vector=vector, tensor=tensor, gpsimd=gpsimd)


LEFT = CONV - 1
EXT = LEFT + SEQ + LEFT + DEC
CONVS = EXT - LEFT
DEC_AT = SEQ + LEFT
CW_SPAN = CONVS // 5
CONV_SPANS = [(a, CW_SPAN) for a in range(0, CONVS, CW_SPAN)]
UNITS = 4 * len(CONV_SPANS)


def stage_convolve(c):
    nc, sb = c.nc, Sbuf(c.nc, c.after_project)
    W = CW_SPAN + LEFT
    parT = c.parT
    stateT = sb("v_stateT", [P, 4, LEFT])
    zeros, ones = sb("v_zeros", [P, LEFT]), sb("v_ones", [P, LEFT])
    start = sb.at
    a, g, x_in, y0, y1, y_out, next_taps, taps = (sb(f"v_{n}", [P, w]) for n, w in (
        ("a", W), ("g", W), ("x", W), ("y0", CW_SPAN), ("y1", CW_SPAN), ("yout", CW_SPAN), ("next_taps", CONV + 1), ("taps", CONV + 1)))
    y = (y0, y1)
    RING = 4
    product = [sb(f"v_product{r}", [P, CW_SPAN]) for r in range(RING)]
    c.after_convolve = sb.at
    under = Sbuf(nc, start)
    par = under("v_par", [P, CW])
    state = under("v_state", [LEFT, CW])
    assert under.at <= sb.at
    S = c.sem
    par_full, par_turned, par_ready, fills_made = (S("v_" + n) for n in ("par_full", "par_turned", "par_ready", "fills_made"))
    taps_taken = S("v_taps_taken")
    full, unit_full, glu_done, y_started, made, added, moved, unit_moved = (
        S("v_" + n) for n in ("full", "unit_full", "glu_done", "y_started", "made", "added", "moved", "unit_moved"))

    counts = {"full": 0, "moved": 0}

    def load(sp, u):
        s, x = u // 5, u % 5
        if u == 0:
            sp.wait_ge(par_ready, 2)
            sp.wait_ge(fills_made, 2)
            for sem, n in c.conv_inputs_stored:
                sp.wait_ge(sem, n)
        else:
            sp.wait_ge(glu_done, u)
            sp.wait_ge(taps_taken, u)
        first = x * CW_SPAN - LEFT
        n = SEQ - first
        pieces = [(next_taps[:], parT[:, s, 0:CONV + 1])]
        if u and x == 0:
            pieces += [(c.tailsT[:, s - 1, 0, :], x_in[:, W - DEC - 2 * LEFT:W - DEC - LEFT]), (c.tailsT[:, s - 1, 1, :], x_in[:, W - LEFT:W])]
        for buf, slot, between in ((a, S_GA, stateT[:, s, :]), (g, S_GG, ones[:])):
            src = c.T_dram[slot + s]
            if x == 0:
                pieces += [(buf[:, 0:LEFT], zeros[:]), (buf[:, LEFT:W], src[:, 0:CW_SPAN])]
            elif x < 4:
                pieces += [(buf[:], src[:, first:first + W])]
            else:
                pieces += [(buf[:, 0:n], src[:, first:SEQ]), (buf[:, n:n + LEFT], between), (buf[:, n + LEFT:W], src[:, SEQ:TOK])]
        for dst, src in pieces:
            sp.dma_start(dst, src).then_inc(full, 16)
            counts["full"] += 16
        sp.wait_ge(full, counts["full"])
        sp.sem_inc(unit_full, 1)

    def move(sp, u):
        s, x = u // 5, u % 5
        pieces = [(c.Y_dram[s, :, x * CW_SPAN:(x + 1) * CW_SPAN], y_out[:])]
        if u == UNITS - 1:
            pieces += [(c.tailsT[:, s, 0, :], x_in[:, W - DEC - 2 * LEFT:W - DEC - LEFT]), (c.tailsT[:, s, 1, :], x_in[:, W - LEFT:W])]
        sp.wait_ge(added, (u + 1) * (CONV - 1))
        for dst, src in pieces:
            sp.dma_start(dst, src).then_inc(moved, 16)
            counts["moved"] += 16
        sp.wait_ge(moved, counts["moved"])
        sp.sem_inc(unit_moved, 1)

    MADE, ADDED = CONV - 2, CONV - 1

    def make_taps(act, u, half, b):
        for k in range(16 * half + 4 * b, min(16 * half + 4 * b + 4, CONV)) if b < 4 else ():
            if k == 0:
                act.wait_ge(made, u * MADE)
                act.wait_ge(unit_full, u + 1)
                act.copy(taps[:], next_taps[:]).then_inc(taps_taken, 1)
                act.wait_ge(glu_done, u + 1)
                act.wait_ge(added, u * ADDED)
                act.wait_ge(taps_taken, u + 1)
                act.activation(y[0][:], x_in[:, 0:CW_SPAN], ACT.Identity, scale=taps[:, 0:1], bias=taps[:, CONV:CONV + 1]
                               ).then_inc(y_started, 1)
            elif k == 1:
                act.activation(y[1][:], x_in[:, 1:1 + CW_SPAN], ACT.Identity, scale=taps[:, 1:2]).then_inc(y_started, 1)
            else:
                n = k - 2
                if n >= RING:
                    act.wait_ge(added, u * ADDED + (n - RING + 1))
                act.activation(product[n % RING][:], x_in[:, k:k + CW_SPAN], ACT.Identity, scale=taps[:, k:k + 1]).then_inc(made, 1)

    def add_taps(pool, u, half):
        if half == 0:
            pool.wait_ge(unit_full, u + 1)
            pool.wait_ge(made, u * MADE)
            pool.tensor_tensor(x_in[:], a[:], g[:], ALU.mult).then_inc(glu_done, 1)
        for k in range(max(2, 16 * half), min(16 * half + 16, CONV)):
            n = k - 2
            if n < 2:
                pool.wait_ge(y_started, u * 2 + (n + 1))
            else:
                pool.wait_ge(added, u * ADDED + (n - 1))
            pool.wait_ge(made, u * MADE + (n + 1))
            pool.tensor_tensor(y[n % 2][:], y[n % 2][:], product[n % RING][:], ALU.add).then_inc(added, 1)
        if half:
            pool.wait_ge(added, u * ADDED + MADE)
            pool.wait_ge(unit_moved, u)
            pool.tensor_tensor(y_out[:], y[0][:], y[1][:], ALU.add).then_inc(added, 1)

    def sync(sp):
        for s, n in c.scores_stored:
            sp.wait_ge(s, n)
        for row, name, n in ((0, "conv_w", CONV), (CONV, "conv_b", 1), (CONV + 1, "conv_ln_g", 1), (CONV + 2, "conv_ln_b", 1)):
            sp.dma_start(par[row:row + n, :], c.I[name]).then_inc(par_full, 16)
        sp.dma_start(state[:], c.I["state_conv"]).then_inc(par_full, 16)

    def tensor(pe):
        for s, n in c.scores_stored:
            pe.wait_ge(s, n)
        pe.wait_ge(par_full, 80)
        for s in range(4):
            pe.transpose(c.psum[:, 5, s * 64:s * 64 + CONV + 3], par[0:CONV + 3, s * P:(s + 1) * P], c.ident[0:CONV + 3, 0:CONV + 3])
            last = pe.transpose(c.psum[:, 6, s * 64:s * 64 + LEFT], state[:, s * P:(s + 1) * P], c.ident[0:LEFT, 0:LEFT])
        last.then_inc(par_turned, 1)

    def scalar(act):
        for s, n in c.scores_stored:
            act.wait_ge(s, n)
        act.wait_ge(par_turned, 1)
        act.copy(parT[:], c.psum[:, 5, 0:256].rearrange("q (s n) -> q s n", s=4)[:, :, 0:CONV + 3]).then_inc(par_ready, 1)
        act.copy(stateT[:], c.psum[:, 6, 0:256].rearrange("q (s n) -> q s n", s=4)[:, :, 0:LEFT]).then_inc(par_ready, 1)

    def gpsimd(pool):
        for s, n in c.scores_stored:
            pool.wait_ge(s, n)
        pool.memset(zeros[:], 0.0).then_inc(fills_made, 1)
        pool.memset(ones[:], 1.0).then_inc(fills_made, 1)

    c.make_taps, c.add_taps, c.load_unit, c.move_unit = make_taps, add_taps, load, move
    return Programs(sync=sync, scalar=scalar, tensor=tensor, gpsimd=gpsimd)


def stage_swish(c):
    nc, sb = c.nc, Sbuf(c.nc, c.after_gmlp)
    X = len(CONV_SPANS)
    ones = sb("w_ones", [P, P])
    gate = [sb(f"w_gate{s}", [P, TOK]) for s in range(2)]
    y, y_full = c.y, c.y_full
    squares = [sb(f"w_squares{p}", [P, 4, CW_SPAN]) for p in range(2)]
    rstd, tmp = sb("w_rstd", [P, CONVS]), sb("w_tmp", [P, CONVS])
    tails = sb("w_tails", [LEFT, 2, CW])
    assert sb.at <= c.free_until
    S = c.sem
    own_steps = S("w_steps")
    z_full = [S(f"w_z_full{p}") for p in range(2)]
    ones_made, tail_turned, tail_copied, tails_stored = (S("w_" + n) for n in ("ones", "tail_turned", "tail_copied", "tails_stored"))
    summed, centred, squared, var_summed, rooted, acted, normed, gated, stored = (
        S("w_" + n) for n in ("summed", "centred", "squared", "var_summed", "rooted", "acted", "normed", "gated", "stored"))
    span = lambda x: slice(x * CW_SPAN, (x + 1) * CW_SPAN)
    SUM, VAR, TAIL = (0, 1), 3, 2

    def sync(sp):
        for s in range(4):
            if s == 2:
                c.load_keys(sp)
            if s >= 2:
                sp.wait_ge(gated, s - 1)
            sp.dma_start(gate[s % 2][:], c.T_dram[S_ZC + s]).then_inc(z_full[s % 2], 16)
        for s in range(4):
            sp.wait_ge(gated, s + 1)
            sp.dma_start(c.B_dram[2, s, :, 0:SEQ], y[:, s, 0:SEQ]).then_inc(stored, 16)
            sp.dma_start(c.B_dram[2, s, :, SEQ:SEQ + DEC], y[:, s, DEC_AT:CONVS]).then_inc(stored, 16)
        sp.wait_ge(tail_copied, 4)
        sp.dma_start(c.O["conv_prompt"], tails[:, 0, :]).then_inc(tails_stored, 16)
        sp.dma_start(c.O["conv_sample"], tails[:, 1, :]).then_inc(tails_stored, 16)
        sp.wait_ge(tails_stored, 32)
        sp.wait_ge(stored, 128)

    def tensor(pe):
        for s, n in c.gmlp_done:
            pe.wait_ge(s, n)
        pe.wait_ge(ones_made, 1)
        pe.wait_ge(y_full, 64)

        def total(bank, values, sem):
            for s in range(4):
                last = pe.matmul(c.psum[:, bank, 0:CW_SPAN], ones[:], values(s), start=(s == 0), stop=(s == 3))
            last.then_inc(sem, 1)

        for x in range(X + 1):
            if x < X:
                if x > 1:
                    pe.wait_ge(centred, x - 1)
                total(SUM[x % 2], lambda s: y[:, s, span(x)], summed)
            if x:
                pe.wait_ge(squared, x)
                total(VAR + x - 1, lambda s: squares[(x - 1) % 2][:, s, :], var_summed)
        for s in range(4):
            if s >= 1:
                pe.wait_ge(tail_copied, s)
            for u in range(2):
                last = pe.transpose(c.psum[0:LEFT, TAIL, u * P:(u + 1) * P], c.tailsT[:, s, u, :], c.ident[:])
            last.then_inc(tail_turned, 1)

    def vector(vec):
        steps = Steps(vec, own_steps)
        do = steps.did_wait
        vec.memset(ones[:], 1.0 / CW).then_inc(ones_made, 1)
        for x in range(X):
            vec.wait_ge(summed, x + 1)
            mean = c.psum[:, SUM[x % 2], 0:CW_SPAN].unsqueeze(1).to_broadcast([P, 4, CW_SPAN])
            vec.tensor_tensor(y[:, :, span(x)], y[:, :, span(x)], mean, ALU.subtract).then_inc(centred, 1)
        vec.wait_ge(centred, X)
        vec.wait_ge(var_summed, X)
        do(vec.tensor_scalar(tmp[:].rearrange("q (b n) -> q b n", b=X), c.psum[:, VAR:VAR + X, 0:CW_SPAN], EPS, None, ALU.add))
        vec.sem_inc(rooted, 1)
        vec.wait_ge(acted, 1)
        do(vec.reciprocal(rstd[:], rstd[:]))
        do(vec.tensor_tensor(tmp[:], tmp[:], rstd[:], ALU.mult))
        do(vec.tensor_tensor(tmp[:], tmp[:], rstd[:], ALU.mult))
        do(vec.tensor_scalar(tmp[:], tmp[:], -0.5, 1.5, ALU.mult, ALU.add))
        do(vec.tensor_tensor(rstd[:], rstd[:], tmp[:], ALU.mult))
        for s in range(4):
            vec.tensor_tensor(y[:, s, :], y[:, s, :], rstd[:], ALU.mult).then_inc(normed, 1)
        for s in range(4):
            vec.wait_ge(acted, s + 2)
            vec.wait_ge(z_full[s % 2], (s // 2 + 1) * 16)
            z = gate[s % 2]
            do(vec.tensor_tensor(y[:, s, 0:SEQ], y[:, s, 0:SEQ], z[:, 0:SEQ], ALU.mult))
            vec.tensor_tensor(y[:, s, DEC_AT:CONVS], y[:, s, DEC_AT:CONVS], z[:, SEQ:SEQ + DEC], ALU.mult).then_inc(gated, 1)
        for s in range(4):
            vec.wait_ge(tail_turned, s + 1)
            vec.tensor_copy(tails[:, :, s * P:(s + 1) * P], c.psum[0:LEFT, TAIL, 0:2 * P].rearrange("q (u n) -> q u n", u=2)
                            ).then_inc(tail_copied, 1)

    def scalar(act):
        for x in range(X):
            act.wait_ge(centred, x + 1)
            if x > 1:
                act.wait_ge(var_summed, x - 1)
            act.activation(squares[x % 2][:], y[:, :, span(x)], ACT.Square).then_inc(squared, 1)
        act.wait_ge(rooted, 1)
        act.activation(rstd[:], tmp[:], ACT.Sqrt).then_inc(acted, 1)
        for s in range(4):
            act.wait_ge(normed, s + 1)
            act.activation(y[:, s, :], y[:, s, :], ACT.Silu, scale=c.parT[:, s, CONV + 1:CONV + 2],
                           bias=c.parT[:, s, CONV + 2:CONV + 3]).then_inc(acted, 1)

    c.conv_done = (stored, 128), (tails_stored, 32)
    return Programs(sync=sync, scalar=scalar, vector=vector, tensor=tensor)


LOWEST = -3.0e38


class Actions:

    def __init__(self, start=None, turned=None, unit=None, head=None, weigh=None, all_weighed=None, finish=None):
        nothing = lambda *_: None
        self.start, self.turned, self.unit, self.head = start or nothing, turned or nothing, unit or nothing, head or nothing
        self.weigh, self.all_weighed, self.finish = weigh or nothing, all_weighed or nothing, finish or nothing


def stage_attend_loads(c):
    NV = PAST // P + 1
    sb = Sbuf(c.nc, c.nc.sbuf_usable_end // 32 * 32 - HEADS * SEQ * 4)
    L = c.L = [sb(f"a_l{h}", [P, SEQ]) for h in range(HEADS)]
    c.free_until = sb.at - (HEADS - 1) * SEQ * 4
    c.kraw = kraw = L[1:3]
    c.vraw = L[3][:].rearrange("q (t n) -> q t n", t=DT)
    c.vsraw = L[4][:, 0:NV * P].rearrange("q (t n) -> q t n", t=NV)
    c.cache = L[5][:].rearrange("q (t g u d) -> q t g u d", t=PAST // P, g=KVH, u=2)
    c.new_k = new_k = [L[6 + g][:, 0:DEC] for g in range(KVH)]

    def load_keys(sp):
        for g in range(KVH):
            doubled(sp, kraw[g], c.T_dram[S_K, g * HD:(g + 1) * HD, 0:SEQ], c.k_full)
            doubled(sp, new_k[g], c.T_dram[S_K, g * HD:(g + 1) * HD, SEQ:SEQ + DEC], c.k_full)
            for u in range(2):
                sp.dma_start(c.cache[:, :, g, u, :],
                             c.I["cache_k"].rearrange("(t q g) d -> q t g d", q=P, g=KVH)[:, :, g, :]).then_inc(c.cache_full, 16)
        sp.dma_start(c.vraw, c.O["v_prompt"].rearrange("(t q g) d -> q t (g d)", q=P, g=KVH)).then_inc(c.v_full, 16)
        sp.dma_start(c.vsraw[:, 0:NV - 1, :], c.I["cache_v"].rearrange("(t q g) d -> q t (g d)", q=P, g=KVH)).then_inc(c.vs_full, 16)
        sp.dma_start(c.vsraw[0:DEC, NV - 1, :], c.O["v_sample"].rearrange("(q g) d -> q (g d)", g=KVH)).then_inc(c.vs_full, 16)

    c.load_keys = load_keys
    return Programs()


def stage_attend(c):
    nc, sb = c.nc, Sbuf(c.nc, c.first)
    NS, NV = PAST + DEC, PAST // P + 1
    QK, PT, PO, PB = 2, (2, 3, 4), (5, 6), 7
    RING = len(PT)
    k_hi, k_lo, ks_hi, ks_lo = ([sb(f"a_{n}{g}", [P, w], F32R) for g in range(KVH)]
                                for n, w in (("khi", SEQ), ("klo", SEQ), ("kshi", NS), ("kslo", NS)))
    v_p = sb("a_vp", [P, DT, KVH, P], F32R)
    v_s = sb("a_vs", [P, NV, KVH, P], F32R)
    nd = [sb(f"a_nd{p}", [P, SEQ]) for p in range(2)]
    L, kraw, vraw, vsraw, cache, new_k = c.L, c.kraw, c.vraw, c.vsraw, c.cache, c.new_k
    q2 = [sb(f"a_q2{p}", [P, HEADS, P]) for p in range(2)]
    qs = [sb(f"a_qs{p}", [P, HEADS, P], F32R) for p in range(2)]
    scale = sb("a_scale", [P, HEADS])
    pT_hi = [sb(f"a_pthi{u}", [P, 512], F32R) for u in range(RING)]
    pT_lo = [sb(f"a_ptlo{u}", [P, 512], F32R) for u in range(RING)]
    za = [sb(f"a_za{p}", [HD, HEADS, P]) for p in range(2)]
    oa = [sb(f"a_oa{p}", [HD, HEADS, P]) for p in range(2)]
    o_low = sb("a_olow", [HD, 512])
    peaks = sb("a_peaks", [P, HEADS, 4])
    peak = sb("a_peak", [P, HEADS])
    nbias = sb("a_nbias", [P, HEADS])
    sums = sb("a_sums", [P, HEADS])
    rs = sb("a_rs", [P, HEADS])
    S = c.sem
    own_steps = S("a_steps")
    k_full, v_full, cache_full, vs_full = c.k_full, c.v_full, c.cache_full, c.vs_full
    cache_turned, hi_made = S("a_cache_turned"), S("a_hi_made")
    operands = S("a_operands")
    scale_set = S("a_scale_set")
    nd_full, q_full, za_full, q_scaled, q_hi, q_ready, o_done, stored = (
        [S(f"a_{n}{p}") for p in range(2)] for n in ("nd_full", "q_full", "za_full", "q_scaled", "q_hi", "q_ready", "o_done", "stored"))
    qk_full = S("a_qk_full")
    qk_read = [S(f"a_qk_read{b}") for b in range(QK)]
    po_read = [S(f"a_po_read{g}") for g in range(KVH)]
    mark = S("a_mark")
    head_ready, exp_done, rs_ready, pt_full, pt_hi, bc_full, o_copied = (
        S("a_" + n) for n in ("head_ready", "exp_done", "rs_ready", "pt_full", "pt_hi", "bc_full", "o_copied"))
    pt_lo = [S(f"a_pt_lo{u}") for u in range(RING)]
    pv_used = [S(f"a_pv_used{u}") for u in range(RING)]
    per_tile = [HEADS * len(pieces(keys)) for _, keys in CLASSES]
    before = [4 * sum(per_tile[:j]) for j in range(len(CLASSES))]
    ktiles = [-(-keys // P) for _, keys in CLASSES]
    kt_before = [4 * 2 * sum(ktiles[:j]) for j in range(len(CLASSES))]

    def turn_of(j, m):
        return m - CLASSES[j][0] // 2

    def slot_uses(units, j, slot, slots):
        uses = [len(range(slot, n, slots)) for n in units]
        return uses[j], 2 * sum(uses[:j])

    def score_units(j, t, m, p, g):
        i = turn_of(j, m)
        spans = pieces(CLASSES[j][1])
        for n, (r, (s, (a, w))) in enumerate((r, s) for r in range(4) for s in enumerate(spans)):
            u = before[j] + p * per_tile[j] + g * 4 * len(spans) + n
            x = (2 * p + g) * 4 * len(spans) + n
            turns, before_it = slot_uses([2 * n for n in per_tile], j, x % QK, QK)
            yield 4 * g + r, s, a, w, x % QK, i * turns + (before_it + x // QK), i * (2 * per_tile[j]) + u

    def key_units(j, t, m, p, g):
        i = turn_of(j, m)
        for kt in range(ktiles[j]):
            x = (2 * p + g) * ktiles[j] + kt
            turns, before_it = slot_uses([4 * n for n in ktiles], j, x % RING, RING)
            yield (kt, min(P, CLASSES[j][1] - kt * P), x % RING, i * turns + (before_it + x // RING),
                   i * (4 * ktiles[j]) + (kt_before[j] + x))

    def together(e, weighed, scored, before):
        units = list(score_units(*scored)) if scored else []
        keys = list(key_units(*weighed)) if weighed else []
        if weighed:
            e.start(weighed, keys, before is None)
        issued, heads = 0, []
        for x in range(max(1, len(keys))):
            if weighed:
                e.turned(weighed, keys, x)
            if x == 0 and before:
                e.finish(before)
            for h, at_x in heads:
                if at_x + 2 <= x:
                    e.head(scored, h)
            heads = [(h, at_x) for h, at_x in heads if at_x + 2 > x]
            for unit in units[issued:-(-len(units) * 4 * (x + 1) // (3 * len(keys))) if weighed else None]:
                e.unit(scored, unit)
                issued += 1
                if issued % (len(units) // 4) == 0:
                    heads.append((unit[0], x))
            if weighed:
                e.weigh(weighed, keys, x, scored)
        for h, _ in heads:
            e.head(scored, h)
        if weighed:
            e.all_weighed(weighed, keys)

    def group_order(e, loop):
        with loop(1) as i:
            groups = [(min(t // 4, len(CLASSES) - 1), i + t, i + t // 2, t % 2, g) for t in range(DT) for g in range(KVH)]
            groups += [(4, DT, DT // 2, 0, g) for g in range(KVH)]
            together(e, None, groups[0], None)
            for n, group in enumerate(groups):
                together(e, group, groups[n + 1] if n + 1 < len(groups) else None, groups[n - 1] if n else None)
            e.finish(groups[-1])

    def by_head(slot):
        return c.T_dram[slot:slot + 4].rearrange("s q t -> (s q) t").rearrange("(h d) t -> d h t", d=HD)

    def sync(sp):
        def load(j, t, m, p):
            keys = CLASSES[j][1]
            sp.wait_ge(q_ready[p], m)
            doubled(sp, q2[p][:, :, 0:real(t)], by_head(S_Q)[:, :, at(t)], q_full[p])
            sp.wait_ge(o_done[p], m * 2)
            sp.dma_start(nd[p][:, 0:keys], c.ND_dram[at(t, 1), :, 0:keys].rearrange("a q n -> q (a n)")).then_inc(nd_full[p], 16)
            sp.dma_start(za[p][:, :, 0:real(t)], by_head(S_ZA)[:, :, at(t)]).then_inc(za_full[p], 16)
        query_tiles(lambda j: sp.Fori(0, 2), load)

    def gpsimd(pool):
        for h in range(HEADS):
            pool.memset(scale[:, h:h + 1], HD ** -0.5 * 2.0 ** (h + 1)).then_inc(scale_set, 1)
        pool.wait_ge(scale_set, HEADS)
        scales = scale[:].unsqueeze(2).to_broadcast([P, HEADS, P])
        zeros = c.zero[:].unsqueeze(1).to_broadcast([P, HEADS, P])

        def split(t, m, p):
            pool.wait_ge(q_ready[1 - p], m + p)
            pool.wait_ge(q_full[p], m * 32 + 32)
            pool.wait_ge(o_done[p], m * 2)
            pool.tensor_tensor(q2[p][:], q2[p][:], scales, ALU.mult).then_inc(q_scaled[p], 1)
            pool.wait_ge(q_scaled[p], m + 1)
            pool.tensor_tensor(qs[p][:], q2[p][:], zeros, ALU.add).then_inc(q_hi[p], 1)
            pool.wait_ge(q_hi[p], m + 1)
            pool.tensor_tensor(qs[p][HD:P], q2[p][HD:P], f32(qs[p][HD:P]), ALU.subtract).then_inc(q_ready[p], 1)

        def store(t, m, p):
            pool.wait_ge(o_done[p], m * 2 + 2)
            pool.dma_start(c.B_dram[0].rearrange("s q t -> (s q) t").rearrange("(h d) t -> d h t", d=HD)[:, :, at(t)],
                           oa[p][:, :, 0:real(t)]).then_inc(stored[p], 16)

        split(0, 0, 0)
        with pool.Fori(0, DT // 2) as i:
            split(i * 2 + 1, i, 1)
            store(i * 2, i, 0)
            split(i * 2 + 2, i + 1, 0)
            store(i * 2 + 1, i, 1)
        store(DT, DT // 2, 0)
        for p in range(2):
            pool.wait_ge(stored[p], 16 * (DT // 2 + 1 - p))

    cacheT = [c.psum[:, 2 * g:2 * g + 2, :].rearrange("q b n -> q (b n)") for g in range(KVH)]

    splits = []
    for g in range(KVH):
        splits += [(k_hi[g][:], k_lo[g][:], kraw[g][:], (k_full, 128)),
                   (ks_hi[g][:, 0:PAST], ks_lo[g][:, 0:PAST], cacheT[g], (cache_turned, 1)),
                   (ks_hi[g][:, PAST:], ks_lo[g][:, PAST:], new_k[g], (k_full, 128))]
    for full, n, v, raw, rows, tiles in ((v_full, 16, v_p, vraw, P, slice(0, DT)),
                                         (vs_full, 32, v_s, vsraw, P, slice(0, NV - 1)),
                                         (vs_full, 32, v_s, vsraw, DEC, slice(NV - 1, NV))):
        for g in range(KVH):
            src, dst = raw[0:rows, tiles, g * HD:(g + 1) * HD], v[0:rows, tiles, g, :]
            splits.append((dst[:, :, 0:HD], dst[:, :, HD:P], src, (full, n)))

    def tensor(pe):
        pe.wait_ge(cache_full, 64)
        for g in range(KVH):
            for t in range(PAST // P):
                last = pe.transpose(cacheT[g][:, t * P:(t + 1) * P], cache[:, t, g].rearrange("q u d -> q (u d)"), c.ident[:])
        last.then_inc(cache_turned, 1)
        pe.wait_ge(operands, 1)

        def turn(group, kt, w, u, nu, n):
            g = group[4]
            pe.wait_ge(pt_lo[u], nu)
            for r in range(4):
                last = pe.transpose(c.psum[0:w, PT[u], r * P:(r + 1) * P], L[4 * g + r][:, kt * P:kt * P + w], c.ident[:])
            last.then_inc(pt_full, 1)

        def start(group, keys, first):
            if first:
                turn_head(group)

        def turn_head(group, wanted=range(RING - 1)):
            j, t, m, p, g = group
            for x, key in enumerate(key_units(*group)):
                if x in wanted:
                    if x == 0:
                        pe.wait_ge(exp_done, t * 8 + (4 * g + 4))
                    turn(group, *key)

        def turned(group, keys, x):
            if x + RING - 1 < len(keys):
                turn(group, *keys[x + RING - 1])

        def unit(group, unit):
            (j, t, m, p, g), (h, s, a, w, b, nb, n) = group, unit
            hi, lo = (ks_hi[g], ks_lo[g]) if t is DT else (k_hi[g], k_lo[g])
            if s == 0 and h == 4 * g:
                pe.wait_ge(q_ready[p], m + 1)
            pe.wait_ge(qk_read[b], nb)
            pe.matmul(c.psum[:, b, 0:w], qs[p][:, h, :], hi[:, a:a + w], start=True, stop=False)
            pe.matmul(c.psum[:, b, 0:w], qs[p][:, h, :], lo[:, a:a + w], start=False, stop=True).then_inc(qk_full, 1)

        def weigh(group, keys, x, following):
            j, t, m, p, g = group
            kt, w, u, nu, n = keys[x]
            v = v_s if t is DT else v_p
            pe.wait_ge(pt_lo[u], nu + 1)
            if x == 0:
                pe.wait_ge(po_read[g], t)
            pe.matmul(c.psum[:, PO[g], :], v[0:w, kt, g, :], pT_hi[u][0:w, :], start=(x == 0), stop=False)
            pe.matmul(c.psum[:, PO[g], :], v[0:w, kt, g, :], pT_lo[u][0:w, :], start=False,
                      stop=(x == len(keys) - 1)).then_inc(pv_used[u], 1)
            if following:
                turn_head(following, [x + RING - 1 - len(keys)])

        def all_weighed(group, keys):
            j, t, m, p, g = group
            pe.wait_ge(rs_ready, t * 2 + (g + 1))
            if g:
                pe.wait_ge(o_done[p], m * 2 + 1)
            else:
                pe.wait_ge(o_done[1 - p], (m + p) * 2)
            for r in range(4):
                last = pe.matmul(c.psum[:, PB, r * P:(r + 1) * P], rs[:, 4 * g + r:4 * g + r + 1].to_broadcast([P, P]),
                                 c.ident[:], start=True, stop=True)
            last.then_inc(bc_full, 1)
        group_order(Actions(start=start, turned=turned, unit=unit, weigh=weigh, all_weighed=all_weighed),
                    lambda n: pe.Fori(0, n))

    def scalar(act):
        for hi, _, src, (sem, n) in splits:
            act.wait_ge(sem, n)
            act.copy(hi, src).then_inc(hi_made, 1)

        def head(group, h):
            j, t, m, p, g = group
            n = CLASSES[j][1]
            act.wait_ge(head_ready, t * 8 + (h + 1))
            act.activation(L[h][:, 0:n], L[h][:, 0:n], ACT.Exp, bias=nbias[:, h:h + 1],
                           accum_out=sums[:, h:h + 1]).then_inc(exp_done, 1)

        def turned(group, keys, x):
            kt, w, u, nu, n = keys[x]
            act.wait_ge(pt_full, n + 1)
            act.wait_ge(pv_used[u], nu)
            act.activation(pT_hi[u][0:w, :], c.psum[0:w, PT[u], :], ACT.Copy).then_inc(pt_hi, 1)

        def finish(group):
            j, t, m, p, g = group
            kt, w, u, nu, n = list(key_units(*group))[-1]
            act.wait_ge(pv_used[u], nu + 1)
            act.wait_ge(po_read[1 - g], t + g)
            act.activation(o_low[:], c.psum[HD:P, PO[g], :], ACT.Copy).then_inc(o_copied, 1)
        group_order(Actions(head=head, turned=turned, finish=finish), lambda n: act.Fori(0, n))

    def vector(vec):
        steps = Steps(vec, own_steps)
        do = steps.did_wait
        for n, (hi, lo, src, _) in enumerate(splits):
            vec.wait_ge(hi_made, n + 1)
            do(vec.tensor_tensor(lo, src, f32(hi), ALU.subtract))
        vec.sem_inc(operands, 1)

        def unit(group, unit):
            (j, t, m, p, g), (h, s, a, w, b, nb, n) = group, unit
            spans = len(pieces(CLASSES[j][1]))
            if s == 0 and h == 0:
                vec.wait_ge(nd_full[p], m * 16 + 16)
            vec.wait_ge(qk_full, n + 1)
            vec.sem_inc(mark, 1)
            vec.tensor_tensor_reduce(out=L[h][:, a:a + w], in0=nd[p][:, a:a + w], in1=c.psum[:, b, 0:w],
                                     scale=2.0 ** -(h + 1), scalar=LOWEST, op0=ALU.add, op1=ALU.max,
                                     accum_out=peaks[:, h, s:s + 1]).then_inc(qk_read[b], 1)
            if s == spans - 1:
                vec.wait_ge(qk_read[b], nb + 1)
                top = peaks[:, h, 0:1]
                if spans > 1:
                    top = peak[:, h:h + 1]
                    do(vec.tensor_reduce(top, peaks[:, h, 0:spans], AX.X, ALU.max))
                vec.tensor_scalar(nbias[:, h:h + 1], top, -1.0, None, ALU.mult).then_inc(head_ready, 1)

        def start(group, keys, first):
            j, t, m, p, g = group
            vec.wait_ge(exp_done, t * 8 + (4 * g + 4))
            vec.reciprocal(rs[:, 4 * g:4 * g + 4], sums[:, 4 * g:4 * g + 4]).then_inc(rs_ready, 1)

        def turned(group, keys, x):
            kt, w, u, nu, n = keys[x]
            vec.wait_ge(pt_hi, n + 1)
            vec.tensor_tensor(pT_lo[u][0:w, :], c.psum[0:w, PT[u], :], f32(pT_hi[u][0:w, :]), ALU.subtract
                              ).then_inc(pt_lo[u], 1)

        def finish(group):
            j, t, m, p, g = group
            o = oa[p][:, 4 * g:4 * g + 4, :].rearrange("d h t -> d (h t)")
            vec.wait_ge(o_copied, t * 2 + (g + 1))
            vec.wait_ge(bc_full, t * 2 + (g + 1))
            vec.wait_ge(stored[p], m * 16)
            vec.wait_ge(za_full[p], m * 16 + 16)
            vec.tensor_tensor(o, c.psum[0:HD, PO[g], :], o_low[:], ALU.add).then_inc(po_read[g], 1)
            vec.wait_ge(po_read[g], t + 1)
            do(vec.tensor_tensor(o, c.psum[0:HD, PB, :], o, ALU.mult))
            vec.tensor_tensor(o, o, za[p][:, 4 * g:4 * g + 4, :].rearrange("d h t -> d (h t)"), ALU.mult).then_inc(o_done[p], 1)

        own = 2 * TILES + HEADS * (TILES - sum(len(pieces(keys)) == 1 for _, keys in CLASSES) * 4)
        group_order(Actions(start=start, turned=turned, unit=unit, finish=finish), lambda n: steps.turns(n, own))

    c.attended = (stored[0], 16 * (DT // 2 + 1)), (stored[1], 16 * (DT // 2))
    return Programs(sync=sync, scalar=scalar, vector=vector, tensor=tensor, gpsimd=gpsimd)


def split_weights(c, prefix, plan, buffers, loaded=(), loaded_full=None):
    n_loaded, n_raw = len(loaded), len(buffers)
    full, hi_done, lo_done = [], c.sem(f"{prefix}w_hi"), c.sem(f"{prefix}w_lo")
    raw = list(loaded) + [buffers[n % n_raw] for n in range(len(plan) - n_loaded)]
    for r in range(n_raw):
        full.append(c.sem(f"{prefix}w_full{r}"))

    def scalar(act):
        def load(n):
            m = n - n_loaded
            if m >= n_raw or n_loaded:
                act.wait_ge(lo_done, n - n_raw + 1 if m >= n_raw else n_loaded)
            act.dma_start(raw[n][:], plan[n][0]).then_inc(full[m % n_raw], 16)

        def high(n):
            act.copy(plan[n][1], raw[n][:]).then_inc(hi_done, 1)

        if n_loaded:
            act.wait_ge(loaded_full, 16 * n_loaded)
            for n in range(n_loaded):
                high(n)
        for n in range(n_loaded, n_loaded + n_raw):
            load(n)
        for n in range(n_loaded, len(plan)):
            m = n - n_loaded
            act.wait_ge(full[m % n_raw], 16 * (m // n_raw + 1))
            high(n)
            if m and n - 1 + n_raw < len(plan):
                load(n - 1 + n_raw)

    def vector(vec):
        for n, (_, hi, lo) in enumerate(plan):
            vec.wait_ge(hi_done, n + 1)
            vec.tensor_tensor(lo, raw[n][:], f32(hi), ALU.subtract).then_inc(lo_done, 1)

    def ready(eng, n=len(plan)):
        eng.wait_ge(lo_done, n)
    return Programs(scalar=scalar, vector=vector, ready=ready)


def stage_merge(c):
    nc, sb = c.nc, Sbuf(c.nc, c.first)
    names = ("w_branch_a", "w_branch_b", "w_branch_c")
    w_hi = sb("m_whi", [P, 3, 4, D], F32R)
    w_lo = sb("m_wlo", [P, 3, 4, D], F32R)
    top = Sbuf(nc, nc.sbuf_usable_end // 32 * 32 - KD * D * 4)
    start = top.at
    raws = [top(f"m_raw{r}", [P, D]) for r in range(KD)]
    c.w_out_raw, c.w_out_full = raws, c.sem("m_w_out_full")
    weights = split_weights(c, "m_", [(c.I[names[b]][k * P:(k + 1) * P, :], w_hi[:, b, k, :], w_lo[:, b, k, :])
                                      for b in range(3) for k in range(4)], raws)
    o_raw = [sb(f"m_oraw{x}", [P, 4, SPAN]) for x in range(2)]
    o_hi = [sb(f"m_ohi{x}", [P, 4, SPAN], F32R) for x in range(2)]
    o_lo = [sb(f"m_olo{x}", [P, 4, SPAN], F32R) for x in range(2)]
    gate = [sb(f"m_gate{x}", [P, 2, SPAN]) for x in range(4)]
    merged = sb("m_merged", [P, 8, SPAN])
    tmp = [sb(f"m_tmp{x}", [P, SPAN]) for x in range(2)]
    assert sb.at <= start
    S = c.sem
    o_full = [S(f"m_o_full{x}") for x in range(2)]
    o_hi_done = [S(f"m_o_hi{x}") for x in range(2)]
    o_lo_done = [S(f"m_o_lo{x}") for x in range(2)]
    g_full = [S(f"m_g_full{x}") for x in range(4)]
    product, gated, added, stored = S("m_product"), S("m_gated"), S("m_added"), S("m_stored")

    def spans(eng, body, before_last=lambda: None):
        with eng.Fori(0, len(SPANS) // 2) as i:
            for y in range(2):
                for b in range(3):
                    body(i, y, b, bass.ds(i * 2 * SPAN + y * SPAN, SPAN))
        before_last()
        for b in range(3):
            body(2, 0, b, slice(4 * SPAN, TOK))

    def wait(eng, sem, i, y, n, per=24):
        n += per * y
        eng.wait_ge(sem, i * (2 * per) + (n if isinstance(i, int) else max(0, n)))

    def buffer(i, y, b):
        return (3 * y + b) % 2, i * 3 + (3 * y + b) // 2

    def sync(sp):
        for s, n in c.attended:
            sp.wait_ge(s, n)

        def load(i, y, b, cols):
            u, nu = buffer(i, y, b)
            sp.wait_ge(o_lo_done[u], nu)
            sp.dma_start(o_raw[u][:], c.B_dram[b, :, :, cols].rearrange("s q t -> q s t")).then_inc(o_full[u], 16)
            for n in range(4):
                wait(sp, gated, i, y, 8 * b - 8 + 2 * n + 2)
                slot = S_G + 8 * b + 2 * n
                sp.dma_start(gate[n][:], c.T_dram[slot:slot + 2, :, cols].rearrange("s q t -> q s t")).then_inc(g_full[n], 16)
        spans(sp, load)

    def gpsimd(pool):
        def split(i, y, b, cols):
            u, nu = buffer(i, y, b)
            zeros = c.zero[:].unsqueeze(1).to_broadcast([P, 4, SPAN])
            pool.wait_ge(o_full[u], nu * 16 + 16)
            wait(pool, product, i, y, 8 * b - 8)
            pool.tensor_tensor(o_hi[u][:], o_raw[u][:], zeros, ALU.add).then_inc(o_hi_done[u], 1)
            pool.wait_ge(o_hi_done[u], nu + 1)
            pool.tensor_tensor(o_lo[u][:], o_raw[u][:], f32(o_hi[u][:]), ALU.subtract
                               ).then_inc(o_lo_done[u], 1)
        for s, n in c.attended:
            pool.wait_ge(s, n)
        spans(pool, split)

    def tensor(pe):
        def products(i, y, b, cols):
            u, nu = buffer(i, y, b)
            weights.ready(pe, 4 * (b + 1))
            pe.wait_ge(o_lo_done[u], nu + 1)
            for n in range(8):
                wait(pe, gated, i, y, 8 * b - 8 + n + 1)
                for k in range(4):
                    for q, (wt, o) in enumerate(((w_hi, o_hi), (w_hi, o_lo), (w_lo, o_hi))):
                        last = pe.matmul(c.psum[:, n, 0:SPAN], wt[:, b, k, n * P:(n + 1) * P], o[u][:, k, :],
                                         start=(k == 0 and q == 0), stop=(k == 3 and q == 2))
                last.then_inc(product, 1)
        spans(pe, products)

    def scalar(act):
        for s, n in c.attended:
            act.wait_ge(s, n)
        weights.scalar(act)
        def store(i, y, b, cols):
            if b == 2:
                act.wait_ge(added, i * 32 + (16 * y + 16))
                act.dma_start(c.M_dram[:, :, cols].rearrange("s q t -> q s t"), merged[:]).then_inc(stored, 16)

        def load_w_out():
            weights.ready(act)
            for k in range(KD):
                act.dma_start(raws[k][:], c.I["w_out"][k * P:(k + 1) * P, :]).then_inc(c.w_out_full, 16)
        spans(act, store, load_w_out)

    def vector(vec):
        weights.vector(vec)

        def gating(i, y, b, cols):
            for n in range(8):
                wait(vec, product, i, y, 8 * b + n + 1)
                if n % 2 == 0:
                    vec.wait_ge(g_full[n // 2], i * 96 + (48 * y + 16 * b + 16))
                dst = merged[:, n, :] if b == 0 else tmp[n % 2][:, :]
                if b == 0:
                    vec.wait_ge(stored, i * 32 + 16 * y)
                else:
                    vec.wait_ge(added, i * 32 + (16 * y + 8 * (b - 1) + n))
                vec.tensor_tensor(dst, c.psum[:, n, 0:SPAN], gate[n // 2][:, n % 2, :], ALU.mult).then_inc(gated, 1)
                if b:
                    wait(vec, gated, i, y, 8 * b + n + 1)
                    vec.tensor_tensor(merged[:, n, :], merged[:, n, :], dst, ALU.add).then_inc(added, 1)
        spans(vec, gating)

    c.merged_stored = ((stored, 16 * len(SPANS)),)
    c.merged = ((gated, 24 * len(SPANS)),)
    return Programs(sync=sync, scalar=scalar, vector=vector, tensor=tensor, gpsimd=gpsimd)


FINISH_STEPS = 2 * (1 + RSQRT_STEPS) + 1


def stage_finish(c):
    nc, sb = c.nc, Sbuf(c.nc, c.first)
    KP = 2
    wo_hi, wo_lo, wg_hi, wg_lo = (sb(f"f_{n}", [P, KD, D], F32R) for n in ("wohi", "wolo", "wghi", "wglo"))
    wp_hi, wp_lo = (sb(f"f_{n}", [P, KP, D], F32R) for n in ("wphi", "wplo"))
    ple_g = sb("f_pleg", [P, D])
    m_raw = sb("f_mraw", [P, KD, P])
    m_hi = sb("f_mhi", [P, KD, P], F32R)
    m_lo = sb("f_mlo", [P, KD, P], F32R)
    x = [sb(f"f_x{p}", [P, D]) for p in range(2)]
    pl = [sb(f"f_p{p}", [P, KP * P]) for p in range(2)]
    fin_g = sb("f_fing", [P, D])
    p_hi = sb("f_phi", [P, KP, P], F32R)
    p_lo = sb("f_plo", [P, KP, P], F32R)
    xn = sb("f_xn", [P, D])
    y = [sb(f"f_y{p}", [P, D]) for p in range(2)]
    h_hi = sb("f_hhi", [P, KD, P], F32R)
    h_lo = sb("f_hlo", [P, KD, P], F32R)
    sig = sb("f_sig", [P, D])
    weights = split_weights(c, "f_", [(c.I[name][k * P:(k + 1) * P, :], hi[:, k, :], lo[:, k, :])
                                      for name, hi, lo, ks in (("w_out", wo_hi, wo_lo, KD), ("w_ple_gate", wg_hi, wg_lo, KD),
                                                               ("w_ple", wp_hi, wp_lo, KP)) for k in range(ks)],
                            y + [sb("f_raw", [P, D])], c.w_out_raw, c.w_out_full)
    ssq = sb("f_ssq", [P, 2])
    var, rstd, tmp = sb("f_var", [P, 1]), sb("f_rstd", [P, 1]), sb("f_tmp", [P, 1])
    S = c.sem
    own_steps = S("f_steps")
    g_full = S("f_g_full")
    m_full, m_hi_done, m_lo_done = S("f_m_full"), S("f_m_hi"), S("f_m_lo")
    x_full = [S(f"f_x_full{p}") for p in range(2)]
    p_full = [S(f"f_p_full{p}") for p in range(2)]
    out_product, added, squared, normed, x_turned, h_hi_done, h_lo_done, p_turned = (
        S("f_" + n) for n in ("out_product", "added", "squared", "normed", "x_turned", "h_hi", "h_lo", "p_turned"))
    p_hi_done, p_lo_done, ple_product, gate_product, sig_done, summed, last_squared = (
        S("f_" + n) for n in ("p_hi", "p_lo", "ple_product", "gate_product", "sig_done", "summed", "last_squared"))
    finished = [S(f"f_finished{p}") for p in range(2)]
    stored = [S(f"f_stored{p}") for p in range(2)]
    pair = lambda b: c.psum[:, b:b + 2, :].rearrange("q b n -> q (b n)")
    b_out, b_turn, b_gate, b_ple = 0, 2, 4, 6
    xT = pair(b_turn).rearrange("q (k n) -> q k n", k=KD)
    pT = pair(b_turn)[:, 0:KP * P].rearrange("q (k n) -> q k n", k=KP)

    def pipelined(loop, body):
        body(0, 0, 0, True, False)
        with loop as i:
            body(i * 2 + 1, i, 1, False, False)
            body(i * 2 + 2, i + 1, 0, False, False)
        body(DT - 1, DT // 2 - 1, 1, False, False)
        body(DT, DT // 2, 0, False, True)

    def sync(sp):
        for s, n in c.merged_stored:
            sp.wait_ge(s, n)
        sp.dma_start(ple_g[:], c.I["ple_norm_g"].partition_broadcast(P)).then_inc(g_full, 16)

        def load(t, m, p):
            last = isinstance(t, int)
            n, rows, r = ("sample", slice(0, DEC), DEC) if last else ("prompt", at(t), P)
            sp.wait_ge(m_lo_done, t)
            sp.dma_start(m_raw[:, :, 0:r], c.M_dram[:, :, at(t)].rearrange("s q t -> q s t")).then_inc(m_full, 16)
            sp.wait_ge(finished[p], m)
            sp.dma_start(x[p][0:r, :], c.I["x_" + n][rows, :]).then_inc(x_full[p], 16)
            sp.dma_start(pl[p][0:r, :], c.I["p_" + n][rows, :]).then_inc(p_full[p], 16)
        token_tiles(sp, load)

    def tensor(pe):
        def three(bank, lhs_hi, lhs_lo, w_hi, w_lo, ks):
            for half in range(2):
                cols = slice(half * 512, half * 512 + 512)
                for k in range(ks):
                    for q, (a, w) in enumerate(((lhs_hi, w_hi), (lhs_lo, w_hi), (lhs_hi, w_lo))):
                        last = pe.matmul(pair(bank)[:, cols], a[:, k, :], w[:, k, cols],
                                         start=(k == 0 and q == 0), stop=(k == ks - 1 and q == 2))
            return last

        def out(t):
            pe.wait_ge(m_lo_done, t + 1)
            if not (isinstance(t, int) and t == 0):
                pe.wait_ge(added, t)
            three(b_out, m_hi, m_lo, wo_hi, wo_lo, KD).then_inc(out_product, 1)

        def body(t, m, p, first, last):
            pe.wait_ge(normed, t + 1)
            if not first:
                pe.wait_ge(p_lo_done, t)
            for k in range(KD):
                ins = pe.transpose(xT[:, k, :], xn[:, k * P:(k + 1) * P], c.ident[:])
            ins.then_inc(x_turned, 1)
            if not last:
                out(t + 1)
            pe.wait_ge(p_full[p], m * 16 + 16)
            pe.wait_ge(h_lo_done, t + 1)
            for k in range(KP):
                ins = pe.transpose(pT[:, k, :], pl[p][:, k * P:(k + 1) * P], c.ident[:])
            ins.then_inc(p_turned, 1)
            if first:
                weights.ready(pe)
            else:
                pe.wait_ge(sig_done, t)
            three(b_gate, h_hi, h_lo, wg_hi, wg_lo, KD).then_inc(gate_product, 1)
            pe.wait_ge(p_lo_done, t + 1)
            if not first:
                pe.wait_ge(summed, t)
            three(b_ple, p_hi, p_lo, wp_hi, wp_lo, KP).then_inc(ple_product, 1)

        weights.ready(pe, KD)
        out(0)
        pipelined(pe.Fori(0, DT // 2 - 1), body)

    def gpsimd(pool):
        zeros = c.zero[:].unsqueeze(1).to_broadcast([P, KD, P])

        def split(t, m, p):
            pool.wait_ge(m_full, t * 16 + 16)
            pool.wait_ge(out_product, t)
            pool.tensor_tensor(m_hi[:], m_raw[:], zeros, ALU.add).then_inc(m_hi_done, 1)
            pool.wait_ge(m_hi_done, t + 1)
            pool.tensor_tensor(m_lo[:], m_raw[:], f32(m_hi[:]), ALU.subtract).then_inc(m_lo_done, 1)
        for s, n in c.merged_stored:
            pool.wait_ge(s, n)
        token_tiles(pool, split)

    def scalar(act):
        for s, n in c.merged:
            act.wait_ge(s, n)
        weights.scalar(act)
        act.dma_start(fin_g[:], c.I["final_norm_g"].partition_broadcast(P)).then_inc(g_full, 16)

        def square(t, p, first=False):
            act.wait_ge(added, t + 1)
            if not first:
                act.wait_ge(summed, t - 1)
            act.activation(sig[:], x[p][:], ACT.Square, accum_out=ssq[:, 0:1]).then_inc(squared, 1)

        def last_square(t, m, p):
            act.wait_ge(summed, t + 1)
            act.wait_ge(stored[p], m * 16)
            act.activation(y[p][:], x[p][:], ACT.Square, accum_out=ssq[:, 1:2]).then_inc(last_squared, 1)

        def store(t, m, p, last=False):
            act.wait_ge(finished[p], m + 1)
            act.dma_start(c.O["y_sample"] if last else c.O["y_prompt"][at(t), :], y[p][0:DEC if last else P, :]
                          ).then_inc(stored[p], 16)

        def body(t, m, p, first, last):
            act.wait_ge(x_turned, t + 1)
            if not first:
                act.wait_ge(gate_product, t)
            act.copy(h_hi[:], xT).then_inc(h_hi_done, 1)
            if not first:
                last_square(t - 1, m - 1 + p, 1 - p)
            act.wait_ge(p_turned, t + 1)
            if not first:
                act.wait_ge(ple_product, t)
            act.copy(p_hi[:], pT).then_inc(p_hi_done, 1)
            if not last:
                square(t + 1, 1 - p, first)
            if not first:
                store(t - 1, m - 1 + p, 1 - p)
            act.wait_ge(squared, t + (1 if last else 2))
            act.wait_ge(gate_product, t + 1)
            act.activation(sig[:], pair(b_gate), ACT.Sigmoid).then_inc(sig_done, 1)

        square(0, 0, True)
        pipelined(act.Fori(0, DT // 2 - 1), body)
        last_square(DT, DT // 2, 0)
        store(DT, DT // 2, 0, True)
        for p in range(2):
            act.wait_ge(stored[p], 16 * len(range(p, TILES, 2)))

    def vector(vec):
        weights.vector(vec)
        steps = Steps(vec, own_steps)
        do = steps.did_wait

        def root(col):
            do(vec.tensor_scalar(var[:], ssq[:, col:col + 1], 1.0 / D, EPS, ALU.mult, ALU.add))
            rsqrt(steps, rstd[:], var[:], tmp[:])

        def add(t, m, p):
            vec.wait_ge(out_product, t + 1)
            vec.wait_ge(x_full[p], m * 16 + 16)
            vec.tensor_tensor(x[p][:], x[p][:], pair(b_out), ALU.add).then_inc(added, 1)

        def norm(t, p):
            vec.wait_ge(squared, t + 1)
            root(0)
            vec.wait_ge(x_turned, t)
            vec.scalar_tensor_tensor(out=xn[:], in0=x[p][:], scalar=rstd[:], in1=ple_g[:], op0=ALU.mult,
                                     op1=ALU.mult).then_inc(normed, 1)
            vec.wait_ge(normed, t + 1)

        def end(t, p):
            vec.wait_ge(sig_done, t + 1)
            vec.wait_ge(ple_product, t + 1)
            do(vec.tensor_tensor(sig[:], pair(b_ple), sig[:], ALU.mult))
            vec.tensor_tensor(x[p][:], x[p][:], sig[:], ALU.add).then_inc(summed, 1)
            vec.wait_ge(last_squared, t + 1)
            root(1)
            vec.scalar_tensor_tensor(out=y[p][:], in0=x[p][:], scalar=rstd[:], in1=fin_g[:], op0=ALU.mult,
                                     op1=ALU.mult).then_inc(finished[p], 1)

        def body(t, m, p, first, last):
            vec.wait_ge(h_hi_done, t + 1)
            vec.tensor_tensor(h_lo[:], xT, f32(h_hi[:]), ALU.subtract).then_inc(h_lo_done, 1)
            if not first:
                end(t - 1, 1 - p)
            if not last:
                add(t + 1, m + p, 1 - p)
            vec.wait_ge(p_hi_done, t + 1)
            vec.tensor_tensor(p_lo[:], pT, f32(p_hi[:]), ALU.subtract).then_inc(p_lo_done, 1)
            if not first:
                vec.wait_ge(finished[1 - p], m + p)
            if not last:
                norm(t + 1, 1 - p)

        vec.wait_ge(g_full, 32)
        add(0, 0, 0)
        norm(0, 0)
        pipelined(steps.turns(DT // 2 - 1, 2 * FINISH_STEPS), body)
        end(DT, 0)

    return Programs(sync=sync, scalar=scalar, vector=vector, tensor=tensor, gpsimd=gpsimd)


def stage_turnover(c):
    arrived, cleared = c.lasting_sem("arrived"), c.lasting_sem("cleared")
    numbers = c.release_semaphores()

    def report(eng):
        eng.drain().then_inc(arrived, 1)
        eng.wait_ge(cleared, 1)

    def gpsimd(pool):
        pool.drain().then_inc(arrived, 1)
        pool.wait_ge(arrived, 5)
        pool.sem_clear(numbers).then_inc(cleared, 1)
        pool.wait_ge(cleared, 1)

    return Programs(sync=report, scalar=report, vector=report, tensor=report, gpsimd=gpsimd)


OUTPUTS = [("y_prompt", (1, SEQ, D)), ("y_sample", (1, DEC, D)),
           ("k_prompt", (1, 1, SEQ, KVH, HD)), ("v_prompt", (1, 1, SEQ, KVH, HD)),
           ("ik_prompt", (1, 1, SEQ, HD)), ("conv_prompt", (1, 1, CONV - 1, CW)),
           ("k_sample", (1, 1, DEC, KVH, HD)), ("v_sample", (1, 1, DEC, KVH, HD)),
           ("ik_sample", (1, 1, DEC, HD)), ("conv_sample", (1, 1, CONV - 1, CW)),
           ("gmlp_sample", (1, 1, DEC, BW))]


def build(nc, I, O, stages=None):
    with ExitStack() as ctx:
        c = Shared()
        c.nc, c.I, c.O = nc, I, O
        c.lasting_sem = lambda name: ctx.enter_context(nc.semaphore(name))
        passing, held = ExitStack(), []

        def sem(name):
            held.append(passing.enter_context(nc.semaphore(name)))
            return held[-1]

        def release_semaphores():
            numbers = sorted(s.num for s in held)
            held.clear()
            passing.close()
            assert numbers == list(range(numbers[0], numbers[-1] + 1)), numbers
            return range(numbers[0], numbers[-1] + 1)

        c.sem, c.release_semaphores = sem, release_semaphores
        c.psum = ctx.enter_context(nc.psum_tensor("psum", [P, 8, 512], F32))
        sb = Sbuf(nc, (nc.sbuf_base + 31) // 32 * 32)
        c.ident = sb("ident", [P, P])
        c.zero = sb("zero", [P, 1])
        c.k_full, c.v_full, c.cache_full, c.vs_full = (c.lasting_sem("a_" + n) for n in ("k_full", "v_full", "cache_full", "vs_full"))
        c.ident_ready = c.lasting_sem("ident_ready")
        c.aw = sb("aw", [P, TILES, IH])
        c.sg = sb("sg", [P, TILES, IH])
        c.weights_ready = c.lasting_sem("weights_ready")
        c.w_full = c.lasting_sem("j_w_full")
        c.acc_stored = [c.lasting_sem(f"i_stored{p}") for p in range(2)]
        c.qpos = sb("qpos", [P, TILES])
        c.lim = sb("lim", [P, TILES])
        c.parT = sb("parT", [P, 4, CONV + 3])
        c.tailsT = sb("tailsT", [P, 4, 2, LEFT])
        c.first = sb.at
        c.hT_hi = sb("hT_hi", [P, KD, TOK], F32R)
        c.hT_lo = sb("hT_lo", [P, KD, TOK], F32R)
        c.after_hT = sb.at
        c.Y_dram = nc.dram_tensor("Y_dram", [4, P, CONVS], F32).ap()
        c.ND_dram = nc.dram_tensor("ND_dram", [TILES, P, SEQ], F32).ap()
        c.M_dram = nc.dram_tensor("M_dram", [KD, P, TOK], F32).ap()
        c.B_dram = nc.dram_tensor("B_dram", [3, 4, P, TOK], F32).ap()
        c.SC_dram = nc.dram_tensor("SC_dram", [TILES, P, SEQ], F32).ap()
        c.T_dram = nc.dram_tensor("T_dram", [SLOTS, P, TOK], F32).ap()
        identity_step = c.lasting_sem("identity_step")
        parts = [s(c) for s in (stages or STAGES)]
        block = ctx.enter_context(nc.Block())

        @block.sync
        def _(sp):
            for s in parts:
                if s.sync:
                    s.sync(sp)

        @block.gpsimd
        def _(pool):
            pool.memset(c.zero[:], 0.0).then_inc(identity_step, 1)
            pool.memset(c.ident[:], 0.0).then_inc(identity_step, 1)
            pool.wait_ge(identity_step, 2)
            pool.affine_select(out=c.ident[:], in_=c.ident[:], compare_op=ALU.not_equal, fill=1.0, base=0,
                               pattern=[[-1, P]], channel_multiplier=1).then_inc(c.ident_ready, 1)
            for s in parts:
                if s.gpsimd:
                    s.gpsimd(pool)

        @block.scalar
        def _(act):
            for s in parts:
                if s.scalar:
                    s.scalar(act)

        @block.vector
        def _(vec):
            for s in parts:
                if s.vector:
                    s.vector(vec)

        @block.tensor
        def _(pe):
            for s in parts:
                if s.tensor:
                    s.tensor(pe)
        passing.close()


STAGES = [stage_constants, stage_norm, stage_project_first, stage_natural, stage_scores, stage_convolve, stage_select, stage_project_rest, stage_gmlp, stage_attend_loads, stage_swish, stage_turnover, stage_attend, stage_merge, stage_finish]


def kernel(**inputs):
    import concourse.bacc as bacc
    from concourse.bass_utils import run_bass_kernel_spmd

    nc = bacc.Bacc("TRN2", target_bir_lowering=False, num_devices=1)
    arrays, I, O = {}, {}, {}
    for name, value in inputs.items():
        a = np.ascontiguousarray(value)
        arrays[f"in_{name}"] = a = a.reshape(-1, a.shape[-1])
        I[name] = nc.dram_tensor(f"in_{name}", a.shape, F32, kind="ExternalInput").ap()
    for name, shape in OUTPUTS:
        O[name] = nc.dram_tensor(f"out_{name}", (int(np.prod(shape[:-1])), shape[-1]), F32,
                                 kind="ExternalOutput").ap()
    build(nc, I, O)
    r = run_bass_kernel_spmd(nc, [arrays], core_ids=[0])
    return tuple(np.asarray(r.results[0][f"out_{name}"]).reshape(shape) for name, shape in OUTPUTS)
```
